# Optimizing a Trainium2 kernel written in Bass

```python
import jax, jax.numpy as jnp
from jax import lax
import numpy as np

D_MODEL = 1024
BATCH = 1
SEQ = 1024
DEPTH = 1

GRID_W = 64
CTX_LEN = 256

RET_HEADS = 4
RET_DK = 256
RET_DV = 512
RET_CHUNK = 128
RET_QK_W = RET_HEADS * RET_DK
RET_V_W = RET_HEADS * RET_DV

ATT_HEADS = 8
ATT_KV_HEADS = 2
ATT_HEAD_DIM = 128
ATT_Q_W = ATT_HEADS * ATT_HEAD_DIM
ATT_KV_W = ATT_KV_HEADS * ATT_HEAD_DIM
ROPE_THETA = 10000.0
Q_BLOCK = 128

NORM_EPS = 1e-6

IN_SPLITS = (RET_QK_W, RET_V_W, ATT_KV_W, ATT_KV_W,
             RET_QK_W, RET_V_W, ATT_Q_W, ATT_Q_W, D_MODEL, D_MODEL)
KV_COLS = RET_QK_W + RET_V_W + 2 * ATT_KV_W
IN_COLS = KV_COLS + RET_QK_W + RET_V_W + 2 * ATT_Q_W + 2 * D_MODEL

kernel_name = "hybrid_retention_gqa_prefix_dit_block"

def rms_norm(x, w=None):
    xf = x.astype(jnp.float32)
    y = xf * lax.rsqrt(jnp.mean(xf * xf, axis=-1, keepdims=True) + NORM_EPS)
    if w is not None:
        y = y * w.astype(jnp.float32)
    return y.astype(x.dtype)

def split_cols(p, widths):
    out, start = [], 0
    for w in widths:
        out.append(p[..., start:start + w])
        start += w
    return out

def adaln_params(cvec, w_ada, b_ada):
    mod = jax.nn.silu(cvec) @ w_ada + b_ada
    return split_cols(mod, (D_MODEL, D_MODEL, D_MODEL))

def axial_rope(L):
    rows = L // GRID_W
    row = jnp.repeat(jnp.arange(rows, dtype=jnp.float32), GRID_W)
    col = jnp.tile(jnp.arange(GRID_W, dtype=jnp.float32), rows)
    half = ATT_HEAD_DIM // 2
    freqs = ROPE_THETA ** (-jnp.arange(0, half, 2, dtype=jnp.float32) / half)
    ang = jnp.concatenate([row[:, None] * freqs, col[:, None] * freqs], axis=-1)
    return jnp.cos(ang), jnp.sin(ang)

def apply_rope(x, cos, sin):
    B, L, H, D = x.shape
    xp = x.astype(jnp.float32).reshape(B, L, H, D // 2, 2)
    x0, x1 = xp[..., 0], xp[..., 1]
    c, s = cos[None, :, None, :], sin[None, :, None, :]
    out = jnp.stack([x0 * c - x1 * s, x0 * s + x1 * c], axis=-1)
    return out.reshape(B, L, H, D).astype(x.dtype)

def ret_kv(k_flat, v_flat):
    B, L, _ = k_flat.shape
    k = k_flat.reshape(B, L, RET_HEADS, RET_DK) * (RET_DK ** -0.5)
    v = v_flat.reshape(B, L, RET_HEADS, RET_DV)
    return k, v

def retention_scan(q, k, v, log_gamma, s0):
    B, L, H, _ = q.shape
    n = L // RET_CHUNK

    def chunks(t):
        return t.astype(jnp.float32).reshape(B, n, RET_CHUNK, H, t.shape[-1]).transpose(1, 0, 3, 2, 4)

    qc, kc, vc = chunks(q), chunks(k), chunks(v)
    idx = jnp.arange(RET_CHUNK, dtype=jnp.float32)
    lg = log_gamma.astype(jnp.float32)[:, None]
    rel = idx[:, None] - idx[None, :]
    decay_mask = jnp.where(rel >= 0, jnp.exp(lg[:, :, None] * jnp.maximum(rel, 0.0)), 0.0)
    q_decay = jnp.exp(lg * (idx + 1.0))
    k_decay = jnp.exp(lg * (RET_CHUNK - 1.0 - idx))
    chunk_decay = jnp.exp(lg[:, 0] * RET_CHUNK)

    def step(s, inp):
        qi, ki, vi = inp
        scores = jnp.einsum('bhid,bhjd->bhij', qi, ki) * decay_mask
        intra = jnp.einsum('bhij,bhje->bhie', scores, vi)
        cross = jnp.einsum('bhid,bhde->bhie', qi * q_decay[..., None], s)
        s_new = s * chunk_decay[:, None, None] + jnp.einsum('bhjd,bhje->bhde', ki * k_decay[..., None], vi)
        return s_new, intra + cross

    _, out = lax.scan(step, s0.astype(jnp.float32), (qc, kc, vc))
    return out.transpose(1, 0, 3, 2, 4).reshape(B, L, H, v.shape[-1])

def ctx_final_states(k, v, log_gamma):
    L = k.shape[1]
    pos = jnp.arange(L, dtype=jnp.float32)
    w_f = jnp.exp(log_gamma[0][:, None] * (L - 1.0 - pos))
    w_b = jnp.exp(log_gamma[1][:, None] * pos)
    kf, vf = k.astype(jnp.float32), v.astype(jnp.float32)
    s_f = jnp.einsum('blhd,hl,blhe->bhde', kf, w_f, vf)
    s_b = jnp.einsum('blhd,hl,blhe->bhde', kf, w_b, vf)
    return s_f, s_b

def retention_branch(q_flat, k, v, gate_flat, log_gamma, states):
    B, L, _ = q_flat.shape
    q = q_flat.reshape(B, L, RET_HEADS, RET_DK)
    o_f = retention_scan(q, k, v, log_gamma[0], states[0])
    o_b = retention_scan(q[:, ::-1], k[:, ::-1], v[:, ::-1], log_gamma[1], states[1])[:, ::-1]
    o = rms_norm(o_f + o_b)
    return o.reshape(B, L, RET_V_W).astype(gate_flat.dtype) * jax.nn.silu(gate_flat)

def att_heads(t_flat, n_heads, norm_w, rope):
    B, L, _ = t_flat.shape
    t = rms_norm(t_flat.reshape(B, L, n_heads, ATT_HEAD_DIM), norm_w)
    if rope is not None:
        t = apply_rope(t, rope[0], rope[1])
    return t

def gqa_block_attention(q, k_all, v_all):
    B, S, Hq, D = q.shape
    nb = S // Q_BLOCK
    rep = Hq // ATT_KV_HEADS
    qb = q.reshape(B, nb, Q_BLOCK, ATT_KV_HEADS, rep, D).transpose(1, 0, 2, 3, 4, 5)
    scale = D ** -0.5

    def one_block(qi):
        s = jnp.einsum('bqgrd,bkgd->bgrqk', qi, k_all).astype(jnp.float32) * scale
        p = jax.nn.softmax(s, axis=-1)
        return jnp.einsum('bgrqk,bkgd->bqgrd', p.astype(v_all.dtype), v_all)

    o = lax.map(one_block, qb)
    return o.transpose(1, 0, 2, 3, 4, 5).reshape(B, S, Hq * D)

def merge_branches(y_ret, y_att, mg_ret, mg_att, w_o_ret, w_o_att, w_out):
    y = jax.nn.sigmoid(mg_ret) * (y_ret @ w_o_ret) + jax.nn.sigmoid(mg_att) * (y_att @ w_o_att)
    return y @ w_out

def trunk_layer(x, ctx, c, c_ctx, norm_w, w_ada, b_ada, w_in, ret_log2_decay,
                q_norm_w, k_norm_w, w_o_ret, w_o_att, w_out, update_ctx):
    B, S, _ = x.shape
    shift, scale, gate = adaln_params(c, w_ada, b_ada)
    shift_c, scale_c, gate_c = adaln_params(c_ctx, w_ada, b_ada)
    hx = rms_norm(x, norm_w) * (1 + scale[:, None]) + shift[:, None]
    hc = rms_norm(ctx, norm_w) * (1 + scale_c) + shift_c
    log_gamma = jnp.log1p(-jnp.exp2(ret_log2_decay.astype(jnp.float32)))

    px = hx @ w_in
    ret_k, ret_v, att_k, att_v, ret_q, ret_g, att_q, att_g, mg_ret, mg_att = split_cols(px, IN_SPLITS)
    pc = hc @ (w_in if update_ctx else w_in[:, :KV_COLS])
    c_ret_k, c_ret_v, c_att_k, c_att_v = split_cols(pc, IN_SPLITS[:4])

    kc, vc = ret_kv(c_ret_k, c_ret_v)
    ctx_states = ctx_final_states(kc, vc, log_gamma)
    kca = att_heads(c_att_k, ATT_KV_HEADS, k_norm_w, None)
    vca = c_att_v.reshape(B, CTX_LEN, ATT_KV_HEADS, ATT_HEAD_DIM)

    kx, vx = ret_kv(ret_k, ret_v)
    y_ret = retention_branch(ret_q, kx, vx, ret_g, log_gamma, ctx_states)

    rope = axial_rope(S)
    qxa = att_heads(att_q, ATT_HEADS, q_norm_w, rope)
    kxa = att_heads(att_k, ATT_KV_HEADS, k_norm_w, rope)
    vxa = att_v.reshape(B, S, ATT_KV_HEADS, ATT_HEAD_DIM)
    k_all = jnp.concatenate([kxa, kca], axis=1)
    v_all = jnp.concatenate([vxa, vca], axis=1)
    y_att = gqa_block_attention(qxa, k_all, v_all) * jax.nn.silu(att_g)

    out = merge_branches(y_ret, y_att, mg_ret, mg_att, w_o_ret, w_o_att, w_out)
    x_new = x + gate[:, None] * out

    if update_ctx:
        _, _, _, _, c_ret_q, c_ret_g, c_att_q, c_att_g, c_mg_ret, c_mg_att = split_cols(pc, IN_SPLITS)
        zero = jnp.zeros((B, RET_HEADS, RET_DK, RET_DV), jnp.float32)
        yc_ret = retention_branch(c_ret_q, kc, vc, c_ret_g, log_gamma, (zero, zero))
        qca = att_heads(c_att_q, ATT_HEADS, q_norm_w, None)
        yc_att = gqa_block_attention(qca, kca, vca) * jax.nn.silu(c_att_g)
        out_c = merge_branches(yc_ret, yc_att, c_mg_ret, c_mg_att, w_o_ret, w_o_att, w_out)
        ctx = ctx + gate_c * out_c
    return x_new, ctx

def setup_inputs(seed: int = 0) -> dict:
    key = jax.random.key(seed)
    ks = jax.random.split(key, 15)
    f32 = jnp.float32
    nrm = lambda k, shape: jax.random.normal(k, shape, f32)
    x = nrm(ks[0], (BATCH, SEQ, D_MODEL))
    c = nrm(ks[1], (BATCH, D_MODEL))
    ctx = nrm(ks[2], (BATCH, CTX_LEN, D_MODEL))
    c_ctx = nrm(ks[3], (D_MODEL,))
    norm_w = 1.0 + 0.02 * nrm(ks[4], (DEPTH, D_MODEL))
    w_ada = nrm(ks[5], (DEPTH, D_MODEL, 3 * D_MODEL)) * (0.5 * D_MODEL ** -0.5)
    b_ada = 0.02 * nrm(ks[6], (DEPTH, 3 * D_MODEL))
    w_in = nrm(ks[7], (DEPTH, D_MODEL, IN_COLS)) * (D_MODEL ** -0.5)
    base = -5.0 - jnp.arange(RET_HEADS, dtype=f32)
    ret_log2_decay = base[None, None, :] + 0.1 * nrm(ks[8], (DEPTH, 2, RET_HEADS))
    q_norm_w = 1.0 + 0.02 * nrm(ks[9], (DEPTH, ATT_HEAD_DIM))
    k_norm_w = 1.0 + 0.02 * nrm(ks[10], (DEPTH, ATT_HEAD_DIM))
    w_o_ret = nrm(ks[11], (DEPTH, RET_V_W, D_MODEL)) * (RET_V_W ** -0.5)
    w_o_att = nrm(ks[12], (DEPTH, ATT_Q_W, D_MODEL)) * (ATT_Q_W ** -0.5)
    w_out = nrm(ks[13], (DEPTH, D_MODEL, D_MODEL)) * (D_MODEL ** -0.5)
    return {"x": x, "c": c, "ctx": ctx, "c_ctx": c_ctx, "norm_w": norm_w,
            "w_ada": w_ada, "b_ada": b_ada, "w_in": w_in, "ret_log2_decay": ret_log2_decay,
            "q_norm_w": q_norm_w, "k_norm_w": k_norm_w, "w_o_ret": w_o_ret,
            "w_o_att": w_o_att, "w_out": w_out}

def reference(x, c, ctx, c_ctx, norm_w, w_ada, b_ada, w_in, ret_log2_decay,
              q_norm_w, k_norm_w, w_o_ret, w_o_att, w_out):
    for layer in range(DEPTH):
        x, ctx = trunk_layer(x, ctx, c, c_ctx, norm_w[layer], w_ada[layer], b_ada[layer],
                             w_in[layer], ret_log2_decay[layer], q_norm_w[layer], k_norm_w[layer],
                             w_o_ret[layer], w_o_att[layer], w_out[layer],
                             update_ctx=(layer < DEPTH - 1))
    return x


_drawn_inputs = setup_inputs


def setup_inputs(seed=0):
    import zlib

    import numpy as np

    out = dict(_drawn_inputs(seed))
    spreads = {}
    factors = {'ctx': 3.605,
     'c_ctx': 3.154,
     'norm_w': 8.0,
     'b_ada': 4.838,
     'q_norm_w': 8.0,
     'k_norm_w': 8.0}
    for name, (base, spread) in spreads.items():
        noise = np.random.default_rng([zlib.crc32(name.encode()), seed]).standard_normal(out[name].shape)
        drawn = base * np.exp(spread * noise) if base else spread * noise
        out[name] = __import__('jax').numpy.asarray(drawn.astype(out[name].dtype))
    for name, factor in factors.items():
        out[name] = (out[name] * factor).astype(out[name].dtype)
    return out
```

```python
from contextlib import ExitStack

import numpy as np

import concourse.bass as bass
from concourse import mybir
from concourse.alu_op_type import AluOpType as ALU

F32 = mybir.dt.float32
F32R = mybir.dt.float32r
ACT = mybir.ActivationFunctionType
AX = mybir.AxisListType

P = 128
D = 1024
SEQ = 1024
CTX = 256
GRID_W = 64
KT = D // P
TT = SEQ // P
CT = CTX // P
RH, RDK, RDV = 4, 256, 512
AH, AKV, AD = 8, 2, 128
EPS = 1e-6
ROPE_THETA = 10000.0
W = 512
CH = 256
NCH = SEQ // CH

B_RK, B_RV, B_AKV, B_RQ, B_RG, B_AQ, B_AG, B_MR, B_MA = 0, 2, 6, 7, 9, 13, 15, 17, 19
NB = 21
CTX_BLOCKS = 7


def shape_constants():
    half = AD // 2
    rows = np.repeat(np.arange(SEQ // GRID_W, dtype=np.float32), GRID_W)
    cols = np.tile(np.arange(GRID_W, dtype=np.float32), SEQ // GRID_W)
    freqs = (np.float32(ROPE_THETA) ** (-np.arange(0, half, 2, dtype=np.float32) / np.float32(half))).astype(np.float32)
    ang = np.concatenate([rows[:, None] * freqs, cols[:, None] * freqs], axis=-1).astype(np.float32)
    rope = np.stack([np.cos(ang), np.sin(ang)]).astype(np.float32)
    p = np.arange(P, dtype=np.float32)
    exps = [p + 1, p + 129, 255 - p, 127 - p, p * 0 + 256, 256 - p, 128 - p, p, p + 128, p * 0 + 256]
    j = p[:, None, None] + P * np.arange(2, dtype=np.float32)[None, :, None]
    i = np.arange(CH, dtype=np.float32)[None, None, :]
    d = i - j
    rel = np.stack([np.maximum(d, 0), np.maximum(-d, 0), d >= 0, d <= 0], axis=1).reshape(P, 4, 2 * CH)
    return {"ident_in": np.eye(P, dtype=np.float32), "rope_in": rope,
            "decay_exp_in": np.stack(exps, axis=1).astype(np.float32), "rel_in": rel.astype(np.float32)}


def build_program(nc, x, c, ctx, c_ctx, norm_w, w_ada, b_ada, w_in, ret_log2_decay,
                  q_norm_w, k_norm_w, w_o_ret, w_o_att, w_out,
                  ident_in, rope_in, decay_exp_in, rel_in, out):
    with ExitStack() as held:
        def sem(name):
            return held.enter_context(nc.semaphore(name))

        def sb(stack, name, shape, dt=F32):
            return stack.enter_context(nc.sbuf_tensor(name, shape, dt))

        def scratch(name, shape):
            return nc.dram_tensor(name, shape, F32, kind="Internal").ap()

        proj_x = scratch("proj_x", (NB, 4, P, 2 * W))
        proj_c = scratch("proj_c", (CTX_BLOCKS, P, CT * W))

        ident = sb(held, "ident", [P, P])
        vec_cols = sb(held, "vec_cols", [P, 48])
        mod = sb(held, "mod", [P, 3 * KT, 2])
        log_gamma = sb(held, "log_gamma", [P, 2 * RH])
        decay = sb(held, "decay", [P, RH * 10])
        head_decay = sb(held, "head_decay", [P, 10])
        head_gamma = sb(held, "head_gamma", [P, 2])
        kd_decay = sb(held, "kd_decay", [P, 2, 2])
        tile_rstd = sb(held, "tile_rstd", [P, AH])
        ssq_q = sb(held, "ssq_q", [P, TT, AH])
        ssq_k = sb(held, "ssq_k", [P, TT + CT, AKV])
        ps = held.enter_context(nc.psum_tensor("ps", [P, 8, W], F32))

        proj_mem = held.enter_context(ExitStack())
        hx_hi = sb(proj_mem, "hx_hi", [P, KT, SEQ], F32R)
        hx_lo = sb(proj_mem, "hx_lo", [P, KT, SEQ], F32R)
        hc_hi = sb(proj_mem, "hc_hi", [P, KT, CTX], F32R)
        hc_lo = sb(proj_mem, "hc_lo", [P, KT, CTX], F32R)
        w_raw, w_hi, w_lo = [None, None], [None, None], [None, None]

        def weight_slot(s):
            w_raw[s] = sb(proj_mem, f"w_raw{s}", [P, KT, W])
            w_hi[s] = sb(proj_mem, f"w_hi{s}", [P, KT, W], F32R)
            w_lo[s] = sb(proj_mem, f"w_lo{s}", [P, KT, W], F32R)

        weight_slot(0)
        with ExitStack() as m:
            xs = sb(m, "xs", [P, TT, D])
            ada = sb(m, "ada", [P, 4, KT, P])
            cs = sb(m, "cs", [P, CT, D])
            modulated = sb(m, "modulated", [P, 2, W])
            vec_rows = sb(m, "vec_rows", [48, P])
            ssq_x = sb(m, "ssq_x", [P, TT + CT])
            rms_x = sb(m, "rms_x", [P, TT + CT])
            rstd_x = sb(m, "rstd_x", [P, TT + CT])
            a_col = sb(m, "a_col", [P, KT, 2])
            square_junk = sb(m, "square_junk", [P, D])
            log2_decay = sb(m, "log2_decay", [P, 2 * RH])
            lg = sb(m, "lg", [P, 8, 2 * RH])
            decay_exp = sb(m, "decay_exp", [P, 10])
        weight_slot(1)
        stage = sb(proj_mem, "stage", [P, 2, 2 * W])
        stage_c = sb(proj_mem, "stage_c", [P, CT, W])
        heads_in = sb(proj_mem, "heads_in", [P, 2, W])
        heads_w = sb(proj_mem, "heads_w", [P, W])
        rope_t = sb(proj_mem, "rope_t", [P, W])
        rope_cs = sb(proj_mem, "rope_cs", [P, 2, TT, AD // 2])
        qk_norm = sb(proj_mem, "qk_norm", [P, 2, AD])
        head_junk = sb(proj_mem, "head_junk", [P, 4, AD])
        proj_mem.close()

        y_ret = scratch("y_ret", (RH * 4, P, SEQ))
        with ExitStack() as m:
            rel = sb(m, "rel", [P, 4, 2 * CH])
            rk_raw = sb(m, "rk_raw", [P, 2, SEQ])
            rq_raw = sb(m, "rq_raw", [P, 2, SEQ])
            rv_raw = sb(m, "rv_raw", [P, TT, RDV])
            ck_raw = sb(m, "ck_raw", [P, CT, RDK])
            cv_raw = sb(m, "cv_raw", [P, CT, RDV])
            rk = [sb(m, f"rk_{x}", [P, 2, SEQ], F32R) for x in ("hi", "lo")]
            rq = [sb(m, f"rq_{x}", [P, 2, SEQ], F32R) for x in ("hi", "lo")]
            rv = [sb(m, f"rv_{x}", [P, TT, RDV], F32R) for x in ("hi", "lo")]
            cv = [sb(m, f"cv_{x}", [P, CT, RDV], F32R) for x in ("hi", "lo")]
            kd = [[sb(m, f"kd{d}_{x}", [P, 2, RDK], F32R) for x in ("hi", "lo")] for d in range(2)]
            state = [sb(m, f"state{d}", [P, 2, RDV]) for d in range(2)]
            state_r = [[sb(m, f"state{d}_{x}", [P, 2, RDV], F32R) for x in ("hi", "lo")] for d in range(2)]
            probs = sb(m, "probs", [P, 2 * CH])
            probs_r = [sb(m, f"probs_{x}", [P, 2, CH], F32R) for x in ("hi", "lo")]
            mask = sb(m, "mask", [P, 2 * CH])
            mask_b = sb(m, "mask_b", [P, 2 * CH])
            ret_o = sb(m, "ret_o", [P, TT, RDV])
            ret_junk = sb(m, "ret_junk", [P, RDV])
            ret_ms = sb(m, "ret_ms", [P, 3, TT])
            gate_y = sb(m, "gate_y", [P, 4, SEQ])

        y_att = scratch("y_att", (AH, P, SEQ))
        KEYS = SEQ + CTX
        NKT = KEYS // P
        with ExitStack() as m:
            kv_raw = sb(m, "kv_raw", [P, NKT, W])
            ak = [sb(m, f"ak_{x}", [P, AKV, KEYS], F32R) for x in ("hi", "lo")]
            av = [sb(m, f"av_{x}", [P, NKT, AKV * AD], F32R) for x in ("hi", "lo")]
            aq_raw = sb(m, "aq_raw", [P, 2, W])
            aq = [sb(m, f"aq_{x}", [P, AH, P], F32R) for x in ("hi", "lo")]
            soft = [sb(m, f"soft{i}", [P, KEYS]) for i in range(2)]
            soft_t = [[sb(m, f"soft_t{g}_{x}", [P, NKT, 4, P], F32R) for x in ("hi", "lo")] for g in range(AKV)]
            att_y = sb(m, "att_y", [P, AH, SEQ])
            ada_g = sb(m, "ada_g", [P, KT, P])
            rms_q = sb(m, "rms_q", [P, TT * AH])
            rstd_q = sb(m, "rstd_q", [P, TT * AH])
            rms_k = sb(m, "rms_k", [P, NKT * AKV])
            rstd_k = sb(m, "rstd_k", [P, NKT * AKV])
            row_max = sb(m, "row_max", [P, 2, 4])
            neg_max = sb(m, "neg_max", [P, 2])
            row_sum = sb(m, "row_sum", [P, 2])
            row_inv = sb(m, "row_inv", [P, 2])

        with ExitStack() as m:
            y_raw = sb(m, "y_raw", [P, 2, 2, W])
            y_r = [sb(m, f"y_{x}", [P, 3 * KT, W], F32R) for x in ("hi", "lo")]
            ow_raw = [sb(m, f"ow_raw{i}", [P, KT, P]) for i in range(3)]
            ow = [[sb(m, f"ow{i}_{x}", [P, KT, P], F32R) for x in ("hi", "lo")] for i in range(3)]
            merge_gate = sb(m, "merge_gate", [P, 2, W])
            merged = sb(m, "merged", [P, 2, W])
            z_r = [sb(m, f"z_{x}", [P, KT, W], F32R) for x in ("hi", "lo")]
            out_t = sb(m, "out_t", [P, 2, W])
            res = sb(m, "res", [P, 4, D])

        ident_in_s, vec_in, small_in, ctx_in = sem("ident_in"), sem("vec_in"), sem("small_in"), sem("ctx_in")
        x_in = [sem(f"x_in{i}") for i in range(4)]
        ada_in = [sem(f"ada_in{i}") for i in range(4)]
        w_in_s = [sem(f"w_in{i}") for i in range(2)]
        vec_silu, vec_turned, vec_copied = sem("vec_silu"), sem("vec_turned"), sem("vec_copied")
        x_squared, ms_done, rms_done, x_normed = sem("x_squared"), sem("ms_done"), sem("rms_done"), sem("x_normed")
        ada_used, mod_done = sem("ada_used"), sem("mod_done")
        unit_turned, unit_modulated, unit_hi = sem("unit_turned"), sem("unit_modulated"), sem("unit_hi")
        unit_lo_pool, unit_lo_dve = sem("unit_lo_pool"), sem("unit_lo_dve")
        dve_step, lg_act, lg_dve, decay_done = sem("dve_step"), sem("lg_act"), sem("lg_dve"), sem("decay_done")
        w_hi_done, w_lo_done = sem("w_hi_done"), sem("w_lo_done")
        tile_done, tile_out = sem("tile_done"), sem("tile_out")
        heads_squared, heads_roped = sem("heads_squared"), sem("heads_roped")
        stored = [sem(f"stored{i}") for i in range(2)]
        stored_c = sem("stored_c")

        rel_in_s, ck_in, cv_in, rk_in, rq_in, rv_in, gate_in = (
            sem(n) for n in ("rel_in", "ck_in", "cv_in", "rk_in", "rq_in", "rv_in", "gate_in"))
        head_ready, kd_ready = sem("head_ready"), sem("kd_ready")
        cv_hi_done, cv_lo_done, g03_hi_done, g03_lo_pool, g03_lo_dve, g12_hi_done, g12_lo_done = (
            sem(n) for n in ("cv_hi", "cv_lo", "g03_hi", "g03_lo_pool", "g03_lo_dve", "g12_hi", "g12_lo"))
        k_turned, kd_hi_done, kd_lo_done = ([sem(f"{n}{d}") for d in range(2)] for n in ("k_turned", "kd_hi", "kd_lo"))
        delta_done, state_done, state_hi_done, state_lo_done, cross_done, cross_out = (
            [sem(f"{n}{d}") for d in range(2)]
            for n in ("delta_done", "state_done", "state_hi", "state_lo", "cross_done", "cross_out"))
        scores_done, probs_done, probs_hi_done, probs_lo_done, intra_done, intra_out = (
            sem(n) for n in ("scores_done", "probs_done", "probs_hi", "probs_lo", "intra_done", "intra_out"))
        mask_exp, mask_done = sem("mask_exp"), sem("mask_done")
        o_squared, o_ms, o_rms, o_rstd, o_normed, o_turned, y_out, y_stored = (
            sem(n) for n in ("o_squared", "o_ms", "o_rms", "o_rstd", "o_normed", "o_turned", "y_out", "y_stored"))

        PAIRS = ((0, 3), (1, 2))

        def both(v, pair):
            a, e = pair
            return v[:, a:e + 1:e - a]

        def chunks_of(v):
            return v.rearrange("p d (c i) -> p c d i", c=NCH)

        def v_chunks(v):
            return v.rearrange("p (c t) e -> p c (t e)", c=NCH)

        tile_ready = sem("tile_ready")
        kv_in, att_gate_in, ada_g_in = sem("kv_in"), sem("att_gate_in"), sem("ada_g_in")
        aq_in = [sem(f"aq_in{i}") for i in range(2)]
        ms_qk, rms_qk, rstd_qk, keys_normed, ak_turned, ak_hi_done, ak_lo_done, av_hi_done, av_lo_done = (
            sem(n) for n in ("ms_qk", "rms_qk", "rstd_qk", "keys_normed", "ak_turned", "ak_hi", "ak_lo", "av_hi", "av_lo"))
        aq_turned, aq_hi_done, aq_lo_done = sem("aq_turned"), sem("aq_hi"), sem("aq_lo")
        sc_bank, max_bank, max_all, neg_done, exp_done, inv_done, soft_done, soft_turned, soft_hi, soft_lo = (
            sem(n) for n in ("sc_bank", "max_bank", "max_all", "neg_done", "exp_done", "inv_done", "soft_done",
                             "soft_turned", "soft_hi", "soft_lo"))
        pv_done, att_out, att_stored, ada_g_done, gate_col = (
            sem(n) for n in ("pv_done", "att_out", "att_stored", "ada_g_done", "gate_col"))
        y_in = [sem(f"y_in{i}") for i in range(2)]
        ow_in = [sem(f"ow_in{i}") for i in range(3)]
        y_hi_done, y_lo_done, ow_hi_done, ow_lo_done, ow_used = (
            sem(n) for n in ("y_hi_done", "y_lo_done", "ow_hi_done", "ow_lo_done", "ow_used"))
        mg_in, mg_used, merged_part, merged_done, z_hi_done, z_lo_done = (
            sem(n) for n in ("mg_in", "mg_used", "merged_part", "merged_done", "z_hi", "z_lo"))
        res_in, out_gated, out_turned, out_added, out_stored = (
            sem(n) for n in ("res_in", "out_gated", "out_turned", "out_added", "out_stored"))

        HALVES = SEQ // W
        CHUNKS = 4 * KT

        def chunk_slot(c):
            return c % 3, c // 3

        SLOT_USES = (11, 11, 10)

        def bank_span(b, n):
            return ps[:, b:b + 3, :].rearrange("p b n -> p (b n)")[:, 0:n]

        def rstd_of(t, u):
            return tile_rstd[:, u:u + 1]

        def mod_col(t):
            return mod[:, bass.ds(t + 2 * KT, 1), 0:1].rearrange("p o v -> p (o v)")

        def row_of(v, n):
            return v[:, bass.ds(n, 1), :].rearrange("p o i -> p (o i)")

        def o_bank(g, e):
            return 0 if g == 0 else (6, 7, 1, 1)[e]

        O_GROUPS = ((2, 3, 4, 5), (6, 7, 0, 1))

        def decay_at(h, i):
            return head_decay[:, i:i + 1]

        UNITS_X, UNITS = 2 * KT, 3 * KT

        def unit_bank(u):
            return 2 + u % 6 if u < UNITS_X else 5 + (u - UNITS_X) % 3

        def unit_target(u):
            if u < UNITS_X:
                at = slice((u // KT) * W, (u // KT + 1) * W)
                return hx_hi[:, u % KT, at], hx_lo[:, u % KT, at]
            return hc_hi[:, u % KT, :], hc_lo[:, u % KT, :]

        def heads_index(b):
            return 0 if b == B_AKV else TT + CT

        def tiles_of(b0):
            return TT + CT if b0 < CTX_BLOCKS else TT

        class Steps:

            def __init__(self, eng, sem, start=0):
                self.eng, self.sem, self.n = eng, sem, start

            def then(self, ins):
                self.n = self.n + 1
                ins.then_inc(self.sem, 1)
                self.eng.wait_ge(self.sem, self.n)

        def split_lo_first(pool):
            pool.wait_ge(w_hi_done, 1)
            pool.tensor_tensor(w_lo[0][:], w_raw[0][:], w_hi[0][:].bitcast(F32), ALU.subtract).then_inc(w_lo_done, 1)

        def unit_hi_half(act, u):
            n = W if u < UNITS_X else CTX
            act.wait_ge(unit_modulated, u + 1)
            act.copy(unit_target(u)[0], modulated[:, u % 2, 0:n]).then_inc(unit_hi, 1)

        block = held.enter_context(nc.Block())

        @block.sync
        def _(sp):
            sp.dma_start(ident[:], ident_in).then_inc(ident_in_s, 16)
            sp.dma_start(vec_rows[0:8, :], c.rearrange("o (k p) -> (o k) p", p=P)).then_inc(vec_in, 16)
            sp.dma_start(vec_rows[8:16, :], c_ctx.rearrange("(k p) -> k p", p=P)).then_inc(vec_in, 16)
            sp.dma_start(vec_rows[16:24, :], norm_w.rearrange("o (k p) -> (o k) p", p=P)).then_inc(vec_in, 16)
            sp.dma_start(vec_rows[24:48, :], b_ada.rearrange("o (k p) -> (o k) p", p=P)).then_inc(vec_in, 16)
            x_tiles = x[0].rearrange("(t p) d -> p t d", p=P)
            for i in range(4):
                sp.dma_start(xs[:, 2 * i:2 * i + 2, :], x_tiles[:, 2 * i:2 * i + 2, :]).then_inc(x_in[i], 16)
            ada_tiles = w_ada[0].rearrange("(k p) n -> p k n", p=P)
            for n in range(2 * KT):
                if n >= 4:
                    sp.wait_ge(ada_used, n - 3)
                sp.dma_start(ada[:, n % 4], ada_tiles[:, :, n * P:(n + 1) * P]).then_inc(ada_in[n % 4], 16)

            w_tiles = w_in[0].rearrange("(k p) n -> p k n", p=P)

            def load_weights(b, s):
                sp.dma_start(w_raw[s][:], w_tiles[:, :, bass.ds(b * W, W)]).then_inc(w_in_s[s], 16)

            load_weights(0, 0)
            sp.dma_start(cs[:], ctx[0].rearrange("(t p) d -> p t d", p=P)).then_inc(ctx_in, 16)
            sp.wait_ge(unit_lo_pool, UNITS // 2)
            sp.wait_ge(unit_lo_dve, UNITS // 2)
            sp.wait_ge(unit_hi, UNITS)
            sp.wait_ge(decay_done, 8)
            load_weights(1, 1)
            rope_src = rope_in.rearrange("s (t p) e -> s p t e", p=P)
            for i in range(2):
                sp.dma_start(rope_cs[:, i], rope_src[i]).then_inc(small_in, 16)
                sp.dma_start(qk_norm[:, i, :], (q_norm_w if i == 0 else k_norm_w).partition_broadcast(P)
                             .rearrange("p o d -> p (o d)")).then_inc(small_in, 16)

            def project(b, s, more, kind):
                if more:
                    sp.wait_ge(w_hi_done, b + 1)
                    sp.wait_ge(w_lo_done, b + 1)
                    load_weights(b + 2, s)
                for g in range(4):
                    if kind in ("akv", "aq"):
                        base = 0 if kind == "akv" else TT + CT + (b - B_AQ) * TT
                        sp.wait_ge(heads_roped, base + 2 * g + 2)
                    else:
                        n0 = 10 * b if kind in ("rk", "rv") else 10 * CTX_BLOCKS + 8 * (b - CTX_BLOCKS)
                        sp.wait_ge(tile_out, n0 + 2 * g + 2)
                    sp.dma_start(proj_x[b, g], stage[:, g % 2, :]).then_inc(stored[g % 2], 16)
                if kind in ("rk", "rv", "akv"):
                    if kind == "akv":
                        sp.wait_ge(heads_roped, TT + CT)
                    else:
                        sp.wait_ge(tile_out, 10 * b + 10)
                    sp.dma_start(proj_c[b], stage_c[:].rearrange("p t n -> p (t n)")).then_inc(stored_c, 16)

            project(0, 0, True, "rk")
            project(1, 1, True, "rk")
            with sp.Fori(B_RV, B_AKV, 2) as b:
                project(b, 0, True, "rv")
                project(b + 1, 1, True, "rv")
            project(B_AKV, 0, True, "akv")
            with sp.Fori(B_RQ, B_AQ, 2) as b:
                project(b, 1, True, "t")
                project(b + 1, 0, True, "t")
            project(B_AQ, 1, True, "aq")
            project(B_AQ + 1, 0, True, "aq")
            with sp.Fori(B_AG, NB - 3, 2) as b:
                project(b, 1, True, "t")
                project(b + 1, 0, True, "t")
            project(NB - 2, 1, False, "t")
            project(NB - 1, 0, False, "t")
            for s in range(2):
                sp.wait_ge(stored[s], 16 * 2 * NB)
            sp.wait_ge(stored_c, 16 * CTX_BLOCKS)

            groups = proj_x.rearrange("b g p n -> (b g) p n")
            sp.dma_start(rel[:], rel_in).then_inc(rel_in_s, 16)

            def load_head(h, first):
                pair, at = (h // 2, h % 2 * RDK) if isinstance(h, int) else (sp.snap(h // 2), sp.snap(h % 2 * RDK))
                k_at, v_at, q_at = 4 * B_RK + 2 * h, 4 * B_RV + 4 * h, 4 * B_RQ + 2 * h
                if not first:
                    sp.wait_ge(g03_lo_pool, 2 * h)
                    sp.wait_ge(kd_lo_done[0], 4 * h - 3)
                    sp.wait_ge(kd_lo_done[1], 4 * h - 3)
                sp.dma_start(ck_raw[:], proj_c[bass.ds(pair, 1)].rearrange("b p (t n) -> p (b t) n", t=CT)
                             [:, :, bass.ds(at, RDK)]).then_inc(ck_in, 16)
                if not first:
                    sp.wait_ge(cv_lo_done, h)
                sp.dma_start(cv_raw[:], proj_c[B_RV + h].rearrange("p (t n) -> p t n", t=CT)).then_inc(cv_in, 16)
                if not first:
                    sp.wait_ge(g12_lo_done, 3 * h)
                    sp.wait_ge(g03_lo_dve, h)
                    sp.wait_ge(k_turned[0], 3 * h)
                    sp.wait_ge(k_turned[1], 3 * h)
                sp.dma_start(rk_raw[:], groups[bass.ds(k_at, 2)].rearrange("g p n -> p g n")).then_inc(rk_in, 16)
                sp.dma_start(rv_raw[:], groups[bass.ds(v_at, 4)].rearrange("g p (t e) -> p g t e", t=2)).then_inc(rv_in, 16)
                sp.dma_start(rq_raw[:], groups[bass.ds(q_at, 2)].rearrange("g p n -> p g n")).then_inc(rq_in, 16)

            def load_gate(h):
                sp.dma_start(gate_y[:], groups[bass.ds(4 * B_RG + 4 * h, 4)].rearrange("g p n -> p g n")).then_inc(gate_in, 16)

            def store_y(h):
                sp.wait_ge(y_out, 8 * h + 8)
                sp.dma_start(y_ret[bass.ds(4 * h, 4)].rearrange("g p n -> p g n"), gate_y[:]).then_inc(y_stored, 16)
                sp.wait_ge(y_stored, 16 * h + 16)

            load_head(0, True)
            load_gate(0)
            with sp.Fori(1, RH) as h:
                load_head(h, False)
                store_y(h - 1)
                load_gate(h)
            store_y(RH - 1)

            sp.wait_ge(y_out, 8 * RH)
            for i, src in ((0, groups[4 * B_AKV:4 * B_AKV + 4].rearrange("g p n -> p g n")), (TT, proj_c[B_AKV])):
                n = TT if i == 0 else CT
                dst = kv_raw[:, i:i + n, :].rearrange("p t n -> p (t n)")
                if i == 0:
                    dst = dst.rearrange("p (g n) -> p g n", g=4)
                sp.dma_start(dst, src).then_inc(kv_in, 16)

            def load_queries(t, half):
                pair, at = (t // 2, t % 2 * W) if isinstance(t, int) else (sp.snap(t // 2), sp.snap(t % 2 * W))
                if not (isinstance(t, int) and t == 0):
                    sp.wait_ge(aq_turned, 2 * t - 1 + half)
                row = groups[bass.ds(pair + 4 * (B_AQ + half), 1)].rearrange("g p n -> (g p) n")
                sp.dma_start(aq_raw[:, half, :], row[:, bass.ds(at, W)]).then_inc(aq_in[half], 16)

            def load_ada_gate(t):
                if not (isinstance(t, int) and t == 0):
                    sp.wait_ge(ada_g_done, t)
                sp.dma_start(ada_g[:], ada_tiles[:, :, bass.ds((t + 2 * KT) * P, P)]).then_inc(ada_g_in, 16)

            load_queries(0, 0)
            load_queries(0, 1)
            load_ada_gate(0)
            sp.dma_start(att_y[:], groups[4 * B_AG:4 * B_AG + 8].rearrange("g p n -> p g n")).then_inc(att_gate_in, 16)
            with sp.Fori(1, TT) as t:
                load_queries(t, 0)
                load_queries(t, 1)
                load_ada_gate(t)
            for half in range(HALVES):
                sp.wait_ge(att_out, 8 * half + 8)
                sp.dma_start(y_att.rearrange("h p n -> p h n")[:, :, half * W:(half + 1) * W],
                             att_y[:, :, half * W:(half + 1) * W]).then_inc(att_stored, 16)
            sp.wait_ge(att_stored, 16 * HALVES)
            sp.wait_ge(gate_col, TT)
            sp.wait_ge(pv_done, 2 * TT)
            ow_ret = w_o_ret[0].rearrange("(b k p) n -> b p k n", p=P, k=KT)
            ow_att = w_o_att[0].rearrange("(k p) n -> p k n", p=P)
            ow_out = w_out[0].rearrange("(k p) n -> p k n", p=P)
            x_rows = x[0].rearrange("(t p) d -> p t d", p=P)
            out_rows = out[0].rearrange("(t p) d -> p t d", p=P)

            def load_chunk(half, c, slot, src):
                done = CHUNKS * half + c
                if not (isinstance(c, int) and half == 0 and c < 3):
                    sp.wait_ge(ow_lo_done, done - (1 if half and isinstance(c, int) and c < 2 else 2))
                sp.dma_start(ow_raw[slot][:], src).then_inc(ow_in[slot], 16)

            def load_merge(half, n):
                at = bass.ds(n * P, P)
                load_chunk(half, 3 * n, 0, ow_ret[0][:, :, at])
                load_chunk(half, 3 * n + 1, 1, ow_ret[1][:, :, at])
                load_chunk(half, 3 * n + 2, 2, ow_att[:, :, at])
                if not (isinstance(n, int) and half == 0 and n == 0):
                    sp.wait_ge(mg_used, KT * half + n)
                for i, b in enumerate((B_MR, B_MA)):
                    src = groups[bass.ds(n + 4 * b, 1)].rearrange("g p n -> (g p) n")
                    sp.dma_start(merge_gate[:, i, :], src[:, half * W:(half + 1) * W]).then_inc(mg_in, 16)

            def load_y(half, i):
                src = y_ret if i < KT else y_att
                a = 2 * i if i < KT else 2 * i - 2 * KT
                if half or i >= 2:
                    sp.wait_ge(y_lo_done, 3 * KT * half + 2 * i - 2)
                sp.dma_start(y_raw[:, i % 2], src[a:a + 2].rearrange("g p n -> p g n")[:, :, half * W:(half + 1) * W]).then_inc(y_in[i % 2], 16)

            for half in range(HALVES):
                if half == 0:
                    load_y(0, 0)
                    load_y(0, 1)
                    load_merge(half, 0)
                    for i in range(2, 3 * KT // 2):
                        load_y(0, i)
                else:
                    load_merge(half, 0)
                with sp.Fori(1, KT) as n:
                    load_merge(half, n)
                if half:
                    sp.wait_ge(out_stored, 16)
                sp.dma_start(res[:], x_rows[:, 4 * half:4 * half + 4, :]).then_inc(res_in, 16)
                for n in range(KT + 3):
                    if n < KT:
                        load_chunk(half, 3 * KT + n, n % 3, ow_out[:, :, n * P:(n + 1) * P])
                    if half == 0 and n >= 3:
                        n -= 3
                        for i in range(12 * n // 8, 12 * (n + 1) // 8):
                            load_y(1, i)
                sp.wait_ge(out_added, KT * half + KT)
                sp.dma_start(out_rows[:, 4 * half:4 * half + 4, :], res[:]).then_inc(out_stored, 16)
            sp.wait_ge(out_stored, 16 * HALVES)

        @block.gpsimd
        def _(pool):
            for u in range(0, UNITS, 2):
                hi, lo = unit_target(u)
                n = W if u < UNITS_X else CTX
                pool.wait_ge(unit_hi, u + 1)
                pool.tensor_tensor(lo, modulated[:, u % 2, 0:n], hi.bitcast(F32), ALU.subtract).then_inc(unit_lo_pool, 1)
                if u == UNITS_X - 2:
                    split_lo_first(pool)

            def split_lo(b, s):
                pool.wait_ge(w_hi_done, b + 1)
                pool.tensor_tensor(w_lo[s][:], w_raw[s][:], w_hi[s][:].bitcast(F32), ALU.subtract).then_inc(w_lo_done, 1)

            split_lo(1, 1)
            with pool.Fori(2, NB - 1, 2) as b:
                split_lo(b, 0)
                split_lo(b + 1, 1)
            split_lo(NB - 1, 0)

            def lo(dst, hi, whole, done):
                pool.tensor_tensor(dst, whole, hi.bitcast(F32), ALU.subtract).then_inc(done, 1)

            def context_lo(h):
                pool.wait_ge(cv_hi_done, h + 1)
                lo(cv[1][:], cv[0][:], cv_raw[:], cv_lo_done)

            def outer_lo(h):
                for i, (r, raw) in enumerate(((rk, rk_raw), (rq, rq_raw))):
                    pool.wait_ge(g03_hi_done, 3 * h + i + 1)
                    lo(both(chunks_of(r[1]), PAIRS[0]), both(chunks_of(r[0]), PAIRS[0]), both(chunks_of(raw), PAIRS[0]), g03_lo_pool)

            def head(h, last):
                for s in range(NCH):
                    pool.wait_ge(probs_hi_done, NCH * h + s + 1)
                    lo(probs_r[1][:].rearrange("p t i -> p (t i)"), probs_r[0][:].rearrange("p t i -> p (t i)"), probs[:], probs_lo_done)
                    if s == 0:
                        for i, (r, raw, view) in enumerate(((rk, rk_raw, chunks_of), (rq, rq_raw, chunks_of), (rv, rv_raw, v_chunks))):
                            pool.wait_ge(g12_hi_done, 3 * h + i + 1)
                            lo(both(view(r[1]), PAIRS[1]), both(view(r[0]), PAIRS[1]), both(view(raw), PAIRS[1]), g12_lo_done)
                    if s == 2 and not last:
                        context_lo(h + 1)
                    if s == 3 and not last:
                        outer_lo(h + 1)

            context_lo(0)
            outer_lo(0)
            with pool.Fori(0, RH - 1) as h:
                head(h, False)
            head(RH - 1, True)

            pool.wait_ge(av_hi_done, 1)
            lo(av[1][:], av[0][:], kv_raw[:, :, AKV * AD:], av_lo_done)

            def split_chunk(half, c, slot, uses):
                pool.wait_ge(ow_hi_done, CHUNKS * half + c + 1)
                lo(ow[slot][1][:], ow[slot][0][:], ow_raw[slot][:], ow_lo_done)

            for half in range(HALVES):
                for i in range(3):
                    split_chunk(half, i, i, SLOT_USES[i] * half + 1)
                with pool.Fori(1, KT) as n:
                    for i in range(3):
                        split_chunk(half, 3 * n + i, i, SLOT_USES[i] * half + n + 1)
                for c in range(3 * KT, CHUNKS):
                    split_chunk(half, c, c % 3, SLOT_USES[c % 3] * half + c // 3 + 1)


        @block.scalar
        def _(act):
            act.dma_start(log2_decay[:], ret_log2_decay[0].rearrange("a h -> (a h)").partition_broadcast(P)).then_inc(small_in, 16)
            act.dma_start(decay_exp[:], decay_exp_in).then_inc(small_in, 16)
            act.wait_ge(vec_in, 64)
            act.activation(vec_rows[0:16, :], vec_rows[0:16, :], ACT.Silu).then_inc(vec_silu, 1)
            for t in range(TT + CT):
                if t < TT:
                    act.wait_ge(x_in[t // 2], 16)
                else:
                    act.wait_ge(ctx_in, 16)
                if t:
                    act.wait_ge(x_squared, t)
                src = xs[:, t, :] if t < TT else cs[:, t - TT, :]
                act.activation(square_junk[:], src, ACT.Square, accum_out=ssq_x[:, t:t + 1]).then_inc(x_squared, 1)
                for i, (a, e) in enumerate(NORM_GROUPS):
                    if t == e - 1:
                        act.wait_ge(ms_done, i + 1)
                        act.activation(rms_x[:, a:e], rms_x[:, a:e], ACT.Sqrt).then_inc(rms_done, 1)
                if t == TT - 1:
                    for u in range(UNITS_X):
                        unit_hi_half(act, u)
            for u in range(UNITS_X, UNITS):
                unit_hi_half(act, u)
            act.wait_ge(small_in, 32)
            act.activation(lg[:, 0, :], log2_decay[:], ACT.Exp, scale=LN2).then_inc(lg_act, 1)
            act.wait_ge(lg_dve, 1)
            act.activation(lg[:, 2, :], lg[:, 1, :], ACT.Ln).then_inc(lg_act, 1)
            act.wait_ge(lg_dve, 2)
            for h in range(RH):
                for d in range(2):
                    act.activation(decay[:, 10 * h + 5 * d:10 * h + 5 * d + 5], decay_exp[:, 5 * d:5 * d + 5], ACT.Exp,
                                   scale=log_gamma[:, RH * d + h:RH * d + h + 1]).then_inc(decay_done, 1)

            def plain_tile(b, n0, j, bank, func, scale):
                act.wait_ge(tile_done, n0 + j + 1)
                if j < TT:
                    g = j // 2
                    if j % 2 == 0 and not (isinstance(b, int) and b == 0 and g < 2):
                        act.wait_ge(stored[g % 2], 16 * (2 * b + g // 2))
                    dst = stage[:, g % 2, (j % 2) * W:(j % 2 + 1) * W]
                else:
                    if j == TT and not (isinstance(b, int) and b == 0):
                        act.wait_ge(stored_c, 16 * b)
                    dst = stage_c[:, j - TT, :]
                act.activation(dst, ps[:, bank, :], func, scale=scale).then_inc(tile_out, 1)

            def heads_tile(k, n, j, tiles, heads, stat):
                act.wait_ge(tile_done, n + 1)
                if not (isinstance(k, int) and k < 2):
                    act.wait_ge(heads_roped, k - 1)
                if not (isinstance(k, int) and k < 1):
                    act.wait_ge(heads_squared, k)
                act.copy(heads_in[:, j % 2, :], ps[:, j % (tiles // 2), :]).then_inc(tile_out, 1)
                act.wait_ge(tile_out, n + 1)
                for h in range(heads):
                    sq = act.activation(head_junk[:, h, :], heads_in[:, j % 2, h * AD:(h + 1) * AD], ACT.Square,
                                        accum_out=stat[:, h:h + 1])
                sq.then_inc(heads_squared, 1)

            for b in range(B_RV):
                for j in range(TT + CT):
                    plain_tile(b, 10 * b, j, j % 5, ACT.Copy, RDK ** -0.5)
            with act.Fori(B_RV, B_AKV, 1) as b:
                for j in range(TT + CT):
                    plain_tile(b, 10 * b, j, j % 5, ACT.Copy, 1.0)
            for j in range(TT + CT):
                heads_tile(j, 10 * B_AKV + j, j, TT + CT, AKV, ssq_k[:, j, :])
            act.wait_ge(heads_roped, TT + CT)
            with act.Fori(B_RQ, B_RG, 1) as b:
                for j in range(TT):
                    plain_tile(b, 8 * b + 14, j, j % 4, ACT.Copy, 1.0)
            with act.Fori(B_RG, B_AQ, 1) as b:
                for j in range(TT):
                    plain_tile(b, 8 * b + 14, j, j % 4, ACT.Silu, 1.0)
            for i in range(2):
                for j in range(TT):
                    heads_tile(TT + CT + TT * i + j, 8 * (B_AQ + i) + 14 + j, j, TT, 4, ssq_q[:, j, 4 * i:4 * i + 4])
            act.wait_ge(heads_roped, TT + CT + 2 * TT)
            with act.Fori(B_AG, B_MR, 1) as b:
                for j in range(TT):
                    plain_tile(b, 8 * b + 14, j, j % 4, ACT.Silu, 1.0)
            with act.Fori(B_MR, NB, 1) as b:
                for j in range(TT):
                    plain_tile(b, 8 * b + 14, j, j % 4, ACT.Sigmoid, 1.0)

            def kd_hi(h, m, d):
                if not (isinstance(h, int) and h == 0 and m == 0):
                    act.wait_ge(delta_done[d], 4 * h + m)
                if m == 0:
                    act.wait_ge(ck_in, 16 * h + 16)
                else:
                    act.wait_ge(k_turned[d], 3 * h + m)
                for j in range(2):
                    src = ck_raw[:, j, :] if m == 0 else ps[:, 0, j * RDK:(j + 1) * RDK]
                    ins = act.activation(kd[d][0][:, j, :], src, ACT.Copy, scale=kd_decay[:, d, j:j + 1])
                ins.then_inc(kd_hi_done[d], 1)

            def state_hi(h, m, d):
                act.wait_ge(state_done[d], 4 * h + m + 1)
                if not (isinstance(h, int) and h == 0 and m == 0):
                    act.wait_ge(cross_done[d], 4 * h + m)
                act.copy(state_r[d][0][:], state[d][:]).then_inc(state_hi_done[d], 1)

            def o_squares(h, g):
                first = isinstance(h, int) and h == 0 and g == 0
                act.wait_ge(intra_out, 4 * h + 3 + g)
                act.wait_ge(cross_out[1], 4 * h + 3 + g)
                for i, t in enumerate(O_GROUPS[g]):
                    if not (first and i == 0):
                        act.wait_ge(o_squared, 8 * h + 4 * g + i)
                    act.activation(ret_junk[:], ret_o[:, t, :], ACT.Square,
                                   accum_out=ret_ms[:, 0, 4 * g + i:4 * g + i + 1]).then_inc(o_squared, 1)

            def o_root(h, g):
                act.wait_ge(o_ms, 2 * h + g + 1)
                act.activation(ret_ms[:, 1, 4 * g:4 * g + 4], ret_ms[:, 1, 4 * g:4 * g + 4], ACT.Sqrt).then_inc(o_rms, 1)

            def o_scale(h, g):
                act.wait_ge(o_rstd, 2 * h + g + 1)
                for i, t in enumerate(O_GROUPS[g]):
                    ins = act.activation(ret_o[:, t, :], ret_o[:, t, :], ACT.Copy, scale=ret_ms[:, 2, 4 * g + i:4 * g + i + 1])
                ins.then_inc(o_normed, 1)

            def cross_first(h, s, d):
                c = s if d == 0 else NCH - 1 - s
                act.wait_ge(cross_done[d], 4 * h + s + 1)
                act.wait_ge(head_ready, h + 1)
                if not (isinstance(h, int) and h == 0):
                    act.wait_ge(o_turned, 8 * h)
                for i in range(2):
                    ins = act.activation(ret_o[:, 2 * c + i, :], ps[:, 2 + 2 * d + i, :], ACT.Copy, scale=decay_at(h, 5 * d + i))
                ins.then_inc(cross_out[d], 1)

            def context_keys(h):
                act.wait_ge(kd_ready, 2 * h + 2)
                kd_hi(h, 0, 0)
                kd_hi(h, 0, 1)

            def mask_exps(h):
                if not (isinstance(h, int) and h == 0):
                    act.wait_ge(probs_done, 4 * h)
                for d, m in enumerate((mask, mask_b)):
                    act.activation(m[:], rel[:, d, :], ACT.Exp, scale=head_gamma[:, d:d + 1]).then_inc(mask_exp, 1)

            def probs_hi(h, s):
                act.wait_ge(probs_done, 4 * h + s + 1)
                if not (isinstance(h, int) and h == 0 and s == 0):
                    act.wait_ge(intra_done, 4 * h + s)
                act.copy(probs_r[0][:].rearrange("p t i -> p (t i)"), probs[:]).then_inc(probs_hi_done, 1)

            def head(h, last):
                first = isinstance(h, int) and h == 0
                for s in range(NCH):
                    if s == 0 and not first:
                        o_squares(h - 1, 1)
                    state_hi(h, s, 0)
                    if s == 0 and not first:
                        o_root(h - 1, 1)
                    state_hi(h, s, 1)
                    if s == 0 and not first:
                        o_scale(h - 1, 1)
                    probs_hi(h, s)
                    if s == 1:
                        cross_first(h, s, 0)
                    if s < NCH - 1:
                        kd_hi(h, s + 1, 0)
                    if s == 1:
                        cross_first(h, s, 1)
                    if s < NCH - 1:
                        kd_hi(h, s + 1, 1)
                    if s == 0:
                        cross_first(h, s, 0)
                        cross_first(h, s, 1)
                if not last:
                    context_keys(h + 1)
                o_squares(h, 0)
                if not last:
                    mask_exps(h + 1)
                o_root(h, 0)
                o_scale(h, 0)

            act.wait_ge(rel_in_s, 16)
            context_keys(0)
            mask_exps(0)
            head(0, False)
            with act.Fori(1, RH - 1) as h:
                head(h, False)
            head(RH - 1, True)
            o_squares(RH - 1, 1)
            o_root(RH - 1, 1)
            o_scale(RH - 1, 1)

            act.wait_ge(ms_qk, 1)
            act.activation(rms_k[:], rms_k[:], ACT.Sqrt)
            act.activation(rms_q[:], rms_q[:], ACT.Sqrt).then_inc(rms_qk, 1)
            for g in range(AKV):
                act.wait_ge(ak_turned, g + 1)
                act.copy(ak[0][:, g, :], bank_span(3 * g, KEYS)).then_inc(ak_hi_done, 1)

            def queries_hi(t, half):
                act.wait_ge(aq_turned, 2 * t + half + 1)
                act.copy(aq[0][:, 4 * half:4 * half + 4, :].rearrange("p h i -> p (h i)"), ps[:, 6, :]).then_inc(aq_hi_done, 1)

            def exponent(t, u):
                k = AH * t + u
                act.wait_ge(neg_done, k + 1)
                if not (isinstance(t, int) and t == 0 and u < 2):
                    act.wait_ge(soft_turned, k - 1)
                act.activation(soft[u % 2][:], bank_span(0, KEYS), ACT.Exp, bias=neg_max[:, u % 2:u % 2 + 1],
                               scale=rstd_of(t, u), accum_out=row_sum[:, u % 2:u % 2 + 1]).then_inc(exp_done, 1)

            def scale_soft(t, u):
                k = AH * t + u
                act.wait_ge(inv_done, k + 1)
                act.activation(soft[u % 2][:], soft[u % 2][:], ACT.Copy, scale=row_inv[:, u % 2:u % 2 + 1]).then_inc(soft_done, 1)

            def soft_hi_half(t, u):
                k = AH * t + u
                act.wait_ge(soft_turned, k + 1)
                act.copy(soft_t[u // 4][0][:, :, u % 4, :], bank_span(3, KEYS).rearrange("p (k i) -> p k i", k=NKT)).then_inc(soft_hi, 1)

            def tile(t):
                first = isinstance(t, int) and t == 0
                for u in range(AH):
                    exponent(t, u)
                    scale_soft(t, u)
                    if u > 0:
                        soft_hi_half(t, u - 1)
                    elif not first:
                        soft_hi_half(t - 1, AH - 1)
                    if u == 1:
                        queries_hi(t, 1)
                    if u == 5 and not (isinstance(t, int) and t == TT - 1):
                        queries_hi(t + 1, 0)

            queries_hi(0, 0)
            tile(0)
            with act.Fori(1, TT - 1) as t:
                tile(t)
            tile(TT - 1)
            soft_hi_half(TT - 1, AH - 1)

            def chunk_hi(half, c, slot, uses):
                act.wait_ge(ow_in[slot], 16 * uses)
                if not (isinstance(c, int) and half == 0 and c < 3):
                    act.wait_ge(ow_used, CHUNKS * half + c - (1 if half and isinstance(c, int) and c < 2 else 2))
                act.copy(ow[slot][0][:], ow_raw[slot][:]).then_inc(ow_hi_done, 1)

            def chunk_hi_at(half, c):
                chunk_hi(half, c, c % 3, SLOT_USES[c % 3] * half + c // 3 + 1)

            def y_hi(half, i):
                act.wait_ge(y_in[(i // 2) % 2], 16 * (3 * KT // 4 * half + i // 4 + 1))
                act.copy(y_r[0][:, i, :], y_raw[:, (i // 2) % 2, i % 2, :]).then_inc(y_hi_done, 1)

            for half in range(HALVES):
                for c in range(3):
                    chunk_hi_at(half, c)
                if half == 0:
                    for i in range(3 * KT):
                        y_hi(0, i)
                with act.Fori(1, KT) as n:
                    for i in range(3):
                        chunk_hi(half, 3 * n + i, i, SLOT_USES[i] * half + n + 1)
                for c in range(3):
                    chunk_hi_at(half, 3 * KT + c)
                for n in range(KT):
                    k = KT * half + n
                    act.wait_ge(ow_used, CHUNKS * half + 3 * KT + n + 1)
                    if k >= 2:
                        act.wait_ge(out_turned, k - 1)
                    act.activation(out_t[:, n % 2, :], ps[:, 2 + n % 2, :], ACT.Copy, scale=mod[:, 2 * KT + n, 0:1]).then_inc(out_gated, 1)
                    if n + 3 < KT:
                        chunk_hi_at(half, 3 * KT + n + 3)
                    if half == 0:
                        for i in range(3 * n, 3 * n + 3):
                            y_hi(1, i)

        @block.vector
        def _(dve):
            own = Steps(dve, dve_step)
            dve.wait_ge(vec_turned, 1)
            dve.tensor_copy(vec_cols[:], ps[:, 0, 0:48]).then_inc(vec_copied, 1)

            def norm_group(i):
                a, e = NORM_GROUPS[i]
                dve.wait_ge(x_squared, e)
                dve.tensor_scalar(rms_x[:, a:e], ssq_x[:, a:e], 1.0 / D, EPS, ALU.mult, ALU.add).then_inc(ms_done, 1)
                dve.wait_ge(rms_done, i + 1)
                own.then(dve.reciprocal(rstd_x[:, a:e], rms_x[:, a:e]))
                for t in range(a, e):
                    v = xs[:, t, :] if t < TT else cs[:, t - TT, :]
                    dve.tensor_scalar(v, v, rstd_x[:, t:t + 1], None, ALU.mult).then_inc(x_normed, 1)

            def unit(u):
                hi, lo = unit_target(u)
                n = W if u < UNITS_X else CTX
                v = 0 if u < UNITS_X else 1
                dve.wait_ge(unit_turned, u + 1)
                if u >= 2:
                    dve.wait_ge(unit_hi, u - 1)
                    if u % 2:
                        dve.wait_ge(unit_lo_dve, (u - 1) // 2)
                    else:
                        dve.wait_ge(unit_lo_pool, u // 2)
                dve.tensor_scalar(modulated[:, u % 2, 0:n], ps[:, unit_bank(u), 0:n], a_col[:, u % KT, v:v + 1],
                                  mod[:, u % KT, v:v + 1], ALU.mult, ALU.add).then_inc(unit_modulated, 1)

            def unit_lo(u):
                hi, lo = unit_target(u)
                n = W if u < UNITS_X else CTX
                dve.wait_ge(unit_hi, u + 1)
                dve.tensor_tensor(lo, modulated[:, u % 2, 0:n], hi.bitcast(F32), ALU.subtract).then_inc(unit_lo_dve, 1)

            norm_group(0)
            norm_group(1)
            dve.wait_ge(ada_used, 2 * KT)
            own.then(dve.tensor_tensor(mod[:, 0:2 * KT, :], ps[:, 1, 0:4 * KT].rearrange("p (n v) -> p n v", v=2),
                                       vec_cols[:, 24:24 + 2 * KT].unsqueeze(2).to_broadcast([P, 2 * KT, 2]), ALU.add))
            own.then(dve.tensor_scalar(a_col[:], mod[:, KT:2 * KT, :], 1.0, None, ALU.add))
            own.then(dve.tensor_tensor(a_col[:], a_col[:], vec_cols[:, 16:24].unsqueeze(2).to_broadcast([P, KT, 2]),
                                       ALU.mult))

            def split_hi(b, s, used_tiles, loads):
                if used_tiles is not None:
                    dve.wait_ge(tile_done, used_tiles)
                dve.wait_ge(w_in_s[s], 16 * loads)
                dve.tensor_copy(w_hi[s][:], w_raw[s][:]).then_inc(w_hi_done, 1)

            for u in range(UNITS_X):
                unit(u)
                if u % 2:
                    unit_lo(u)
                if u == 3:
                    split_hi(0, 0, None, 1)
            norm_group(2)
            for u in range(UNITS_X, UNITS):
                unit(u)
                if u % 2:
                    unit_lo(u)
            dve.wait_ge(lg_act, 1)
            u_, w_, ln_, d_, m_, r_ = (lg[:, i, :] for i in range(6))
            dve.tensor_scalar(w_, u_, -1.0, 1.0, ALU.mult, ALU.add).then_inc(lg_dve, 1)
            dve.wait_ge(lg_dve, 1)
            own.then(dve.tensor_scalar(d_, w_, -1.0, None, ALU.add))
            own.then(dve.tensor_scalar(m_, d_, 0.0, None, ALU.is_equal))
            own.then(dve.tensor_tensor(d_, d_, m_, ALU.add))
            own.then(dve.reciprocal(r_, d_))
            own.then(dve.tensor_tensor(r_, r_, u_, ALU.mult))
            dve.wait_ge(lg_act, 2)
            own.then(dve.tensor_tensor(r_, r_, ln_, ALU.mult))
            own.then(dve.tensor_tensor(m_, m_, u_, ALU.mult))
            own.then(dve.tensor_tensor(r_, r_, m_, ALU.add))
            dve.tensor_scalar(log_gamma[:], r_, -1.0, None, ALU.mult).then_inc(lg_dve, 1)

            def rotate_tile(k, n, j, heads, t, w_index, dst, slot_free):
                src = heads_in[:, j % 2, :]
                dve.wait_ge(tile_out, n + 1)
                slot_free()
                wide = heads * AD
                bcast = qk_norm[:, w_index, :].unsqueeze(1).to_broadcast([P, heads, AD])
                to = heads_w[:, 0:wide] if t is not None else dst[:, 0:wide]
                if wide < W:
                    own.then(dve.tensor_copy(dst[:, wide:W], src[:, wide:W]))
                ins = dve.tensor_tensor(to.rearrange("p (h e) -> p h e", h=heads),
                                        src[:, 0:wide].rearrange("p (h e) -> p h e", h=heads), bcast, ALU.mult)
                if t is None:
                    ins.then_inc(heads_roped, 1)
                    return
                own.then(ins)

                def pairs(v):
                    return v[:, 0:wide].rearrange("p (h e two) -> p h e two", h=heads, two=2)

                def table(i):
                    return rope_cs[:, i, t, :].unsqueeze(1).to_broadcast([P, heads, AD // 2])

                xw, rot, d = pairs(heads_w), pairs(rope_t), pairs(dst)
                dve.tensor_tensor(d[:, :, :, 0], xw[:, :, :, 0], table(0), ALU.mult)
                own.then(dve.tensor_tensor(d[:, :, :, 1], xw[:, :, :, 1], table(0), ALU.mult))
                dve.tensor_tensor(rot[:, :, :, 0], xw[:, :, :, 1], table(1), ALU.mult)
                own.then(dve.tensor_tensor(rot[:, :, :, 1], xw[:, :, :, 0], table(1), ALU.mult))
                own.then(dve.tensor_tensor(d[:, :, :, 0], d[:, :, :, 0], rot[:, :, :, 0], ALU.subtract))
                dve.tensor_tensor(d[:, :, :, 1], d[:, :, :, 1], rot[:, :, :, 1], ALU.add).then_inc(heads_roped, 1)
                dve.wait_ge(heads_roped, k + 1)

            def stage_slot(b, j):
                def free():
                    if j % 2 == 0:
                        dve.wait_ge(stored[(j // 2) % 2], 16 * (2 * b + j // 4))
                return stage[:, (j // 2) % 2, (j % 2) * W:(j % 2 + 1) * W], free

            split_hi(1, 1, None, 1)
            split_hi(2, 0, 10, 2)
            split_hi(3, 1, 20, 2)
            with dve.Fori(4, B_AKV + 2, 2) as b:
                split_hi(b, 0, 10 * b - 10, b // 2 + 1)
                split_hi(b + 1, 1, 10 * b, b // 2 + 1)
            dve.wait_ge(small_in, 96)
            for j in range(TT + CT):
                if j < TT:
                    dst, free = stage_slot(B_AKV, j)
                    rotate_tile(j, 10 * B_AKV + j, j, AKV, j, 1, dst, free)
                else:
                    rotate_tile(j, 10 * B_AKV + j, j, AKV, None, 1, stage_c[:, j - TT, :],
                                lambda: dve.wait_ge(stored_c, 16 * B_AKV))
            with dve.Fori(8, 14, 2) as b:
                split_hi(b, 0, 8 * b + 6, b // 2 + 1)
                split_hi(b + 1, 1, 8 * b + 14, b // 2 + 1)
            for i in range(2):
                b = B_AQ + i
                split_hi(b + 1, (b + 1) % 2, 8 * b + 14, (b + 1) // 2 + 1)
                for j in range(TT):
                    dst, free = stage_slot(b, j)
                    rotate_tile(TT + CT + TT * i + j, 8 * b + 14 + j, j, 4, j, 0, dst, free)
            with dve.Fori(16, NB - 1, 2) as b:
                split_hi(b, 0, 8 * b + 6, b // 2 + 1)
                split_hi(b + 1, 1, 8 * b + 14, b // 2 + 1)
            split_hi(NB - 1, 0, 8 * (NB - 1) + 6, (NB - 1) // 2 + 1)

            def kd_lo(h, m, d):
                dve.wait_ge(kd_hi_done[d], 4 * h + m + 1)
                for j in range(2):
                    src = ck_raw[:, j, :] if m == 0 else ps[:, 0, j * RDK:(j + 1) * RDK]
                    ins = dve.scalar_tensor_tensor(out=kd[d][1][:, j, :], in0=src, scalar=kd_decay[:, d, j:j + 1],
                                                   in1=kd[d][0][:, j, :].bitcast(F32), op0=ALU.mult, op1=ALU.subtract)
                ins.then_inc(kd_lo_done[d], 1)

            def delta_ps(d):
                return ps[:, 2 + 2 * d:4 + 2 * d, :]

            def update_state(h, m, d):
                dve.wait_ge(delta_done[d], 4 * h + m + 1)
                if not (isinstance(h, int) and h == 0 and m == 0):
                    dve.wait_ge(state_lo_done[d], 4 * h + m)
                    dve.wait_ge(state_hi_done[d], 4 * h + m)
                if m == 0:
                    dve.tensor_copy(state[d][:], delta_ps(d)).then_inc(state_done[d], 1)
                else:
                    dve.scalar_tensor_tensor(out=state[d][:], in0=state[d][:], scalar=decay_at(h, 5 * d + 4),
                                             in1=delta_ps(d), op0=ALU.mult, op1=ALU.add).then_inc(state_done[d], 1)

            def state_lo(h, m, d):
                dve.wait_ge(state_hi_done[d], 4 * h + m + 1)
                dve.tensor_tensor(state_r[d][1][:], state[d][:], state_r[d][0][:].bitcast(F32),
                                  ALU.subtract).then_inc(state_lo_done[d], 1)

            def mean_square(h, g):
                dve.wait_ge(o_squared, 8 * h + 4 * g + 4)
                dve.tensor_scalar(ret_ms[:, 1, 4 * g:4 * g + 4], ret_ms[:, 0, 4 * g:4 * g + 4], 1.0 / RDV, EPS,
                                  ALU.mult, ALU.add).then_inc(o_ms, 1)

            def rstd(h, g):
                dve.wait_ge(o_rms, 2 * h + g + 1)
                dve.reciprocal(ret_ms[:, 2, 4 * g:4 * g + 4], ret_ms[:, 1, 4 * g:4 * g + 4]).then_inc(o_rstd, 1)

            def gated(h, g, e):
                bank = o_bank(g, e)
                dve.wait_ge(o_turned, 8 * h + 4 * g + e + 1)
                dve.wait_ge(gate_in, 16 * h + 16)
                if g == 0:
                    v = gate_y[:, e, 2 * P:6 * P]
                    dve.tensor_tensor(v, ps[:, bank, :], v, ALU.mult).then_inc(y_out, 1)
                else:
                    v = gate_y[:, e, 6 * P:8 * P]
                    dve.tensor_tensor(v, ps[:, bank, 0:2 * P], v, ALU.mult)
                    v = gate_y[:, e, 0:2 * P]
                    dve.tensor_tensor(v, ps[:, bank, 2 * P:4 * P], v, ALU.mult).then_inc(y_out, 1)

            def cross_again(h, s, d):
                c = s if d == 0 else NCH - 1 - s
                dve.wait_ge(cross_done[d], 4 * h + s + 1)
                dve.wait_ge(cross_out[1 - d], 4 * h + NCH - s)
                if d == 1:
                    dve.wait_ge(intra_out, 4 * h + NCH - s)
                for i in range(2):
                    ins = dve.scalar_tensor_tensor(out=ret_o[:, 2 * c + i, :], in0=ps[:, 2 + 2 * d + i, :],
                                                   scalar=decay_at(h, 5 * d + i), in1=ret_o[:, 2 * c + i, :],
                                                   op0=ALU.mult, op1=ALU.add)
                ins.then_inc(cross_out[d], 1)

            def key_decays(h):
                if not (isinstance(h, int) and h == 0):
                    dve.wait_ge(mask_exp, 2 * h)
                    dve.wait_ge(kd_hi_done[0], 4 * h)
                    dve.wait_ge(kd_hi_done[1], 4 * h)
                    dve.wait_ge(kd_lo_done[0], 4 * h)
                    dve.wait_ge(kd_lo_done[1], 4 * h)
                dve.tensor_scalar(kd_decay[:], decay[:, bass.ds(h * 10, 10)].rearrange("p (d c) -> p d c", d=2)[:, :, 2:4],
                                  1.0, None, ALU.mult).then_inc(kd_ready, 1)
                dve.tensor_scalar(head_gamma[:], log_gamma[:].rearrange("p (d h) -> p d h", d=2)[:, :, bass.ds(h, 1)]
                                  .rearrange("p d o -> p (d o)"), 1.0, None, ALU.mult).then_inc(kd_ready, 1)
                dve.wait_ge(kd_ready, 2 * h + 2)

            def head_decays(h):
                if not (isinstance(h, int) and h == 0):
                    dve.wait_ge(cross_out[0], 4 * h)
                    dve.wait_ge(cross_out[1], 4 * h)
                dve.tensor_scalar(head_decay[:], decay[:, bass.ds(h * 10, 10)], 1.0, None, ALU.mult).then_inc(head_ready, 1)
                dve.wait_ge(head_ready, h + 1)

            def context_values(h):
                dve.wait_ge(cv_in, 16 * h + 16)
                if not (isinstance(h, int) and h == 0):
                    dve.wait_ge(delta_done[1], 4 * h - 3)
                dve.tensor_copy(cv[0][:], cv_raw[:]).then_inc(cv_hi_done, 1)

            OPERANDS = ((rk, rk_raw, chunks_of, rk_in), (rq, rq_raw, chunks_of, rq_in), (rv, rv_raw, v_chunks, rv_in))

            def outer_hi(h, i):
                r, raw, view, arrived = OPERANDS[i]
                dve.wait_ge(arrived, 16 * h + 16)
                dve.tensor_copy(both(view(r[0]), PAIRS[0]), both(view(raw), PAIRS[0])).then_inc(g03_hi_done, 1)

            def inner_hi(i):
                r, raw, view, _ = OPERANDS[i]
                dve.tensor_copy(both(view(r[0]), PAIRS[1]), both(view(raw), PAIRS[1])).then_inc(g12_hi_done, 1)

            def outer_values_lo(h):
                dve.wait_ge(g03_hi_done, 3 * h + 3)
                dve.tensor_tensor(both(v_chunks(rv[1]), PAIRS[0]), both(v_chunks(rv_raw), PAIRS[0]),
                                  both(v_chunks(rv[0]), PAIRS[0]).bitcast(F32), ALU.subtract).then_inc(g03_lo_dve, 1)

            def make_mask(h):
                dve.wait_ge(mask_exp, 2 * h + 2)
                dve.tensor_tensor(mask[:], mask[:], rel[:, 2, :], ALU.mult).then_inc(mask_done, 1)
                dve.tensor_tensor(mask_b[:], mask_b[:], rel[:, 3, :], ALU.mult).then_inc(mask_done, 1)
                dve.wait_ge(mask_done, 3 * h + 2)
                dve.tensor_tensor(mask[:], mask[:], mask_b[:], ALU.add).then_inc(mask_done, 1)

            def new_state(h, m):
                update_state(h, m, 0)
                state_lo(h, m, 0)
                update_state(h, m, 1)

            def mask_scores(h, s):
                dve.wait_ge(scores_done, 4 * h + s + 1)
                if s == 0:
                    dve.wait_ge(mask_done, 3 * h + 3)
                if not (isinstance(h, int) and h == 0 and s == 0):
                    dve.wait_ge(probs_lo_done, 4 * h + s)
                dve.tensor_tensor(probs[:], ps[:, 1, :], mask[:], ALU.mult).then_inc(probs_done, 1)

            def add_intra(h, s):
                dve.wait_ge(intra_done, 4 * h + s + 1)
                dve.wait_ge(cross_out[0], 4 * h + s + 1)
                v = ret_o[:, 2 * s:2 * s + 2, :]
                dve.tensor_tensor(v, v, ps[:, 6:8, :], ALU.add).then_inc(intra_out, 1)

            def head(h, last):
                first = isinstance(h, int) and h == 0
                mask_scores(h, 0)
                if not first:
                    gated(h - 1, 0, 2)
                state_lo(h, 0, 1)
                outer_values_lo(h)
                if not first:
                    gated(h - 1, 0, 3)
                    gated(h - 1, 1, 0)
                    gated(h - 1, 1, 1)
                kd_lo(h, 1, 0)
                inner_hi(0)
                inner_hi(1)
                if not first:
                    gated(h - 1, 1, 2)
                kd_lo(h, 1, 1)
                if not first:
                    gated(h - 1, 1, 3)
                inner_hi(2)
                add_intra(h, 0)
                new_state(h, 1)
                mask_scores(h, 1)
                state_lo(h, 1, 1)
                kd_lo(h, 2, 0)
                kd_lo(h, 2, 1)
                add_intra(h, 1)
                new_state(h, 2)
                mask_scores(h, 2)
                state_lo(h, 2, 1)
                cross_again(h, 2, 0)
                kd_lo(h, 3, 0)
                cross_again(h, 2, 1)
                kd_lo(h, 3, 1)
                if not last:
                    context_values(h + 1)
                add_intra(h, 2)
                new_state(h, 3)
                mask_scores(h, 3)
                state_lo(h, 3, 1)
                if not last:
                    key_decays(h + 1)
                cross_again(h, 3, 0)
                if not last:
                    kd_lo(h + 1, 0, 0)
                    kd_lo(h + 1, 0, 1)
                    outer_hi(h + 1, 0)
                cross_again(h, 3, 1)
                mean_square(h, 0)
                if not last:
                    outer_hi(h + 1, 1)
                    make_mask(h + 1)
                rstd(h, 0)
                add_intra(h, 3)
                if last:
                    gated(h, 0, 0)
                    gated(h, 0, 1)
                    mean_square(h, 1)
                    rstd(h, 1)
                    gated(h, 0, 2)
                    gated(h, 0, 3)
                else:
                    head_decays(h + 1)
                    outer_hi(h + 1, 2)
                    update_state(h + 1, 0, 0)
                    gated(h, 0, 0)
                    state_lo(h + 1, 0, 0)
                    mean_square(h, 1)
                    update_state(h + 1, 0, 1)
                    rstd(h, 1)
                    gated(h, 0, 1)

            key_decays(0)
            head_decays(0)
            context_values(0)
            kd_lo(0, 0, 0)
            kd_lo(0, 0, 1)
            outer_hi(0, 0)
            outer_hi(0, 1)
            make_mask(0)
            outer_hi(0, 2)
            new_state(0, 0)
            head(0, False)
            with dve.Fori(1, RH - 1) as h:
                head(h, False)
            head(RH - 1, True)
            for e in range(4):
                gated(RH - 1, 1, e)

            dve.wait_ge(y_stored, 16 * RH)
            dve.wait_ge(heads_squared, TT + CT + 2 * TT)
            dve.tensor_scalar(rms_k[:], ssq_k[:].rearrange("p t h -> p (t h)"), 1.0 / AD, EPS, ALU.mult, ALU.add)
            dve.tensor_scalar(rms_q[:], ssq_q[:].rearrange("p t h -> p (t h)"), AD * EPS, None, ALU.add).then_inc(ms_qk, 1)
            dve.wait_ge(rms_qk, 1)
            dve.reciprocal(rstd_k[:], rms_k[:]).then_inc(rstd_qk, 1)
            dve.reciprocal(rstd_q[:], rms_q[:]).then_inc(rstd_qk, 1)
            dve.wait_ge(rstd_qk, 2)
            dve.wait_ge(kv_in, 32)
            keys = kv_raw[:, :, 0:AKV * AD].rearrange("p t (h e) -> p t h e", h=AKV)
            for g in range(AKV):
                r = rstd_k[:].rearrange("p (t h) -> p t h", h=AKV)[:, :, g:g + 1].to_broadcast([P, NKT, AD])
                dve.tensor_tensor(keys[:, :, g, :], keys[:, :, g, :], r, ALU.mult).then_inc(keys_normed, 1)
            dve.tensor_copy(av[0][:], kv_raw[:, :, AKV * AD:]).then_inc(av_hi_done, 1)
            for g in range(AKV):
                dve.wait_ge(ak_hi_done, g + 1)
                dve.tensor_tensor(ak[1][:, g, :], bank_span(3 * g, KEYS), ak[0][:, g, :].bitcast(F32), ALU.subtract).then_inc(ak_lo_done, 1)

            def queries_lo(t, half):
                dve.wait_ge(aq_hi_done, 2 * t + half + 1)
                dst, hi = (v[:, 4 * half:4 * half + 4, :].rearrange("p h i -> p (h i)") for v in (aq[1], aq[0]))
                dve.tensor_tensor(dst, ps[:, 6, :], hi.bitcast(F32), ALU.subtract).then_inc(aq_lo_done, 1)

            def row_maxima(t, u):
                k = AH * t + u
                i = u % 2
                if not (isinstance(t, int) and t == 0 and u < 2):
                    dve.wait_ge(exp_done, k - 1)
                for b in range(3):
                    dve.wait_ge(sc_bank, 3 * k + b + 1)
                    dve.tensor_reduce(row_max[:, i, b:b + 1], ps[:, b, 0:min(W, KEYS - b * W)], AX.X, ALU.max).then_inc(max_bank, 1)
                dve.wait_ge(max_bank, 3 * k + 3)
                dve.tensor_reduce(row_max[:, i, 3:4], row_max[:, i, 0:3], AX.X, ALU.max).then_inc(max_all, 1)
                dve.wait_ge(max_all, k + 1)
                dve.scalar_tensor_tensor(out=neg_max[:, i:i + 1], in0=row_max[:, i, 3:4], scalar=-1.0, in1=rstd_of(t, u),
                                         op0=ALU.mult, op1=ALU.mult).then_inc(neg_done, 1)

            def inverse(t, u):
                k = AH * t + u
                i = u % 2
                dve.wait_ge(exp_done, k + 1)
                if not (isinstance(t, int) and t == 0 and u < 2):
                    dve.wait_ge(soft_done, k - 1)
                dve.reciprocal(row_inv[:, i:i + 1], row_sum[:, i:i + 1]).then_inc(inv_done, 1)

            def soft_lo_half(t, u):
                k = AH * t + u
                dve.wait_ge(soft_hi, k + 1)
                for b in range(3):
                    k0, k1 = 4 * b, min(4 * b + 4, NKT)
                    hi, dst = (soft_t[u // 4][i][:, k0:k1, u % 4, :] for i in range(2))
                    dve.tensor_tensor(dst, ps[:, 3 + b, 0:(k1 - k0) * P].rearrange("p (k i) -> p k i", i=P), hi.bitcast(F32),
                                      ALU.subtract).then_inc(soft_lo, 1)

            def gate_out(t, g):
                dve.wait_ge(pv_done, 2 * t + g + 1)
                v = att_y[:, 4 * g:4 * g + 4, bass.ds(t * P, P)]
                dve.tensor_tensor(v, ps[:, 7, :].rearrange("p (h i) -> p h i", h=4), v, ALU.mult).then_inc(att_out, 1)

            def ada_gate(t):
                dve.wait_ge(ada_g_done, t + 1)
                dve.tensor_tensor(mod_col(t), ps[:, 6, 0:1], vec_cols[:, bass.ds(t + 24 + 2 * KT, 1)], ALU.add).then_inc(gate_col, 1)

            def tile(t):
                first = isinstance(t, int) and t == 0
                last = isinstance(t, int) and t == TT - 1
                if not first:
                    inverse(t - 1, AH - 1)
                dve.tensor_scalar(tile_rstd[:], rstd_q[:, bass.ds(t * AH, AH)], 1.0, None, ALU.mult).then_inc(tile_ready, 1)
                dve.wait_ge(tile_ready, t + 1)
                for u in range(AH):
                    if u > 0:
                        inverse(t, u - 1)
                    row_maxima(t, u)
                    if u > 1:
                        soft_lo_half(t, u - 2)
                    elif not first:
                        soft_lo_half(t - 1, AH - 2 + u)
                    if u == 2:
                        queries_lo(t, 1)
                    if u == 6 and not last:
                        queries_lo(t + 1, 0)
                    if u in (1, 5) and not first:
                        gate_out(t - 1, u // 4)
                    if u == 7:
                        ada_gate(t)

            queries_lo(0, 0)
            dve.wait_ge(att_gate_in, 16)
            tile(0)
            with dve.Fori(1, TT - 1) as t:
                tile(t)
            tile(TT - 1)
            inverse(TT - 1, AH - 1)
            soft_lo_half(TT - 1, AH - 2)
            soft_lo_half(TT - 1, AH - 1)
            gate_out(TT - 1, 0)
            gate_out(TT - 1, 1)

            def y_lo(half, i):
                dve.wait_ge(y_hi_done, 3 * KT * half + i + 1)
                dve.tensor_tensor(y_r[1][:, i, :], y_raw[:, (i // 2) % 2, i % 2, :], y_r[0][:, i, :].bitcast(F32),
                                  ALU.subtract).then_inc(y_lo_done, 1)

            def merge(half, n):
                k = KT * half + n
                dve.wait_ge(mg_in, 32 * k + 32)
                dve.wait_ge(ow_used, CHUNKS * half + 3 * n + 2)
                if not (half == 0 and isinstance(n, int)):
                    dve.wait_ge(z_lo_done, k)
                dve.tensor_tensor(merged[:, 0, :], ps[:, 0, :], merge_gate[:, 0, :], ALU.mult).then_inc(merged_part, 1)
                dve.wait_ge(ow_used, CHUNKS * half + 3 * n + 3)
                dve.tensor_tensor(merged[:, 1, :], ps[:, 1, :], merge_gate[:, 1, :], ALU.mult).then_inc(mg_used, 1)
                dve.wait_ge(mg_used, k + 1)
                dve.tensor_tensor(merged[:, 0, :], merged[:, 0, :], merged[:, 1, :], ALU.add).then_inc(merged_done, 1)
                dve.wait_ge(merged_done, k + 1)
                if half and isinstance(n, int):
                    dve.wait_ge(ow_used, CHUNKS)
                dve.tensor_scalar(row_of(z_r[0], n), merged[:, 0, :], 1.0, None, ALU.mult).then_inc(z_hi_done, 1)
                dve.wait_ge(z_hi_done, k + 1)
                dve.tensor_tensor(row_of(z_r[1], n), merged[:, 0, :], row_of(z_r[0], n).bitcast(F32), ALU.subtract).then_inc(z_lo_done, 1)

            for half in range(HALVES):
                if half == 0:
                    for i in range(3 * KT):
                        y_lo(0, i)
                merge(half, 0)
                with dve.Fori(1, KT) as n:
                    merge(half, n)
                dve.wait_ge(res_in, 16 * half + 16)
                for n in range(KT):
                    if half == 0:
                        for i in range(3 * n, 3 * n + 3):
                            y_lo(1, i)
                    dve.wait_ge(out_turned, KT * half + n + 1)
                    v = res[:, :, n * P:(n + 1) * P]
                    dve.tensor_tensor(v, v, ps[:, 4 + n % 2, :].rearrange("p (t e) -> p t e", t=4), ALU.add).then_inc(out_added, 1)

        @block.tensor
        def _(pe):
            pe.wait_ge(ident_in_s, 16)
            pe.wait_ge(vec_silu, 1)
            pe.transpose(ps[:, 0, 0:48], vec_rows[:], ident[0:48, 0:48]).then_inc(vec_turned, 1)

            def turn(u):
                bank = unit_bank(u)
                if u >= UNITS_X:
                    pe.wait_ge(x_normed, TT + CT)
                    pe.wait_ge(unit_modulated, max(UNITS_X, u - 2))
                else:
                    pe.wait_ge(x_normed, 4 * (u // KT) + 4)
                    if u >= 6:
                        pe.wait_ge(unit_modulated, u - 5)
                k = u % KT
                n = 4 if u < UNITS_X else CT
                for i in range(n):
                    src = xs[:, 4 * (u // KT) + i, k * P:(k + 1) * P] if u < UNITS_X else cs[:, i, k * P:(k + 1) * P]
                    ins = pe.transpose(ps[:, bank, i * P:(i + 1) * P], src, ident[:])
                ins.then_inc(unit_turned, 1)

            for u in range(6):
                turn(u)
            pe.wait_ge(vec_copied, 1)
            vecs = vec_cols[:, 0:2 * KT].rearrange("p (v k) -> p k v", k=KT)
            for n in range(2 * KT):
                pe.wait_ge(ada_in[n % 4], 16 * (n // 4 + 1))
                for k in range(KT):
                    ins = pe.matmul(ps[:, 1, 2 * n:2 * n + 2], ada[:, n % 4, k, :], vecs[:, k, :], start=(k == 0), stop=(k == KT - 1))
                ins.then_inc(ada_used, 1)
            for u in range(6, UNITS_X):
                turn(u)

            def passes(out, stat, mov, stat_at, mov_at, n):
                for k in range(n):
                    for i, (s, m) in enumerate(((0, 0), (0, 1), (1, 0))):
                        ins = pe.matmul(out, stat_at(stat[s], k), mov_at(mov[m], k),
                                        start=(k == 0 and i == 0), stop=(k == n - 1 and i == 2))
                return ins

            def x_tile(n, j, bank, s, transposed):
                pe.wait_ge(tile_out, n - 3)
                wt = (w_hi[s], w_lo[s])
                if transposed:
                    col, half = j // 2, j % 2
                    ins = passes(ps[:, bank, :], wt, (hx_hi, hx_lo), lambda v, k: v[:, k, col * P:(col + 1) * P],
                                 lambda v, k: v[:, k, half * W:(half + 1) * W], KT)
                else:
                    ins = passes(ps[:, bank, :], (hx_hi, hx_lo), wt, lambda v, k: v[:, k, j * P:(j + 1) * P],
                                 lambda v, k: v[:, k, :], KT)
                ins.then_inc(tile_done, 1)

            def c_tile(n, j, bank, s):
                pe.wait_ge(tile_out, n - 3)
                passes(ps[:, bank, :], (hc_hi, hc_lo), (w_hi[s], w_lo[s]),
                       lambda v, k: v[:, k, (j - TT) * P:(j - TT + 1) * P], lambda v, k: v[:, k, :], KT).then_inc(tile_done, 1)

            pe.wait_ge(unit_hi, UNITS_X)
            pe.wait_ge(unit_lo_dve, UNITS_X // 2)
            pe.wait_ge(unit_lo_pool, UNITS_X // 2)
            pe.wait_ge(w_hi_done, 1)
            pe.wait_ge(w_lo_done, 1)
            wt = (w_hi[0], w_lo[0])
            for j in range(TT):
                if j == 4:
                    for u in range(UNITS_X, UNITS):
                        turn(u)
                if j >= 5:
                    pe.wait_ge(tile_out, j - 4)
                col, half = j // 2, j % 2
                passes(ps[:, j % 5, :], wt, (hx_hi, hx_lo), lambda v, k: v[:, k, col * P:(col + 1) * P],
                       lambda v, k: v[:, k, half * W:(half + 1) * W], KT).then_inc(tile_done, 1)
            pe.wait_ge(unit_hi, UNITS)
            pe.wait_ge(unit_lo_dve, UNITS // 2)
            pe.wait_ge(unit_lo_pool, UNITS // 2)
            for j in range(TT, TT + CT):
                c_tile(j, j, j % 5, 0)
            pe.wait_ge(w_lo_done, 2)
            for j in range(TT):
                x_tile(10 + j, j, j % 5, 1, True)
            for j in range(TT, TT + CT):
                c_tile(10 + j, j, j % 5, 1)

            def ctx_block(b, s):
                pe.wait_ge(w_lo_done, b + 1)
                for j in range(TT):
                    x_tile(10 * b + j, j, j % 5, s, False)
                for j in range(TT, TT + CT):
                    c_tile(10 * b + j, j, j % 5, s)

            def x_block(b, s, transposed):
                pe.wait_ge(w_lo_done, b + 1)
                for j in range(TT):
                    x_tile(8 * b + 14 + j, j, j % 4, s, transposed)

            with pe.Fori(B_RV, B_AKV, 2) as b:
                ctx_block(b, 0)
                ctx_block(b + 1, 1)
            ctx_block(B_AKV, 0)
            with pe.Fori(B_RQ, B_AQ, 2) as b:
                x_block(b, 1, True)
                x_block(b + 1, 0, True)
            x_block(B_AQ, 1, False)
            x_block(B_AQ + 1, 0, False)
            with pe.Fori(B_AG, NB, 2) as b:
                x_block(b, 1, True)
                x_block(b + 1, 0, True)

            def turn_keys(h, m, d):
                c = m - 1 if d == 0 else NCH - m
                pe.wait_ge(rk_in, 16 * h + 16)
                if d == 0:
                    pe.wait_ge(kd_lo_done[1], 4 * h + m)
                    if m == 1 and not (isinstance(h, int) and h == 0):
                        pe.wait_ge(y_out, 8 * h - 4)
                else:
                    pe.wait_ge(kd_lo_done[0], 4 * h + m + 1)
                for j in range(2):
                    for e in range(2):
                        at = c * CH + j * P
                        ins = pe.transpose(ps[:, 0, j * RDK + e * P:j * RDK + (e + 1) * P], rk_raw[:, e, at:at + P], ident[:])
                ins.then_inc(k_turned[d], 1)

            def delta(h, m, d):
                pe.wait_ge(kd_lo_done[d], 4 * h + m + 1)
                if m == 0:
                    pe.wait_ge(cv_lo_done, h + 1)
                    vals, v0 = cv, 0
                    if not (isinstance(h, int) and h == 0):
                        pe.wait_ge(cross_out[d], 4 * h)
                else:
                    vals, v0 = rv, 2 * (m - 1 if d == 0 else NCH - m)
                    pe.wait_ge(cross_out[d], 4 * h + m)
                for e in range(2):
                    ins = passes(ps[:, 2 + 2 * d + e, :], kd[d], vals, lambda v, k: v[:, k, e * P:(e + 1) * P],
                                 lambda v, k: v[:, v0 + k, :], 2)
                ins.then_inc(delta_done[d], 1)

            def scores(h, s):
                if s == 0:
                    pe.wait_ge(g03_lo_pool, 2 * h + 2)
                if s == 1:
                    pe.wait_ge(g12_lo_done, 3 * h + 2)
                    if not (isinstance(h, int) and h == 0):
                        pe.wait_ge(y_out, 8 * h)
                if not (isinstance(h, int) and h == 0 and s == 0):
                    pe.wait_ge(probs_done, 4 * h + s)
                at = s * CH
                for j in range(2):
                    ins = passes(ps[:, 1, j * CH:(j + 1) * CH], rk, rq, lambda v, k: v[:, k, at + j * P:at + (j + 1) * P],
                                 lambda v, k: v[:, k, at:at + CH], 2)
                ins.then_inc(scores_done, 1)

            def cross(h, s, d):
                c = s if d == 0 else NCH - 1 - s
                pe.wait_ge(state_lo_done[d], 4 * h + s + 1)
                for i in range(2):
                    at = c * CH + i * P
                    ins = passes(ps[:, 2 + 2 * d + i, :], rq, state_r[d], lambda v, k: v[:, k, at:at + P],
                                 lambda v, k: v[:, k, :], 2)
                ins.then_inc(cross_done[d], 1)

            def intra(h, s):
                pe.wait_ge(probs_lo_done, 4 * h + s + 1)
                if s == 0:
                    pe.wait_ge(g03_lo_dve, h + 1)
                    if not (isinstance(h, int) and h == 0):
                        pe.wait_ge(y_out, 8 * h - 2)
                else:
                    pe.wait_ge(intra_out, 4 * h + s)
                    if s == 1:
                        pe.wait_ge(g12_lo_done, 3 * h + 3)
                for i in range(2):
                    ins = passes(ps[:, 6 + i, :], probs_r, rv, lambda v, k: v[:, k, i * P:(i + 1) * P],
                                 lambda v, k: v[:, 2 * s + k, :], 2)
                ins.then_inc(intra_done, 1)

            def turn_o(h, g, e, last=False):
                bank = o_bank(g, e)
                pe.wait_ge(o_normed, 2 * h + g + 1)
                if g == 0 and e == 0:
                    pe.wait_ge(kd_lo_done[1], 4 * h + 4)
                elif g == 0:
                    pe.wait_ge(y_out, 8 * h + e)
                elif e < 2:
                    pe.wait_ge(intra_out, 4 * h + 4)
                elif e == 2:
                    pe.wait_ge(probs_done, 4 * h + (4 if last else 5))
                else:
                    pe.wait_ge(y_out, 8 * h + 7)
                for i, t in enumerate(O_GROUPS[g]):
                    ins = pe.transpose(ps[:, bank, i * P:(i + 1) * P], ret_o[:, t, e * P:(e + 1) * P], ident[:])
                ins.then_inc(o_turned, 1)

            def head(h, last):
                first = isinstance(h, int) and h == 0
                scores(h, 0)
                if not first:
                    turn_o(h - 1, 0, 2)
                cross(h, 0, 0)
                if not first:
                    turn_o(h - 1, 0, 3)
                    turn_o(h - 1, 1, 0)
                    turn_o(h - 1, 1, 1)
                turn_keys(h, 1, 0)
                cross(h, 0, 1)
                if not first:
                    turn_o(h - 1, 1, 2)
                turn_keys(h, 1, 1)
                if not first:
                    turn_o(h - 1, 1, 3)
                intra(h, 0)
                delta(h, 1, 0)
                delta(h, 1, 1)
                for s in range(1, NCH):
                    scores(h, s)
                    cross(h, s, 0)
                    if s < NCH - 1:
                        turn_keys(h, s + 1, 0)
                    cross(h, s, 1)
                    if s < NCH - 1:
                        turn_keys(h, s + 1, 1)
                    intra(h, s)
                    if s < NCH - 1:
                        delta(h, s + 1, 0)
                        delta(h, s + 1, 1)
                if last:
                    for e in range(4):
                        turn_o(h, 0, e)
                    for e in range(4):
                        turn_o(h, 1, e, True)
                else:
                    delta(h + 1, 0, 0)
                    turn_o(h, 0, 0)
                    delta(h + 1, 0, 1)
                    turn_o(h, 0, 1)

            delta(0, 0, 0)
            delta(0, 0, 1)
            head(0, False)
            with pe.Fori(1, RH - 1) as h:
                head(h, False)
            head(RH - 1, True)

            for g in range(AKV):
                pe.wait_ge(keys_normed, g + 1)
                if g == 0:
                    pe.wait_ge(y_out, 8 * RH)
                for t in range(NKT):
                    ins = pe.transpose(bank_span(3 * g, KEYS)[:, t * P:(t + 1) * P], kv_raw[:, t, g * AD:(g + 1) * AD], ident[:])
                ins.then_inc(ak_turned, 1)

            def turn_queries(t, half):
                pe.wait_ge(aq_in[half], 16 * t + 16)
                if not (isinstance(t, int) and t == 0 and half == 0):
                    pe.wait_ge(aq_lo_done, 2 * t + half)
                if half == 0 and not (isinstance(t, int) and t == 0):
                    pe.wait_ge(sc_bank, 3 * (AH * t - 4))
                if half == 1 and not (isinstance(t, int) and t == 0):
                    pe.wait_ge(gate_col, t)
                for h in range(4):
                    ins = pe.transpose(ps[:, 6, h * P:(h + 1) * P], aq_raw[:, half, h * AD:(h + 1) * AD], ident[:])
                ins.then_inc(aq_turned, 1)

            def att_scores(t, u):
                k = AH * t + u
                if not (isinstance(t, int) and t == 0 and u == 0):
                    pe.wait_ge(exp_done, k)
                if u == 0:
                    pe.wait_ge(aq_lo_done, 2 * t + 1)
                if u == 4:
                    pe.wait_ge(aq_lo_done, 2 * t + 2)
                for b in range(3):
                    n = min(W, KEYS - b * W)
                    passes(ps[:, b, 0:n], aq, ak, lambda v, k: v[:, u, :], lambda v, k: v[:, u // 4, b * W:b * W + n], 1).then_inc(sc_bank, 1)

            def turn_soft(t, u):
                k = AH * t + u
                pe.wait_ge(soft_done, k + 1)
                for j in range(NKT):
                    if j % 4 == 0 and not (isinstance(t, int) and t == 0 and u == 0):
                        pe.wait_ge(soft_lo, 3 * k - 2 + j // 4)
                    ins = pe.transpose(bank_span(3, KEYS)[:, j * P:(j + 1) * P], soft[u % 2][:, j * P:(j + 1) * P], ident[:])
                ins.then_inc(soft_turned, 1)

            def values(t, g, part):
                if part == 0:
                    pe.wait_ge(soft_lo, 3 * (AH * t + 4 * g + 4))
                    if not (isinstance(t, int) and t == 0 and g == 0):
                        pe.wait_ge(att_out, 2 * t + g)
                k0, k1 = ((0, 3), (3, 6), (6, 8), (8, NKT))[part]
                for k in range(k0, k1):
                    for i, (a, b) in enumerate(((0, 0), (0, 1), (1, 0))):
                        ins = pe.matmul(ps[:, 7, :], av[a][:, k, g * AD:(g + 1) * AD],
                                        soft_t[g][b][:, k].rearrange("p h i -> p (h i)"),
                                        start=(k == 0 and i == 0), stop=(k == NKT - 1 and i == 2))
                if part == 3:
                    ins.then_inc(pv_done, 1)

            def tile(t):
                first = isinstance(t, int) and t == 0
                last = isinstance(t, int) and t == TT - 1
                for u in range(AH):
                    att_scores(t, u)
                    if u < 2 and not first:
                        values(t - 1, 0, u + 2)
                    elif 2 <= u <= 5 and not first:
                        values(t - 1, 1, u - 2)
                    elif u >= 6:
                        values(t, 0, u - 6)
                    if u > 0:
                        turn_soft(t, u - 1)
                    elif not first:
                        turn_soft(t - 1, AH - 1)
                    if u == 1:
                        turn_queries(t, 1)
                    if u == 5 and not last:
                        turn_queries(t + 1, 0)
                    if u == 7:
                        pe.wait_ge(ada_g_in, 16 * t + 16)
                        pe.wait_ge(aq_lo_done, 2 * t + (2 if last else 3))
                        for k in range(KT):
                            ins = pe.matmul(ps[:, 6, 0:1], ada_g[:, k, :], vec_cols[:, k:k + 1], start=(k == 0), stop=(k == KT - 1))
                        ins.then_inc(ada_g_done, 1)

            turn_queries(0, 0)
            pe.wait_ge(ak_lo_done, AKV)
            pe.wait_ge(av_lo_done, 1)
            tile(0)
            with pe.Fori(1, TT - 1) as t:
                tile(t)
            tile(TT - 1)
            values(TT - 1, 0, 2)
            turn_soft(TT - 1, AH - 1)
            values(TT - 1, 0, 3)
            for part in range(4):
                values(TT - 1, 1, part)

            def chunk_ready(half, c):
                pe.wait_ge(ow_lo_done, CHUNKS * half + c + 1)

            def branch_tile(half, n, first):
                k = KT * half + n
                for i in range(3):
                    chunk_ready(half, 3 * n + i)
                    bank = 0 if i < 2 else 1
                    if i == 0:
                        if half == 0 and first:
                            pe.wait_ge(exp_done, TT * AH)
                        else:
                            pe.wait_ge(merged_part, k)
                    if i == 2 and not (half == 0 and first):
                        pe.wait_ge(mg_used, k)
                    if first and half:
                        pe.wait_ge(y_lo_done, 3 * KT * HALVES)
                    for j in range(KT):
                        if first and half == 0:
                            pe.wait_ge(y_lo_done, KT * i + j + 1)
                        for q, (a, b) in enumerate(((0, 0), (0, 1), (1, 0))):
                            ins = pe.matmul(ps[:, bank, :], ow[i][a][:, j, :], y_r[b][:, KT * i + j, :],
                                            start=(i != 1 and j == 0 and q == 0), stop=(i != 0 and j == KT - 1 and q == 2))
                    ins.then_inc(ow_used, 1)

            def out_tile(half, n):
                k = KT * half + n
                c = 3 * KT + n
                chunk_ready(half, c)
                if n == 0:
                    pe.wait_ge(z_lo_done, KT * half + KT)
                if k >= 2:
                    pe.wait_ge(out_gated, k - 1)
                for j in range(KT):
                    for q, (a, b) in enumerate(((0, 0), (0, 1), (1, 0))):
                        ins = pe.matmul(ps[:, 2 + n % 2, :], ow[c % 3][a][:, j, :], z_r[b][:, j, :],
                                        start=(j == 0 and q == 0), stop=(j == KT - 1 and q == 2))
                ins.then_inc(ow_used, 1)

            def turn_out(half, n):
                k = KT * half + n
                pe.wait_ge(out_gated, k + 1)
                if k >= 2:
                    pe.wait_ge(out_added, k - 1)
                for j in range(4):
                    ins = pe.transpose(ps[:, 4 + n % 2, j * P:(j + 1) * P], out_t[:, n % 2, j * P:(j + 1) * P], ident[:])
                ins.then_inc(out_turned, 1)

            for half in range(HALVES):
                branch_tile(half, 0, True)
                with pe.Fori(1, KT) as n:
                    branch_tile(half, n, False)
                for n in range(KT):
                    out_tile(half, n)
                    if n:
                        turn_out(half, n - 1)
                turn_out(half, KT - 1)


NORM_GROUPS = ((0, 4), (4, 8), (8, 10))
LN2 = float(np.log(2.0))


_INS = ["x", "c", "ctx", "c_ctx", "norm_w", "w_ada", "b_ada", "w_in", "ret_log2_decay",
        "q_norm_w", "k_norm_w", "w_o_ret", "w_o_att", "w_out"]


def kernel(**inputs):
    import concourse.bacc as bacc
    from concourse.bass_utils import run_bass_kernel_spmd

    nc = bacc.Bacc("TRN2", target_bir_lowering=False, num_devices=1)
    arrays, args = {}, []
    values = {name: np.ascontiguousarray(inputs[name]) for name in _INS}
    values.update(shape_constants())
    for name, a in values.items():
        arrays[f"{name}_dram"] = a
        args.append(nc.dram_tensor(f"{name}_dram", a.shape, mybir.dt.from_np(a.dtype), kind="ExternalInput").ap())
    out = nc.dram_tensor("out_dram", (1, SEQ, D), F32, kind="ExternalOutput").ap()
    build_program(nc, *args, out)
    r = run_bass_kernel_spmd(nc, [arrays], core_ids=[0])
    return r.results[0]["out_dram"]
```

```python
from contextlib import ExitStack

import numpy as np

import concourse.bass as bass
from concourse import mybir
from concourse.alu_op_type import AluOpType as ALU

F32 = mybir.dt.float32
F32R = mybir.dt.float32r
ACT = mybir.ActivationFunctionType
AX = mybir.AxisListType

P = 128
D = 1024
SEQ = 1024
CTX = 256
GRID_W = 64
KT = D // P
TT = SEQ // P
CT = CTX // P
RH, RDK, RDV = 4, 256, 512
AH, AKV, AD = 8, 2, 128
EPS = 1e-6
ROPE_THETA = 10000.0
W = 512
CH = 256
NCH = SEQ // CH

B_RK, B_RV, B_AKV, B_RQ, B_RG, B_AQ, B_AG, B_MR, B_MA = 0, 2, 6, 7, 9, 13, 15, 17, 19
NB = 21
CTX_BLOCKS = 7


def shape_constants():
    half = AD // 2
    rows = np.repeat(np.arange(SEQ // GRID_W, dtype=np.float32), GRID_W)
    cols = np.tile(np.arange(GRID_W, dtype=np.float32), SEQ // GRID_W)
    freqs = (np.float32(ROPE_THETA) ** (-np.arange(0, half, 2, dtype=np.float32) / np.float32(half))).astype(np.float32)
    ang = np.concatenate([rows[:, None] * freqs, cols[:, None] * freqs], axis=-1).astype(np.float32)
    rope = np.stack([np.cos(ang), np.sin(ang)]).astype(np.float32)
    p = np.arange(P, dtype=np.float32)
    exps = [p + 1, p + 129, 255 - p, 127 - p, p * 0 + 256, 256 - p, 128 - p, p, p + 128, p * 0 + 256]
    j = p[:, None, None] + P * np.arange(2, dtype=np.float32)[None, :, None]
    i = np.arange(CH, dtype=np.float32)[None, None, :]
    d = i - j
    rel = np.stack([np.maximum(d, 0), np.maximum(-d, 0), d >= 0, d <= 0], axis=1).reshape(P, 4, 2 * CH)
    return {"ident_in": np.eye(P, dtype=np.float32), "rope_in": rope,
            "decay_exp_in": np.stack(exps, axis=1).astype(np.float32), "rel_in": rel.astype(np.float32)}


def build_program(nc, x, c, ctx, c_ctx, norm_w, w_ada, b_ada, w_in, ret_log2_decay,
                  q_norm_w, k_norm_w, w_o_ret, w_o_att, w_out,
                  ident_in, rope_in, decay_exp_in, rel_in, out):
    with ExitStack() as held:
        def sem(name):
            return held.enter_context(nc.semaphore(name))

        def sb(stack, name, shape, dt=F32):
            return stack.enter_context(nc.sbuf_tensor(name, shape, dt))

        def scratch(name, shape):
            return nc.dram_tensor(name, shape, F32, kind="Internal").ap()

        proj_x = scratch("proj_x", (NB, 4, P, 2 * W))
        proj_c = scratch("proj_c", (CTX_BLOCKS, P, CT * W))

        ident = sb(held, "ident", [P, P])
        vec_cols = sb(held, "vec_cols", [P, 48])
        mod = sb(held, "mod", [P, 3 * KT, 2])
        log_gamma = sb(held, "log_gamma", [P, 2 * RH])
        decay = sb(held, "decay", [P, RH * 10])
        head_decay = sb(held, "head_decay", [P, 10])
        head_gamma = sb(held, "head_gamma", [P, 2])
        kd_decay = sb(held, "kd_decay", [P, 2, 2])
        tile_rstd = sb(held, "tile_rstd", [P, AH])
        ssq_q = sb(held, "ssq_q", [P, TT, AH])
        ssq_k = sb(held, "ssq_k", [P, TT + CT, AKV])
        ps = held.enter_context(nc.psum_tensor("ps", [P, 8, W], F32))

        proj_mem = held.enter_context(ExitStack())
        hx_hi = sb(proj_mem, "hx_hi", [P, KT, SEQ], F32R)
        hx_lo = sb(proj_mem, "hx_lo", [P, KT, SEQ], F32R)
        hc_hi = sb(proj_mem, "hc_hi", [P, KT, CTX], F32R)
        hc_lo = sb(proj_mem, "hc_lo", [P, KT, CTX], F32R)
        with ExitStack() as m:
            ada_rows = sb(m, "ada_rows", [2, 2 * D])
        stage = sb(proj_mem, "stage", [P, 2, 2 * W])

        def weight_halves(s):
            return [sb(proj_mem, f"w{s}_{x}", [P, KT, W], F32R) for x in ("hi", "lo")]

        w_raw = [sb(proj_mem, "w_raw0", [P, KT, W])]
        with ExitStack() as m:
            ada_1_2 = sb(m, "ada_1_2", [P, 2, KT, W])
        halves_0 = weight_halves(0)
        with ExitStack() as m:
            xs = sb(m, "xs", [P, TT, D])
            ada_0_3 = sb(m, "ada_0_3", [P, KT, W])
            cs = sb(m, "cs", [P, CT, D])
            modulated = sb(m, "modulated", [P, 2, W])
            vec_rows = sb(m, "vec_rows", [48, P])
            ssq_x = sb(m, "ssq_x", [P, TT + CT])
            rms_x = sb(m, "rms_x", [P, TT + CT])
            rstd_x = sb(m, "rstd_x", [P, TT + CT])
            a_col = sb(m, "a_col", [P, KT, 2])
            square_junk = sb(m, "square_junk", [P, D])
            log2_decay = sb(m, "log2_decay", [P, 2 * RH])
            lg = sb(m, "lg", [P, 8, 2 * RH])
            decay_exp = sb(m, "decay_exp", [P, 10])
        w_raw.append(sb(proj_mem, "w_raw1", [P, KT, W]))
        w_hi, w_lo = zip(halves_0, weight_halves(1))
        stage_c = sb(proj_mem, "stage_c", [P, CT, W])
        heads_in = sb(proj_mem, "heads_in", [P, 2, W])
        heads_w = sb(proj_mem, "heads_w", [P, W])
        rope_t = sb(proj_mem, "rope_t", [P, W])
        rope_cs = sb(proj_mem, "rope_cs", [P, 2, TT, AD // 2])
        qk_norm = sb(proj_mem, "qk_norm", [P, 2, AD])
        head_junk = sb(proj_mem, "head_junk", [P, 4, AD])
        proj_mem.close()

        y_ret = scratch("y_ret", (RH * 4, P, SEQ))
        with ExitStack() as m:
            rv = [sb(m, f"rv_{x}", [P, TT, RDV], F32R) for x in ("hi", "lo")]
            ret_o = sb(m, "ret_o", [P, TT, RDV])
            gate_y = sb(m, "gate_y", [P, 4, SEQ])
            rk = [sb(m, f"rk_{x}", [P, 2, SEQ], F32R) for x in ("hi", "lo")]
            probs = sb(m, "probs", [P, 2 * CH])
            probs_r = [sb(m, f"probs_{x}", [P, 2, CH], F32R) for x in ("hi", "lo")]
            ret_junk = sb(m, "ret_junk", [P, RDV])
            rq = [sb(m, f"rq_{x}", [P, 2, SEQ], F32R) for x in ("hi", "lo")]
            state = [sb(m, f"state{d}", [P, 2, RDV]) for d in range(2)]
            state_r = [[sb(m, f"state{d}_{x}", [P, 2, RDV], F32R) for x in ("hi", "lo")] for d in range(2)]
            sb(m, "ret_spare", [P, 2 * SEQ])
            rq_raw = sb(m, "rq_raw", [P, 2, SEQ])
            rv_raw = sb(m, "rv_raw", [P, TT, RDV])
            rk_raw = sb(m, "rk_raw", [P, 2, SEQ])
            ck_raw = sb(m, "ck_raw", [P, CT, RDK])
            cv_raw = sb(m, "cv_raw", [P, CT, RDV])
            cv = [sb(m, f"cv_{x}", [P, CT, RDV], F32R) for x in ("hi", "lo")]
            rel = sb(m, "rel", [P, 4, 2 * CH])
            kd = [[sb(m, f"kd{d}_{x}", [P, 2, RDK], F32R) for x in ("hi", "lo")] for d in range(2)]
            mask = sb(m, "mask", [P, 2 * CH])
            mask_b = sb(m, "mask_b", [P, 2 * CH])
            ret_ms = sb(m, "ret_ms", [P, 3, TT])

        y_att = scratch("y_att", (AH, P, SEQ))
        KEYS = SEQ + CTX
        NKT = KEYS // P
        with ExitStack() as m:
            soft_t = [[sb(m, f"soft_t{g}_{x}", [P, NKT, 4, P], F32R) for x in ("hi", "lo")] for g in range(AKV)]
            att_y = sb(m, "att_y", [P, AH, SEQ])
            soft = [sb(m, f"soft{i}", [P, KEYS]) for i in range(2)]
            aq = [sb(m, f"aq_{x}", [P, AH, P], F32R) for x in ("hi", "lo")]
            ada_g = sb(m, "ada_g", [P, KT, P])
            rms_q = sb(m, "rms_q", [P, TT * AH])
            rstd_q = sb(m, "rstd_q", [P, TT * AH])
            rms_k = sb(m, "rms_k", [P, NKT * AKV])
            rstd_k = sb(m, "rstd_k", [P, NKT * AKV])
            row_max = sb(m, "row_max", [P, 2, 4])
            neg_max = sb(m, "neg_max", [P, 2])
            row_sum = sb(m, "row_sum", [P, 2])
            row_inv = sb(m, "row_inv", [P, 2])
            kv_raw = sb(m, "kv_raw", [P, NKT, W])
            aq_raw = sb(m, "aq_raw", [P, 2, W])
            av = [sb(m, f"av_{x}", [P, NKT, AKV * AD], F32R) for x in ("hi", "lo")]
            ak = [sb(m, f"ak_{x}", [P, AKV, KEYS], F32R) for x in ("hi", "lo")]

        with ExitStack() as m:
            y_ret_r = sb(m, "y_ret_r", [P, 2 * KT, 2, W], F32R)
            res = sb(m, "res", [P, 4, D])
            z_r = [sb(m, f"z_{x}", [P, KT, W], F32R) for x in ("hi", "lo")]
            ow = [[sb(m, f"ow{i}_{x}", [P, KT, P], F32R) for x in ("hi", "lo")] for i in range(2)]
            y_raw_2 = sb(m, "y_raw2", [P, 2, W])
            merged = sb(m, "merged", [P, 2, W])
            y_raw = [sb(m, f"y_raw{i}", [P, 2, W]) for i in range(2)] + [y_raw_2]
            ow_raw = [sb(m, f"ow_raw{i}", [P, KT, P]) for i in range(3)]
            ow.append([sb(m, f"ow2_{x}", [P, KT, P], F32R) for x in ("hi", "lo")])
            y_att_r = sb(m, "y_att_r", [P, KT, 2, W], F32R)
            merge_gate = sb(m, "merge_gate", [P, 2, W])
            out_t = sb(m, "out_t", [P, 2, W])

        def y_r(i, part):
            return y_ret_r[:, i, part, :] if i < 2 * KT else y_att_r[:, i - 2 * KT, part, :]

        ident_in_s, vec_in, small_in, ctx_in = sem("ident_in"), sem("vec_in"), sem("small_in"), sem("ctx_in")
        x_in = [sem(f"x_in{i}") for i in range(4)]
        ada_in = [sem(f"ada_in{i}") for i in range(4)]
        w_in_s = [sem(f"w_in{i}") for i in range(2)]
        vec_silu, vec_turned, vec_copied = sem("vec_silu"), sem("vec_turned"), sem("vec_copied")
        x_squared, ms_done, rms_done, x_normed = sem("x_squared"), sem("ms_done"), sem("rms_done"), sem("x_normed")
        ada_used, rows_out, ada_turned = sem("ada_used"), sem("rows_out"), sem("ada_turned")
        unit_turned, unit_modulated, unit_hi = sem("unit_turned"), sem("unit_modulated"), sem("unit_hi")
        unit_lo_pool, unit_lo_dve = sem("unit_lo_pool"), sem("unit_lo_dve")
        dve_step, lg_act, lg_dve, decay_done = sem("dve_step"), sem("lg_act"), sem("lg_dve"), sem("decay_done")
        w_hi_done, w_lo_done = sem("w_hi_done"), sem("w_lo_done")
        w0_hi_done, w0_lo_done = sem("w0_hi_done"), sem("w0_lo_done")
        tile_done, tile_out = sem("tile_done"), sem("tile_out")
        heads_squared, heads_roped = sem("heads_squared"), sem("heads_roped")
        stored = [sem(f"stored{i}") for i in range(2)]
        stored_c = sem("stored_c")

        rel_in_s, ck_in, cv_in, rk_in, rq_in, rv_in, gate_in = (
            sem(n) for n in ("rel_in", "ck_in", "cv_in", "rk_in", "rq_in", "rv_in", "gate_in"))
        head_ready, kd_ready = sem("head_ready"), sem("kd_ready")
        cv_hi_done, cv_lo_done, g03_hi_done, g03_lo_pool, g03_lo_dve, g12_hi_done, g12_lo_done = (
            sem(n) for n in ("cv_hi", "cv_lo", "g03_hi", "g03_lo_pool", "g03_lo_dve", "g12_hi", "g12_lo"))
        k_turned, kd_hi_done, kd_lo_done = ([sem(f"{n}{d}") for d in range(2)] for n in ("k_turned", "kd_hi", "kd_lo"))
        delta_done, state_done, state_hi_done, state_lo_done, cross_done, cross_out = (
            [sem(f"{n}{d}") for d in range(2)]
            for n in ("delta_done", "state_done", "state_hi", "state_lo", "cross_done", "cross_out"))
        scores_done, probs_done, probs_hi_done, probs_lo_done, intra_done, intra_out = (
            sem(n) for n in ("scores_done", "probs_done", "probs_hi", "probs_lo", "intra_done", "intra_out"))
        mask_exp, mask_done = sem("mask_exp"), sem("mask_done")
        o_squared, o_ms, o_rms, o_rstd, o_normed, o_turned, y_out, y_stored = (
            sem(n) for n in ("o_squared", "o_ms", "o_rms", "o_rstd", "o_normed", "o_turned", "y_out", "y_stored"))

        PAIRS = ((0, 3), (1, 2))

        def both(v, pair):
            a, e = pair
            return v[:, a:e + 1:e - a]

        def chunks_of(v):
            return v.rearrange("p d (c i) -> p c d i", c=NCH)

        def v_chunks(v):
            return v.rearrange("p (c t) e -> p c (t e)", c=NCH)

        tile_ready = sem("tile_ready")
        kv_in, att_gate_in, ada_g_in = sem("kv_in"), sem("att_gate_in"), sem("ada_g_in")
        aq_in = [sem(f"aq_in{i}") for i in range(2)]
        ms_qk, rms_qk, rstd_qk, keys_normed, ak_turned, ak_hi_done, ak_lo_done, av_hi_done, av_lo_done = (
            sem(n) for n in ("ms_qk", "rms_qk", "rstd_qk", "keys_normed", "ak_turned", "ak_hi", "ak_lo", "av_hi", "av_lo"))
        aq_turned, aq_hi_done, aq_lo_done = sem("aq_turned"), sem("aq_hi"), sem("aq_lo")
        sc_bank, max_bank, max_all, neg_done, exp_done, inv_done, soft_done, soft_turned, soft_hi, soft_lo = (
            sem(n) for n in ("sc_bank", "max_bank", "max_all", "neg_done", "exp_done", "inv_done", "soft_done",
                             "soft_turned", "soft_hi", "soft_lo"))
        pv_done, att_out, att_stored, ada_g_done, gate_col = (
            sem(n) for n in ("pv_done", "att_out", "att_stored", "ada_g_done", "gate_col"))
        y_in = [sem(f"y_in{i}") for i in range(3)]
        ow_in = [sem(f"ow_in{i}") for i in range(3)]
        y_hi_done, y_lo_done, ow_hi_done, ow_lo_done, ow_used = (
            sem(n) for n in ("y_hi_done", "y_lo_done", "ow_hi_done", "ow_lo_done", "ow_used"))
        mg_in, mg_used, merged_part, merged_done, z_hi_done, z_lo_done = (
            sem(n) for n in ("mg_in", "mg_used", "merged_part", "merged_done", "z_hi", "z_lo"))
        res_in, out_gated, out_turned, out_added, out_stored = (
            sem(n) for n in ("res_in", "out_gated", "out_turned", "out_added", "out_stored"))

        HALVES = SEQ // W
        CHUNKS = 4 * KT

        def chunk_slot(c):
            return c % 3, c // 3

        SLOT_USES = (11, 11, 10)

        def bank_span(b, n):
            return ps[:, b:b + 3, :].rearrange("p b n -> p (b n)")[:, 0:n]

        def turn_bank(u, b):
            return 3 + (3 * u + b) % 4

        def piece(b):
            return 4 * b, min(4 * b + 4, NKT)

        def rstd_of(t, u):
            return tile_rstd[:, u:u + 1]

        def mod_col(t):
            return mod[:, bass.ds(t + 2 * KT, 1), 0:1].rearrange("p o v -> p (o v)")

        def row_of(v, n):
            return v[:, bass.ds(n, 1), :].rearrange("p o i -> p (o i)")

        def o_bank(g, e):
            return 0 if g == 0 else (6, 7, 1, 1)[e]

        O_GROUPS = ((2, 3, 4, 5), (6, 7, 0, 1))

        def decay_at(h, i):
            return head_decay[:, i:i + 1]

        UNITS_X, UNITS = 2 * KT, 3 * KT

        def unit_bank(u):
            if u < KT:
                return 2 + u % 6
            return 4 + u % 4 if u < UNITS_X else 5 + (u - UNITS_X) % 3

        def ada_block(n):
            return ada_0_3[:] if n % 3 == 0 else ada_1_2[:, n - 1]

        def unit_target(u):
            if u < UNITS_X:
                at = slice((u // KT) * W, (u // KT + 1) * W)
                return hx_hi[:, u % KT, at], hx_lo[:, u % KT, at]
            return hc_hi[:, u % KT, :], hc_lo[:, u % KT, :]

        def heads_index(b):
            return 0 if b == B_AKV else TT + CT

        def tiles_of(b0):
            return TT + CT if b0 < CTX_BLOCKS else TT

        class Steps:

            def __init__(self, eng, sem, start=0):
                self.eng, self.sem, self.n = eng, sem, start

            def then(self, ins):
                self.n = self.n + 1
                ins.then_inc(self.sem, 1)
                self.eng.wait_ge(self.sem, self.n)

        def first_split(done_3, done_all, c):
            return done_3 if c < 3 else done_all

        def unit_hi_half(act, u):
            n = W if u < UNITS_X else CTX
            act.wait_ge(unit_modulated, u + 1)
            act.copy(unit_target(u)[0], modulated[:, u % 2, 0:n]).then_inc(unit_hi, 1)

        block = held.enter_context(nc.Block())

        @block.sync
        def _(sp):
            sp.dma_start(ident[:], ident_in).then_inc(ident_in_s, 16)
            sp.dma_start(vec_rows[0:8, :], c.rearrange("o (k p) -> (o k) p", p=P)).then_inc(vec_in, 16)
            sp.dma_start(vec_rows[8:16, :], c_ctx.rearrange("(k p) -> k p", p=P)).then_inc(vec_in, 16)
            sp.dma_start(vec_rows[16:24, :], norm_w.rearrange("o (k p) -> (o k) p", p=P)).then_inc(vec_in, 16)
            sp.dma_start(vec_rows[24:48, :], b_ada.rearrange("o (k p) -> (o k) p", p=P)).then_inc(vec_in, 16)
            x_tiles = x[0].rearrange("(t p) d -> p t d", p=P)
            ada_tiles = w_ada[0].rearrange("(k p) n -> p k n", p=P)
            w_tiles = w_in[0].rearrange("(k p) n -> p k n", p=P)

            def load_ada(n):
                if n == 3:
                    sp.wait_ge(ada_used, 1)
                sp.dma_start(ada_block(n), ada_tiles[:, :, n * W:(n + 1) * W]).then_inc(ada_in[n], 16)

            def load_x(i):
                sp.dma_start(xs[:, 2 * i:2 * i + 2, :], x_tiles[:, 2 * i:2 * i + 2, :]).then_inc(x_in[i], 16)

            def load_weights(b, s):
                sp.dma_start(w_raw[s][:], w_tiles[:, :, bass.ds(b * W, W)]).then_inc(w_in_s[s], 16)

            load_ada(0)
            load_ada(1)
            load_x(0)
            load_x(1)
            load_ada(2)
            load_ada(3)
            load_weights(0, 0)
            load_x(2)
            load_x(3)
            sp.dma_start(cs[:], ctx[0].rearrange("(t p) d -> p t d", p=P)).then_inc(ctx_in, 16)

            def store_first(g):
                sp.wait_ge(tile_out, 2 * g + 2)
                sp.dma_start(proj_x[0, 2 * (g % 2):2 * (g % 2) + 2, :, (g // 2) * W:(g // 2 + 1) * W].rearrange("c p n -> p c n"),
                             stage[:, g % 2, :].rearrange("p (c n) -> p c n", c=2)).then_inc(stored[g % 2], 16)

            store_first(0)
            store_first(1)
            sp.wait_ge(unit_lo_pool, UNITS // 2)
            sp.wait_ge(unit_lo_dve, UNITS // 2)
            sp.wait_ge(unit_hi, UNITS)
            sp.wait_ge(decay_done, 8)
            load_weights(1, 1)
            rope_src = rope_in.rearrange("s (t p) e -> s p t e", p=P)
            for i in range(2):
                sp.dma_start(rope_cs[:, i], rope_src[i]).then_inc(small_in, 16)
                sp.dma_start(qk_norm[:, i, :], (q_norm_w if i == 0 else k_norm_w).partition_broadcast(P)
                             .rearrange("p o d -> p (o d)")).then_inc(small_in, 16)
            sp.wait_ge(w0_hi_done, 3)
            sp.wait_ge(w0_lo_done, 3)
            sp.wait_ge(w_lo_done, 1)
            load_weights(2, 0)
            store_first(2)
            store_first(3)
            sp.wait_ge(tile_out, 10)
            sp.dma_start(proj_c[0], stage_c[:].rearrange("p t n -> p (t n)")).then_inc(stored_c, 16)

            def project(b, s, more, kind):
                if more:
                    sp.wait_ge(w_hi_done, b + 1)
                    sp.wait_ge(w_lo_done, b + 1)
                    load_weights(b + 2, s)
                for g in range(4):
                    if kind in ("akv", "aq"):
                        base = 0 if kind == "akv" else TT + CT + (b - B_AQ) * TT
                        sp.wait_ge(heads_roped, base + 2 * g + 2)
                    else:
                        n0 = 10 * b if kind in ("rk", "rv") else 10 * CTX_BLOCKS + 8 * (b - CTX_BLOCKS)
                        sp.wait_ge(tile_out, n0 + 2 * g + 2)
                    sp.dma_start(proj_x[b, g], stage[:, g % 2, :]).then_inc(stored[g % 2], 16)
                if kind in ("rk", "rv", "akv"):
                    if kind == "akv":
                        sp.wait_ge(heads_roped, TT + CT)
                    else:
                        sp.wait_ge(tile_out, 10 * b + 10)
                    sp.dma_start(proj_c[b], stage_c[:].rearrange("p t n -> p (t n)")).then_inc(stored_c, 16)

            project(1, 1, True, "rk")
            with sp.Fori(B_RV, B_AKV, 2) as b:
                project(b, 0, True, "rv")
                project(b + 1, 1, True, "rv")
            project(B_AKV, 0, True, "akv")
            with sp.Fori(B_RQ, B_AQ, 2) as b:
                project(b, 1, True, "t")
                project(b + 1, 0, True, "t")
            project(B_AQ, 1, True, "aq")
            project(B_AQ + 1, 0, True, "aq")
            with sp.Fori(B_AG, NB - 3, 2) as b:
                project(b, 1, True, "t")
                project(b + 1, 0, True, "t")
            project(NB - 2, 1, False, "t")

            groups = proj_x.rearrange("b g p n -> (b g) p n")

            def load_head(h, first):
                pair, at = (h // 2, h % 2 * RDK) if isinstance(h, int) else (sp.snap(h // 2), sp.snap(h % 2 * RDK))
                k_at, v_at, q_at = 4 * B_RK + 2 * h, 4 * B_RV + 4 * h, 4 * B_RQ + 2 * h
                if not first:
                    sp.wait_ge(g03_lo_pool, 2 * h)
                    sp.wait_ge(kd_lo_done[0], 4 * h - 3)
                    sp.wait_ge(kd_lo_done[1], 4 * h - 3)
                sp.dma_start(ck_raw[:], proj_c[bass.ds(pair, 1)].rearrange("b p (t n) -> p (b t) n", t=CT)
                             [:, :, bass.ds(at, RDK)]).then_inc(ck_in, 16)
                if not first:
                    sp.wait_ge(cv_lo_done, h)
                sp.dma_start(cv_raw[:], proj_c[B_RV + h].rearrange("p (t n) -> p t n", t=CT)).then_inc(cv_in, 16)
                if not first:
                    sp.wait_ge(g12_lo_done, 3 * h)
                    sp.wait_ge(g03_lo_dve, h)
                    sp.wait_ge(k_turned[0], 3 * h)
                    sp.wait_ge(k_turned[1], 3 * h)
                sp.dma_start(rk_raw[:], groups[bass.ds(k_at, 2)].rearrange("g p n -> p g n")).then_inc(rk_in, 16)
                sp.dma_start(rv_raw[:], groups[bass.ds(v_at, 4)].rearrange("g p (t e) -> p g t e", t=2)).then_inc(rv_in, 16)
                sp.dma_start(rq_raw[:], groups[bass.ds(q_at, 2)].rearrange("g p n -> p g n")).then_inc(rq_in, 16)

            def load_gate(h):
                sp.dma_start(gate_y[:], groups[bass.ds(4 * B_RG + 4 * h, 4)].rearrange("g p n -> p g n")).then_inc(gate_in, 16)

            def store_y(h):
                sp.wait_ge(y_out, 8 * h + 8)
                sp.dma_start(y_ret[bass.ds(4 * h, 4)].rearrange("g p n -> p g n"), gate_y[:]).then_inc(y_stored, 16)
                sp.wait_ge(y_stored, 16 * h + 16)

            for s in range(2):
                sp.wait_ge(stored[s], 16 * 2 * (NB - 1))
            sp.wait_ge(stored_c, 16 * CTX_BLOCKS)
            sp.wait_ge(heads_roped, TT + CT + 2 * TT)
            sp.wait_ge(w_hi_done, NB - 1)
            sp.wait_ge(w_lo_done, NB - 1)
            sp.wait_ge(tile_done, 8 * (NB - 1) + 14)
            sp.dma_start(rel[:], rel_in).then_inc(rel_in_s, 16)
            load_head(0, True)
            project(NB - 1, 0, False, "t")
            load_gate(0)
            for s in range(2):
                sp.wait_ge(stored[s], 16 * 2 * NB)
            with sp.Fori(1, RH) as h:
                load_head(h, False)
                store_y(h - 1)
                load_gate(h)
            sp.wait_ge(g12_lo_done, 3 * RH)
            sp.wait_ge(g03_lo_pool, 2 * RH)
            sp.wait_ge(g03_lo_dve, RH)
            for i, src in ((0, groups[4 * B_AKV:4 * B_AKV + 4].rearrange("g p n -> p g n")), (TT, proj_c[B_AKV])):
                n = TT if i == 0 else CT
                dst = kv_raw[:, i:i + n, :].rearrange("p t n -> p (t n)")
                if i == 0:
                    dst = dst.rearrange("p (g n) -> p g n", g=4)
                sp.dma_start(dst, src).then_inc(kv_in, 16)

            def load_queries(t, half):
                pair, at = (t // 2, t % 2 * W) if isinstance(t, int) else (sp.snap(t // 2), sp.snap(t % 2 * W))
                if not (isinstance(t, int) and t == 0):
                    sp.wait_ge(aq_turned, 2 * t - 1 + half)
                row = groups[bass.ds(pair + 4 * (B_AQ + half), 1)].rearrange("g p n -> (g p) n")
                sp.dma_start(aq_raw[:, half, :], row[:, bass.ds(at, W)]).then_inc(aq_in[half], 16)

            def load_ada_gate(t):
                if not (isinstance(t, int) and t == 0):
                    sp.wait_ge(ada_g_done, t)
                sp.dma_start(ada_g[:], ada_tiles[:, :, bass.ds((t + 2 * KT) * P, P)]).then_inc(ada_g_in, 16)

            load_queries(0, 0)
            load_queries(0, 1)
            load_ada_gate(0)
            store_y(RH - 1)
            sp.dma_start(att_y[:], groups[4 * B_AG:4 * B_AG + 8].rearrange("g p n -> p g n")).then_inc(att_gate_in, 16)
            with sp.Fori(1, TT) as t:
                load_queries(t, 0)
                load_queries(t, 1)
                load_ada_gate(t)
            def store_attention(half):
                sp.wait_ge(att_out, 8 * half + 8)
                sp.dma_start(y_att.rearrange("h p n -> p h n")[:, :, half * W:(half + 1) * W],
                             att_y[:, :, half * W:(half + 1) * W]).then_inc(att_stored, 16)

            ow_ret = w_o_ret[0].rearrange("(b k p) n -> b p k n", p=P, k=KT)
            ow_att = w_o_att[0].rearrange("(k p) n -> p k n", p=P)
            ow_out = w_out[0].rearrange("(k p) n -> p k n", p=P)
            x_rows = x[0].rearrange("(t p) d -> p t d", p=P)
            out_rows = out[0].rearrange("(t p) d -> p t d", p=P)

            def load_chunk(half, c, slot, src):
                done = CHUNKS * half + c
                if not (isinstance(c, int) and half == 0 and c < 3):
                    sp.wait_ge(ow_lo_done, done - (1 if half and isinstance(c, int) and c < 2 else 2))
                sp.dma_start(ow_raw[slot][:], src).then_inc(ow_in[slot], 16)

            def load_chunks(half, n):
                at = bass.ds(n * P, P)
                load_chunk(half, 3 * n, 0, ow_ret[0][:, :, at])
                load_chunk(half, 3 * n + 1, 1, ow_ret[1][:, :, at])
                load_chunk(half, 3 * n + 2, 2, ow_att[:, :, at])

            def load_merge(half, n):
                load_chunks(half, n)
                load_gates(half, n)

            def load_gates(half, n):
                if not (isinstance(n, int) and half == 0 and n == 0):
                    sp.wait_ge(mg_used, KT * half + n)
                for i, b in enumerate((B_MR, B_MA)):
                    src = groups[bass.ds(n + 4 * b, 1)].rearrange("g p n -> (g p) n")
                    sp.dma_start(merge_gate[:, i, :], src[:, half * W:(half + 1) * W]).then_inc(mg_in, 16)

            def load_y(half, i):
                src = y_ret if i < KT else y_att
                a = 2 * i if i < KT else 2 * i - 2 * KT
                if half or i >= 3:
                    sp.wait_ge(y_lo_done, 3 * KT * half + 2 * i - 4)
                if half and i == KT:
                    sp.wait_ge(att_stored, 16 * HALVES)
                sp.dma_start(y_raw[i % 3][:], src[a:a + 2].rearrange("g p n -> p g n")[:, :, half * W:(half + 1) * W]).then_inc(y_in[i % 3], 16)

            def store_out(half, part):
                sp.wait_ge(out_added, KT * half + 2 * part + 2)
                at = slice(2 * part * P, (2 * part + 2) * P)
                sp.dma_start(out_rows[:, 4 * half:4 * half + 4, at], res[:, :, at]).then_inc(out_stored, 16)

            store_attention(0)
            sp.wait_ge(aq_turned, 2 * TT)
            sp.wait_ge(ak_lo_done, AKV)
            sp.wait_ge(av_lo_done, 1)
            load_chunk(0, 0, 0, ow_ret[0][:, :, 0:P])
            load_y(0, 0)
            load_chunk(0, 1, 1, ow_ret[1][:, :, 0:P])
            load_y(0, 1)
            load_chunk(0, 2, 2, ow_att[:, :, 0:P])
            sp.wait_ge(sc_bank, 3 * AH * TT)
            sp.wait_ge(ada_g_done, TT)
            load_y(0, 2)
            load_gates(0, 0)
            for i in range(3, 3 * KT // 2):
                if i == KT:
                    sp.wait_ge(att_stored, 16)
                load_y(0, i)
                if i == KT:
                    load_chunks(0, 1)
            store_attention(1)
            load_gates(0, 1)
            for half in range(HALVES):
                if half:
                    load_merge(half, 0)
                    store_out(0, 3)
                    sp.wait_ge(out_stored, 64)
                with sp.Fori(1 if half else 2, KT) as n:
                    load_merge(half, n)
                sp.dma_start(res[:], x_rows[:, 4 * half:4 * half + 4, :]).then_inc(res_in, 16)
                for n in range(3):
                    load_chunk(half, 3 * KT + n, n, ow_out[:, :, n * P:(n + 1) * P])
                for n in range(KT):
                    if n + 3 < KT:
                        load_chunk(half, 3 * KT + n + 3, n % 3, ow_out[:, :, (n + 3) * P:(n + 4) * P])
                    if half == 0:
                        for i in range(12 * n // 8, 12 * (n + 1) // 8):
                            load_y(1, i)
                    if n in (3, 5):
                        store_out(half, n // 2 - 1)
                store_out(half, 2)
            store_out(1, 3)
            sp.wait_ge(out_stored, 64 * HALVES)

        @block.gpsimd
        def _(pool):
            def unit_lo(u):
                hi, lo = unit_target(u)
                n = W if u < UNITS_X else CTX
                pool.wait_ge(unit_hi, u + 1)
                pool.tensor_tensor(lo, modulated[:, u % 2, 0:n], hi.bitcast(F32), ALU.subtract).then_inc(unit_lo_pool, 1)

            def first_lo(c):
                at = slice(c * P, (c + 1) * P)
                pool.wait_ge(first_split(w0_hi_done, w_hi_done, c), c % 3 + 1)
                pool.tensor_tensor(w_lo[0][:, :, at], w_raw[0][:, :, at], w_hi[0][:, :, at].bitcast(F32),
                                   ALU.subtract).then_inc(first_split(w0_lo_done, w_lo_done, c), 1)

            first_lo(0)
            for u in range(0, KT, 2):
                unit_lo(u)
            for c in range(1, 4):
                first_lo(c)
            for u in range(KT, UNITS, 2):
                unit_lo(u)

            def split_lo(b, s):
                pool.wait_ge(w_hi_done, b + 1)
                pool.tensor_tensor(w_lo[s][:], w_raw[s][:], w_hi[s][:].bitcast(F32), ALU.subtract).then_inc(w_lo_done, 1)

            split_lo(1, 1)
            with pool.Fori(2, NB - 1, 2) as b:
                split_lo(b, 0)
                split_lo(b + 1, 1)
            split_lo(NB - 1, 0)

            def lo(dst, hi, whole, done):
                pool.tensor_tensor(dst, whole, hi.bitcast(F32), ALU.subtract).then_inc(done, 1)

            def context_lo(h):
                pool.wait_ge(cv_hi_done, h + 1)
                lo(cv[1][:], cv[0][:], cv_raw[:], cv_lo_done)

            def outer_lo(h):
                for i, (r, raw) in enumerate(((rk, rk_raw), (rq, rq_raw))):
                    pool.wait_ge(g03_hi_done, 3 * h + i + 1)
                    lo(both(chunks_of(r[1]), PAIRS[0]), both(chunks_of(r[0]), PAIRS[0]), both(chunks_of(raw), PAIRS[0]), g03_lo_pool)

            def head(h, last):
                for s in range(NCH):
                    pool.wait_ge(probs_hi_done, NCH * h + s + 1)
                    lo(probs_r[1][:].rearrange("p t i -> p (t i)"), probs_r[0][:].rearrange("p t i -> p (t i)"), probs[:], probs_lo_done)
                    if s == 0:
                        for i, (r, raw, view) in enumerate(((rk, rk_raw, chunks_of), (rq, rq_raw, chunks_of), (rv, rv_raw, v_chunks))):
                            pool.wait_ge(g12_hi_done, 3 * h + i + 1)
                            lo(both(view(r[1]), PAIRS[1]), both(view(r[0]), PAIRS[1]), both(view(raw), PAIRS[1]), g12_lo_done)
                    if s == 2 and not last:
                        context_lo(h + 1)
                    if s == 3 and not last:
                        outer_lo(h + 1)

            context_lo(0)
            outer_lo(0)
            with pool.Fori(0, RH - 1) as h:
                head(h, False)
            head(RH - 1, True)

            pool.wait_ge(av_hi_done, 1)
            lo(av[1][:], av[0][:], kv_raw[:, :, AKV * AD:], av_lo_done)

            def split_chunk(half, c, slot, uses):
                pool.wait_ge(ow_hi_done, CHUNKS * half + c + 1)
                lo(ow[slot][1][:], ow[slot][0][:], ow_raw[slot][:], ow_lo_done)

            for half in range(HALVES):
                for i in range(3):
                    split_chunk(half, i, i, SLOT_USES[i] * half + 1)
                with pool.Fori(1, KT) as n:
                    for i in range(3):
                        split_chunk(half, 3 * n + i, i, SLOT_USES[i] * half + n + 1)
                for c in range(3 * KT, CHUNKS):
                    split_chunk(half, c, c % 3, SLOT_USES[c % 3] * half + c // 3 + 1)


        @block.scalar
        def _(act):
            act.dma_start(log2_decay[:], ret_log2_decay[0].rearrange("a h -> (a h)").partition_broadcast(P)).then_inc(small_in, 16)
            act.dma_start(decay_exp[:], decay_exp_in).then_inc(small_in, 16)
            act.wait_ge(vec_in, 64)
            act.activation(vec_rows[0:16, :], vec_rows[0:16, :], ACT.Silu).then_inc(vec_silu, 1)
            act.wait_ge(small_in, 32)
            act.activation(lg[:, 0, :], log2_decay[:], ACT.Exp, scale=LN2).then_inc(lg_act, 1)
            act.wait_ge(lg_dve, 1)
            act.activation(lg[:, 2, :], lg[:, 1, :], ACT.Ln).then_inc(lg_act, 1)
            act.wait_ge(lg_dve, 2)
            for h in range(RH):
                for d in range(2):
                    act.activation(decay[:, 10 * h + 5 * d:10 * h + 5 * d + 5], decay_exp[:, 5 * d:5 * d + 5], ACT.Exp,
                                   scale=log_gamma[:, RH * d + h:RH * d + h + 1]).then_inc(decay_done, 1)

            def token_squares(i):
                a, e = NORM_GROUPS[i]
                for t in range(a, e):
                    if t < TT:
                        act.wait_ge(x_in[t // 2], 16)
                    else:
                        act.wait_ge(ctx_in, 16)
                    if t:
                        act.wait_ge(x_squared, t)
                    src = xs[:, t, :] if t < TT else cs[:, t - TT, :]
                    act.activation(square_junk[:], src, ACT.Square, accum_out=ssq_x[:, t:t + 1]).then_inc(x_squared, 1)
                act.wait_ge(ms_done, i + 1)
                act.activation(rms_x[:, a:e], rms_x[:, a:e], ACT.Sqrt).then_inc(rms_done, 1)

            token_squares(0)
            for u in range(KT):
                unit_hi_half(act, u)
            token_squares(1)

            def plain_tile(b, n0, j, bank, func, scale):
                act.wait_ge(tile_done, n0 + j + 1)
                if j < TT:
                    g = j // 2
                    if j % 2 == 0 and not (isinstance(b, int) and b == 0 and g < 2):
                        act.wait_ge(stored[g % 2], 16 * (2 * b + g // 2))
                    dst = stage[:, g % 2, (j % 2) * W:(j % 2 + 1) * W]
                else:
                    if j == TT and not (isinstance(b, int) and b == 0):
                        act.wait_ge(stored_c, 16 * b)
                    dst = stage_c[:, j - TT, :]
                act.activation(dst, ps[:, bank, :], func, scale=scale).then_inc(tile_out, 1)

            def heads_tile(k, n, j, tiles, heads, stat):
                act.wait_ge(tile_done, n + 1)
                if not (isinstance(k, int) and k < 2):
                    act.wait_ge(heads_roped, k - 1)
                if not (isinstance(k, int) and k < 1):
                    act.wait_ge(heads_squared, k)
                act.copy(heads_in[:, j % 2, :], ps[:, j % (tiles // 2), :]).then_inc(tile_out, 1)
                act.wait_ge(tile_out, n + 1)
                for h in range(heads):
                    sq = act.activation(head_junk[:, h, :], heads_in[:, j % 2, h * AD:(h + 1) * AD], ACT.Square,
                                        accum_out=stat[:, h:h + 1])
                sq.then_inc(heads_squared, 1)

            units = iter(range(KT, UNITS))
            for j, n in enumerate((4, 4, 0, 0, 3, 3, 2, 0, 0, 0)):
                for _ in range(n):
                    unit_hi_half(act, next(units))
                plain_tile(0, 0, j, j % 5, ACT.Copy, RDK ** -0.5)
            for b in range(1, B_RV):
                for j in range(TT + CT):
                    plain_tile(b, 10 * b, j, j % 5, ACT.Copy, RDK ** -0.5)
            with act.Fori(B_RV, B_AKV, 1) as b:
                for j in range(TT + CT):
                    plain_tile(b, 10 * b, j, j % 5, ACT.Copy, 1.0)
            for j in range(TT + CT):
                heads_tile(j, 10 * B_AKV + j, j, TT + CT, AKV, ssq_k[:, j, :])
            act.wait_ge(heads_roped, TT + CT)
            with act.Fori(B_RQ, B_RG, 1) as b:
                for j in range(TT):
                    plain_tile(b, 8 * b + 14, j, j % 4, ACT.Copy, 1.0)
            with act.Fori(B_RG, B_AQ, 1) as b:
                for j in range(TT):
                    plain_tile(b, 8 * b + 14, j, j % 4, ACT.Silu, 1.0)
            for i in range(2):
                for j in range(TT):
                    heads_tile(TT + CT + TT * i + j, 8 * (B_AQ + i) + 14 + j, j, TT, 4, ssq_q[:, j, 4 * i:4 * i + 4])
            act.wait_ge(heads_roped, TT + CT + 2 * TT)
            with act.Fori(B_AG, B_MR, 1) as b:
                for j in range(TT):
                    plain_tile(b, 8 * b + 14, j, j % 4, ACT.Silu, 1.0)
            with act.Fori(B_MR, NB - 1, 1) as b:
                for j in range(TT):
                    plain_tile(b, 8 * b + 14, j, j % 4, ACT.Sigmoid, 1.0)
            def last_tile(j):
                plain_tile(NB - 1, 8 * (NB - 1) + 14, j, j % 4, ACT.Sigmoid, 1.0)

            def kd_hi(h, m, d):
                if not (isinstance(h, int) and h == 0 and m == 0):
                    act.wait_ge(delta_done[d], 4 * h + m)
                if m == 0:
                    act.wait_ge(ck_in, 16 * h + 16)
                else:
                    act.wait_ge(k_turned[d], 3 * h + m)
                for j in range(2):
                    src = ck_raw[:, j, :] if m == 0 else ps[:, 0, j * RDK:(j + 1) * RDK]
                    ins = act.activation(kd[d][0][:, j, :], src, ACT.Copy, scale=kd_decay[:, d, j:j + 1])
                ins.then_inc(kd_hi_done[d], 1)

            def state_hi(h, m, d):
                act.wait_ge(state_done[d], 4 * h + m + 1)
                if not (isinstance(h, int) and h == 0 and m == 0):
                    act.wait_ge(cross_done[d], 4 * h + m)
                act.copy(state_r[d][0][:], state[d][:]).then_inc(state_hi_done[d], 1)

            def o_squares(h, g):
                first = isinstance(h, int) and h == 0 and g == 0
                act.wait_ge(intra_out, 4 * h + 3 + g)
                act.wait_ge(cross_out[1], 4 * h + 3 + g)
                for i, t in enumerate(O_GROUPS[g]):
                    if not (first and i == 0):
                        act.wait_ge(o_squared, 8 * h + 4 * g + i)
                    act.activation(ret_junk[:], ret_o[:, t, :], ACT.Square,
                                   accum_out=ret_ms[:, 0, 4 * g + i:4 * g + i + 1]).then_inc(o_squared, 1)

            def o_root(h, g):
                act.wait_ge(o_ms, 2 * h + g + 1)
                act.activation(ret_ms[:, 1, 4 * g:4 * g + 4], ret_ms[:, 1, 4 * g:4 * g + 4], ACT.Sqrt).then_inc(o_rms, 1)

            def o_scale(h, g):
                act.wait_ge(o_rstd, 2 * h + g + 1)
                for i, t in enumerate(O_GROUPS[g]):
                    ins = act.activation(ret_o[:, t, :], ret_o[:, t, :], ACT.Copy, scale=ret_ms[:, 2, 4 * g + i:4 * g + i + 1])
                ins.then_inc(o_normed, 1)

            def cross_first(h, s, d):
                c = s if d == 0 else NCH - 1 - s
                act.wait_ge(cross_done[d], 4 * h + s + 1)
                act.wait_ge(head_ready, h + 1)
                if not (isinstance(h, int) and h == 0):
                    act.wait_ge(o_turned, 8 * h)
                for i in range(2):
                    ins = act.activation(ret_o[:, 2 * c + i, :], ps[:, 2 + 2 * d + i, :], ACT.Copy, scale=decay_at(h, 5 * d + i))
                ins.then_inc(cross_out[d], 1)

            def context_keys(h):
                act.wait_ge(kd_ready, 2 * h + 2)
                kd_hi(h, 0, 0)
                kd_hi(h, 0, 1)

            def mask_exps(h):
                if not (isinstance(h, int) and h == 0):
                    act.wait_ge(probs_done, 4 * h)
                for d, m in enumerate((mask, mask_b)):
                    act.activation(m[:], rel[:, d, :], ACT.Exp, scale=head_gamma[:, d:d + 1]).then_inc(mask_exp, 1)

            def probs_hi(h, s):
                act.wait_ge(probs_done, 4 * h + s + 1)
                if not (isinstance(h, int) and h == 0 and s == 0):
                    act.wait_ge(intra_done, 4 * h + s)
                act.copy(probs_r[0][:].rearrange("p t i -> p (t i)"), probs[:]).then_inc(probs_hi_done, 1)

            def head(h, last):
                first = isinstance(h, int) and h == 0
                for s in range(NCH):
                    if s == 0 and not first:
                        o_squares(h - 1, 1)
                    state_hi(h, s, 0)
                    if s == 0 and not first:
                        o_root(h - 1, 1)
                    state_hi(h, s, 1)
                    if s == 0 and not first:
                        o_scale(h - 1, 1)
                    probs_hi(h, s)
                    if s == 1:
                        cross_first(h, s, 0)
                    if s < NCH - 1:
                        kd_hi(h, s + 1, 0)
                    if s == 1:
                        cross_first(h, s, 1)
                    if s < NCH - 1:
                        kd_hi(h, s + 1, 1)
                    if s == 0:
                        cross_first(h, s, 0)
                        cross_first(h, s, 1)
                if not last:
                    context_keys(h + 1)
                o_squares(h, 0)
                if not last:
                    mask_exps(h + 1)
                o_root(h, 0)
                o_scale(h, 0)

            for j in range(6):
                last_tile(j)
            act.wait_ge(rel_in_s, 16)
            context_keys(0)
            mask_exps(0)
            last_tile(6)
            last_tile(7)
            head(0, False)
            act.wait_ge(ms_qk, 1)
            act.activation(rms_k[:], rms_k[:], ACT.Sqrt)
            act.activation(rms_q[:], rms_q[:], ACT.Sqrt).then_inc(rms_qk, 1)
            with act.Fori(1, RH - 1) as h:
                head(h, False)
            head(RH - 1, True)

            def keys_hi(g):
                act.wait_ge(ak_turned, g + 1)
                act.copy(ak[0][:, g, :], bank_span(2, KEYS)).then_inc(ak_hi_done, 1)

            o_squares(RH - 1, 1)
            keys_hi(0)
            o_root(RH - 1, 1)
            o_scale(RH - 1, 1)
            keys_hi(1)

            def queries_hi(t, half):
                act.wait_ge(aq_turned, 2 * t + half + 1)
                act.copy(aq[0][:, 4 * half:4 * half + 4, :].rearrange("p h i -> p (h i)"), ps[:, 6, :]).then_inc(aq_hi_done, 1)

            def exponent(t, u):
                k = AH * t + u
                act.wait_ge(neg_done, k + 1)
                if not (isinstance(t, int) and t == 0 and u < 2):
                    act.wait_ge(soft_turned, k - 1)
                act.activation(soft[u % 2][:], bank_span(0, KEYS), ACT.Exp, bias=neg_max[:, u % 2:u % 2 + 1],
                               scale=rstd_of(t, u), accum_out=row_sum[:, u % 2:u % 2 + 1]).then_inc(exp_done, 1)

            def scale_soft(t, u):
                k = AH * t + u
                act.wait_ge(inv_done, k + 1)
                act.activation(soft[u % 2][:], soft[u % 2][:], ACT.Copy, scale=row_inv[:, u % 2:u % 2 + 1]).then_inc(soft_done, 1)

            def soft_hi_half(t, u):
                k = AH * t + u
                if isinstance(t, int) and t == 0 and u == 0:
                    act.wait_ge(y_stored, 16 * RH)
                act.wait_ge(soft_turned, k + 1)
                b = 0
                while b < 3:
                    e = b + 1
                    while e < 3 and turn_bank(u, e) > turn_bank(u, b):
                        e += 1
                    k0, k1 = piece(b)[0], piece(e - 1)[1]
                    src = ps[:, turn_bank(u, b):turn_bank(u, e - 1) + 1, :].rearrange("p b n -> p (b n)")[:, 0:(k1 - k0) * P]
                    ins = act.copy(soft_t[u // 4][0][:, k0:k1, u % 4, :], src.rearrange("p (k i) -> p k i", i=P))
                    b = e
                ins.then_inc(soft_hi, 1)

            def tile(t):
                first = isinstance(t, int) and t == 0
                for u in range(AH):
                    exponent(t, u)
                    scale_soft(t, u)
                    if u > 0:
                        soft_hi_half(t, u - 1)
                    elif not first:
                        soft_hi_half(t - 1, AH - 1)
                    if u == 1:
                        queries_hi(t, 1)
                    if u == 5 and not (isinstance(t, int) and t == TT - 1):
                        queries_hi(t + 1, 0)

            queries_hi(0, 0)
            tile(0)
            with act.Fori(1, TT - 1) as t:
                tile(t)
            tile(TT - 1)
            soft_hi_half(TT - 1, AH - 1)

            def chunk_hi(half, c, slot, uses):
                act.wait_ge(ow_in[slot], 16 * uses)
                if not (isinstance(c, int) and half == 0 and c < 3):
                    act.wait_ge(ow_used, CHUNKS * half + c - (1 if half and isinstance(c, int) and c < 2 else 2))
                act.copy(ow[slot][0][:], ow_raw[slot][:]).then_inc(ow_hi_done, 1)

            def chunk_hi_at(half, c):
                chunk_hi(half, c, c % 3, SLOT_USES[c % 3] * half + c // 3 + 1)

            def y_hi(half, i):
                act.wait_ge(y_in[(i // 2) % 3], 16 * (KT // 2 * half + i // 6 + 1))
                act.copy(y_r(i, 0), y_raw[(i // 2) % 3][:, i % 2, :]).then_inc(y_hi_done, 1)

            for half in range(HALVES):
                if half == 0:
                    chunk_hi_at(0, 0)
                    act.wait_ge(pv_done, 2 * TT - 1)
                    for i in range(10):
                        y_hi(0, i)
                        if i == 1:
                            chunk_hi_at(0, 1)
                    act.wait_ge(pv_done, 2 * TT)
                    for i in range(10, 3 * KT):
                        y_hi(0, i)
                        if i in (11, 18, 21):
                            chunk_hi_at(0, {11: 2, 18: 3, 21: 4}[i])
                    chunk_hi_at(0, 5)
                else:
                    chunk_hi_at(1, 1)
                    chunk_hi_at(1, 2)
                with act.Fori(1 if half else 2, KT) as n:
                    for i in range(3):
                        chunk_hi(half, 3 * n + i, i, SLOT_USES[i] * half + n + 1)
                for c in range(3):
                    chunk_hi_at(half, 3 * KT + c)
                for n in range(KT):
                    k = KT * half + n
                    if half == 0 and n == KT - 1:
                        chunk_hi_at(1, 0)
                    act.wait_ge(ow_used, CHUNKS * half + 3 * KT + n + 1)
                    if k >= 2:
                        act.wait_ge(out_turned, k - 1)
                    act.activation(out_t[:, n % 2, :], ps[:, 2 + n % 2, :], ACT.Copy, scale=mod[:, 2 * KT + n, 0:1]).then_inc(out_gated, 1)
                    if n + 3 < KT:
                        chunk_hi_at(half, 3 * KT + n + 3)
                    if half == 0:
                        for i in range(3 * n, 3 * n + 3):
                            y_hi(1, i)

        @block.vector
        def _(dve):
            own = Steps(dve, dve_step)
            dve.wait_ge(vec_turned, 1)
            dve.tensor_copy(vec_cols[:], ps[:, 0, 0:48]).then_inc(vec_copied, 1)

            def norm_group(i):
                a, e = NORM_GROUPS[i]
                dve.wait_ge(x_squared, e)
                dve.tensor_scalar(rms_x[:, a:e], ssq_x[:, a:e], 1.0 / D, EPS, ALU.mult, ALU.add).then_inc(ms_done, 1)
                dve.wait_ge(rms_done, i + 1)
                own.then(dve.reciprocal(rstd_x[:, a:e], rms_x[:, a:e]))
                for t in range(a, e):
                    v = xs[:, t, :] if t < TT else cs[:, t - TT, :]
                    dve.tensor_scalar(v, v, rstd_x[:, t:t + 1], None, ALU.mult).then_inc(x_normed, 1)

            def unit(u):
                hi, lo = unit_target(u)
                n = W if u < UNITS_X else CTX
                v = 0 if u < UNITS_X else 1
                dve.wait_ge(unit_turned, u + 1)
                if u >= 2:
                    dve.wait_ge(unit_hi, u - 1)
                    if u % 2:
                        dve.wait_ge(unit_lo_dve, (u - 1) // 2)
                    else:
                        dve.wait_ge(unit_lo_pool, u // 2)
                dve.tensor_scalar(modulated[:, u % 2, 0:n], ps[:, unit_bank(u), 0:n], a_col[:, u % KT, v:v + 1],
                                  mod[:, u % KT, v:v + 1], ALU.mult, ALU.add).then_inc(unit_modulated, 1)

            def unit_lo(u):
                hi, lo = unit_target(u)
                n = W if u < UNITS_X else CTX
                dve.wait_ge(unit_hi, u + 1)
                dve.tensor_tensor(lo, modulated[:, u % 2, 0:n], hi.bitcast(F32), ALU.subtract).then_inc(unit_lo_dve, 1)

            dve.wait_ge(lg_act, 1)
            u_, w_, ln_, d_, m_, r_ = (lg[:, i, :] for i in range(6))
            dve.tensor_scalar(w_, u_, -1.0, 1.0, ALU.mult, ALU.add).then_inc(lg_dve, 1)
            dve.wait_ge(lg_dve, 1)
            own.then(dve.tensor_scalar(d_, w_, -1.0, None, ALU.add))
            own.then(dve.tensor_scalar(m_, d_, 0.0, None, ALU.is_equal))
            own.then(dve.tensor_tensor(d_, d_, m_, ALU.add))
            own.then(dve.reciprocal(r_, d_))
            own.then(dve.tensor_tensor(r_, r_, u_, ALU.mult))
            dve.wait_ge(lg_act, 2)
            own.then(dve.tensor_tensor(r_, r_, ln_, ALU.mult))
            own.then(dve.tensor_tensor(m_, m_, u_, ALU.mult))
            own.then(dve.tensor_tensor(r_, r_, m_, ALU.add))
            dve.tensor_scalar(log_gamma[:], r_, -1.0, None, ALU.mult).then_inc(lg_dve, 1)

            def rows_from_psum(n):
                dve.wait_ge(ada_used, n + 1)
                dve.tensor_copy(ada_rows[:, n * W:(n + 1) * W], ps[0:2, n % 2, :]).then_inc(rows_out, 1)

            rows_from_psum(0)
            norm_group(0)
            for n in range(1, 4):
                rows_from_psum(n)
            dve.wait_ge(ada_turned, 1)
            own.then(dve.tensor_tensor(mod[:, 0:2 * KT, :], ps[:, 0, 0:4 * KT].rearrange("p (n v) -> p n v", v=2),
                                       vec_cols[:, 24:24 + 2 * KT].unsqueeze(2).to_broadcast([P, 2 * KT, 2]), ALU.add))
            own.then(dve.tensor_scalar(a_col[:], mod[:, KT:2 * KT, :], 1.0, None, ALU.add))
            own.then(dve.tensor_tensor(a_col[:], a_col[:], vec_cols[:, 16:24].unsqueeze(2).to_broadcast([P, KT, 2]),
                                       ALU.mult))

            def split_hi(b, s, used_tiles, loads):
                if used_tiles is not None:
                    dve.wait_ge(tile_done, used_tiles)
                dve.wait_ge(w_in_s[s], 16 * loads)
                dve.tensor_copy(w_hi[s][:], w_raw[s][:]).then_inc(w_hi_done, 1)

            def first_hi(c):
                at = slice(c * P, (c + 1) * P)
                dve.wait_ge(w_in_s[0], 16)
                dve.tensor_copy(w_hi[0][:, :, at], w_raw[0][:, :, at]).then_inc(first_split(w0_hi_done, w_hi_done, c), 1)

            for u in range(UNITS):
                if u == KT:
                    norm_group(1)
                if u == 0:
                    first_hi(0)
                if u == 4:
                    first_hi(1)
                if u == 6:
                    first_hi(2)
                if u == 7:
                    first_hi(3)
                unit(u)
                if u % 2:
                    unit_lo(u)

            def rotate_tile(k, n, j, heads, t, w_index, dst, slot_free):
                src = heads_in[:, j % 2, :]
                dve.wait_ge(tile_out, n + 1)
                slot_free()
                wide = heads * AD
                bcast = qk_norm[:, w_index, :].unsqueeze(1).to_broadcast([P, heads, AD])
                to = heads_w[:, 0:wide] if t is not None else dst[:, 0:wide]
                if wide < W:
                    own.then(dve.tensor_copy(dst[:, wide:W], src[:, wide:W]))
                ins = dve.tensor_tensor(to.rearrange("p (h e) -> p h e", h=heads),
                                        src[:, 0:wide].rearrange("p (h e) -> p h e", h=heads), bcast, ALU.mult)
                if t is None:
                    ins.then_inc(heads_roped, 1)
                    return
                own.then(ins)

                def pairs(v):
                    return v[:, 0:wide].rearrange("p (h e two) -> p h e two", h=heads, two=2)

                def table(i):
                    return rope_cs[:, i, t, :].unsqueeze(1).to_broadcast([P, heads, AD // 2])

                xw, rot, d = pairs(heads_w), pairs(rope_t), pairs(dst)
                dve.tensor_tensor(d[:, :, :, 0], xw[:, :, :, 0], table(0), ALU.mult)
                own.then(dve.tensor_tensor(d[:, :, :, 1], xw[:, :, :, 1], table(0), ALU.mult))
                dve.tensor_tensor(rot[:, :, :, 0], xw[:, :, :, 1], table(1), ALU.mult)
                own.then(dve.tensor_tensor(rot[:, :, :, 1], xw[:, :, :, 0], table(1), ALU.mult))
                own.then(dve.tensor_tensor(d[:, :, :, 0], d[:, :, :, 0], rot[:, :, :, 0], ALU.subtract))
                dve.tensor_tensor(d[:, :, :, 1], d[:, :, :, 1], rot[:, :, :, 1], ALU.add).then_inc(heads_roped, 1)
                dve.wait_ge(heads_roped, k + 1)

            def stage_slot(b, j):
                def free():
                    if j % 2 == 0:
                        dve.wait_ge(stored[(j // 2) % 2], 16 * (2 * b + j // 4))
                return stage[:, (j // 2) % 2, (j % 2) * W:(j % 2 + 1) * W], free

            split_hi(1, 1, None, 1)
            split_hi(2, 0, 10, 2)
            split_hi(3, 1, 20, 2)
            with dve.Fori(4, B_AKV + 2, 2) as b:
                split_hi(b, 0, 10 * b - 10, b // 2 + 1)
                split_hi(b + 1, 1, 10 * b, b // 2 + 1)
            dve.wait_ge(small_in, 96)
            for j in range(TT + CT):
                if j < TT:
                    dst, free = stage_slot(B_AKV, j)
                    rotate_tile(j, 10 * B_AKV + j, j, AKV, j, 1, dst, free)
                else:
                    rotate_tile(j, 10 * B_AKV + j, j, AKV, None, 1, stage_c[:, j - TT, :],
                                lambda: dve.wait_ge(stored_c, 16 * B_AKV))
            with dve.Fori(8, 14, 2) as b:
                split_hi(b, 0, 8 * b + 6, b // 2 + 1)
                split_hi(b + 1, 1, 8 * b + 14, b // 2 + 1)
            for i in range(2):
                b = B_AQ + i
                split_hi(b + 1, (b + 1) % 2, 8 * b + 14, (b + 1) // 2 + 1)
                for j in range(TT):
                    dst, free = stage_slot(b, j)
                    rotate_tile(TT + CT + TT * i + j, 8 * b + 14 + j, j, 4, j, 0, dst, free)
            with dve.Fori(16, NB - 1, 2) as b:
                split_hi(b, 0, 8 * b + 6, b // 2 + 1)
                split_hi(b + 1, 1, 8 * b + 14, b // 2 + 1)
            split_hi(NB - 1, 0, 8 * (NB - 1) + 6, (NB - 1) // 2 + 1)

            def kd_lo(h, m, d):
                dve.wait_ge(kd_hi_done[d], 4 * h + m + 1)
                for j in range(2):
                    src = ck_raw[:, j, :] if m == 0 else ps[:, 0, j * RDK:(j + 1) * RDK]
                    ins = dve.scalar_tensor_tensor(out=kd[d][1][:, j, :], in0=src, scalar=kd_decay[:, d, j:j + 1],
                                                   in1=kd[d][0][:, j, :].bitcast(F32), op0=ALU.mult, op1=ALU.subtract)
                ins.then_inc(kd_lo_done[d], 1)

            def delta_ps(d):
                return ps[:, 2 + 2 * d:4 + 2 * d, :]

            def update_state(h, m, d):
                dve.wait_ge(delta_done[d], 4 * h + m + 1)
                if not (isinstance(h, int) and h == 0 and m == 0):
                    dve.wait_ge(state_lo_done[d], 4 * h + m)
                    dve.wait_ge(state_hi_done[d], 4 * h + m)
                if m == 0:
                    dve.tensor_copy(state[d][:], delta_ps(d)).then_inc(state_done[d], 1)
                else:
                    dve.scalar_tensor_tensor(out=state[d][:], in0=state[d][:], scalar=decay_at(h, 5 * d + 4),
                                             in1=delta_ps(d), op0=ALU.mult, op1=ALU.add).then_inc(state_done[d], 1)

            def state_lo(h, m, d):
                dve.wait_ge(state_hi_done[d], 4 * h + m + 1)
                dve.tensor_tensor(state_r[d][1][:], state[d][:], state_r[d][0][:].bitcast(F32),
                                  ALU.subtract).then_inc(state_lo_done[d], 1)

            def mean_square(h, g):
                dve.wait_ge(o_squared, 8 * h + 4 * g + 4)
                dve.tensor_scalar(ret_ms[:, 1, 4 * g:4 * g + 4], ret_ms[:, 0, 4 * g:4 * g + 4], 1.0 / RDV, EPS,
                                  ALU.mult, ALU.add).then_inc(o_ms, 1)

            def rstd(h, g):
                dve.wait_ge(o_rms, 2 * h + g + 1)
                dve.reciprocal(ret_ms[:, 2, 4 * g:4 * g + 4], ret_ms[:, 1, 4 * g:4 * g + 4]).then_inc(o_rstd, 1)

            def gated(h, g, e):
                bank = o_bank(g, e)
                dve.wait_ge(o_turned, 8 * h + 4 * g + e + 1)
                dve.wait_ge(gate_in, 16 * h + 16)
                if g == 0:
                    v = gate_y[:, e, 2 * P:6 * P]
                    dve.tensor_tensor(v, ps[:, bank, :], v, ALU.mult).then_inc(y_out, 1)
                else:
                    v = gate_y[:, e, 6 * P:8 * P]
                    dve.tensor_tensor(v, ps[:, bank, 0:2 * P], v, ALU.mult)
                    v = gate_y[:, e, 0:2 * P]
                    dve.tensor_tensor(v, ps[:, bank, 2 * P:4 * P], v, ALU.mult).then_inc(y_out, 1)

            def cross_again(h, s, d):
                c = s if d == 0 else NCH - 1 - s
                dve.wait_ge(cross_done[d], 4 * h + s + 1)
                dve.wait_ge(cross_out[1 - d], 4 * h + NCH - s)
                if d == 1:
                    dve.wait_ge(intra_out, 4 * h + NCH - s)
                for i in range(2):
                    ins = dve.scalar_tensor_tensor(out=ret_o[:, 2 * c + i, :], in0=ps[:, 2 + 2 * d + i, :],
                                                   scalar=decay_at(h, 5 * d + i), in1=ret_o[:, 2 * c + i, :],
                                                   op0=ALU.mult, op1=ALU.add)
                ins.then_inc(cross_out[d], 1)

            def key_decays(h):
                if not (isinstance(h, int) and h == 0):
                    dve.wait_ge(mask_exp, 2 * h)
                    dve.wait_ge(kd_hi_done[0], 4 * h)
                    dve.wait_ge(kd_hi_done[1], 4 * h)
                    dve.wait_ge(kd_lo_done[0], 4 * h)
                    dve.wait_ge(kd_lo_done[1], 4 * h)
                dve.tensor_scalar(kd_decay[:], decay[:, bass.ds(h * 10, 10)].rearrange("p (d c) -> p d c", d=2)[:, :, 2:4],
                                  1.0, None, ALU.mult).then_inc(kd_ready, 1)
                dve.tensor_scalar(head_gamma[:], log_gamma[:].rearrange("p (d h) -> p d h", d=2)[:, :, bass.ds(h, 1)]
                                  .rearrange("p d o -> p (d o)"), 1.0, None, ALU.mult).then_inc(kd_ready, 1)
                dve.wait_ge(kd_ready, 2 * h + 2)

            def head_decays(h):
                if not (isinstance(h, int) and h == 0):
                    dve.wait_ge(cross_out[0], 4 * h)
                    dve.wait_ge(cross_out[1], 4 * h)
                dve.tensor_scalar(head_decay[:], decay[:, bass.ds(h * 10, 10)], 1.0, None, ALU.mult).then_inc(head_ready, 1)
                dve.wait_ge(head_ready, h + 1)

            def context_values(h):
                dve.wait_ge(cv_in, 16 * h + 16)
                if not (isinstance(h, int) and h == 0):
                    dve.wait_ge(delta_done[1], 4 * h - 3)
                dve.tensor_copy(cv[0][:], cv_raw[:]).then_inc(cv_hi_done, 1)

            OPERANDS = ((rk, rk_raw, chunks_of, rk_in), (rq, rq_raw, chunks_of, rq_in), (rv, rv_raw, v_chunks, rv_in))

            def outer_hi(h, i):
                r, raw, view, arrived = OPERANDS[i]
                dve.wait_ge(arrived, 16 * h + 16)
                dve.tensor_copy(both(view(r[0]), PAIRS[0]), both(view(raw), PAIRS[0])).then_inc(g03_hi_done, 1)

            def inner_hi(i):
                r, raw, view, _ = OPERANDS[i]
                dve.tensor_copy(both(view(r[0]), PAIRS[1]), both(view(raw), PAIRS[1])).then_inc(g12_hi_done, 1)

            def outer_values_lo(h):
                dve.wait_ge(g03_hi_done, 3 * h + 3)
                dve.tensor_tensor(both(v_chunks(rv[1]), PAIRS[0]), both(v_chunks(rv_raw), PAIRS[0]),
                                  both(v_chunks(rv[0]), PAIRS[0]).bitcast(F32), ALU.subtract).then_inc(g03_lo_dve, 1)

            def make_mask(h):
                dve.wait_ge(mask_exp, 2 * h + 2)
                dve.tensor_tensor(mask[:], mask[:], rel[:, 2, :], ALU.mult).then_inc(mask_done, 1)
                dve.tensor_tensor(mask_b[:], mask_b[:], rel[:, 3, :], ALU.mult).then_inc(mask_done, 1)
                dve.wait_ge(mask_done, 3 * h + 2)
                dve.tensor_tensor(mask[:], mask[:], mask_b[:], ALU.add).then_inc(mask_done, 1)

            def new_state(h, m):
                update_state(h, m, 0)
                state_lo(h, m, 0)
                update_state(h, m, 1)

            def mask_scores(h, s):
                dve.wait_ge(scores_done, 4 * h + s + 1)
                if s == 0:
                    dve.wait_ge(mask_done, 3 * h + 3)
                if isinstance(h, int) and h == 0 and s == 0:
                    for i in range(2):
                        dve.wait_ge(stored[i], 16 * 2 * NB)
                if not (isinstance(h, int) and h == 0 and s == 0):
                    dve.wait_ge(probs_lo_done, 4 * h + s)
                dve.tensor_tensor(probs[:], ps[:, 1, :], mask[:], ALU.mult).then_inc(probs_done, 1)

            def add_intra(h, s):
                dve.wait_ge(intra_done, 4 * h + s + 1)
                dve.wait_ge(cross_out[0], 4 * h + s + 1)
                v = ret_o[:, 2 * s:2 * s + 2, :]
                dve.tensor_tensor(v, v, ps[:, 6:8, :], ALU.add).then_inc(intra_out, 1)

            def head(h, last):
                first = isinstance(h, int) and h == 0
                mask_scores(h, 0)
                if not first:
                    gated(h - 1, 0, 2)
                state_lo(h, 0, 1)
                outer_values_lo(h)
                if not first:
                    gated(h - 1, 0, 3)
                    gated(h - 1, 1, 0)
                    gated(h - 1, 1, 1)
                kd_lo(h, 1, 0)
                inner_hi(0)
                inner_hi(1)
                if not first:
                    gated(h - 1, 1, 2)
                kd_lo(h, 1, 1)
                if not first:
                    gated(h - 1, 1, 3)
                inner_hi(2)
                add_intra(h, 0)
                new_state(h, 1)
                mask_scores(h, 1)
                state_lo(h, 1, 1)
                kd_lo(h, 2, 0)
                kd_lo(h, 2, 1)
                add_intra(h, 1)
                new_state(h, 2)
                mask_scores(h, 2)
                state_lo(h, 2, 1)
                cross_again(h, 2, 0)
                kd_lo(h, 3, 0)
                cross_again(h, 2, 1)
                kd_lo(h, 3, 1)
                if not last:
                    context_values(h + 1)
                add_intra(h, 2)
                new_state(h, 3)
                mask_scores(h, 3)
                state_lo(h, 3, 1)
                if not last:
                    key_decays(h + 1)
                cross_again(h, 3, 0)
                if not last:
                    kd_lo(h + 1, 0, 0)
                    kd_lo(h + 1, 0, 1)
                    outer_hi(h + 1, 0)
                cross_again(h, 3, 1)
                mean_square(h, 0)
                if not last:
                    outer_hi(h + 1, 1)
                    make_mask(h + 1)
                rstd(h, 0)
                if last:
                    normalise_keys()
                add_intra(h, 3)
                if last:
                    gated(h, 0, 0)
                    gated(h, 0, 1)
                    mean_square(h, 1)
                    keys_lo(0)
                    gated(h, 0, 2)
                    gated(h, 0, 3)
                    rstd(h, 1)
                    values_hi()
                    keys_lo(1)
                else:
                    head_decays(h + 1)
                    outer_hi(h + 1, 2)
                    update_state(h + 1, 0, 0)
                    gated(h, 0, 0)
                    state_lo(h + 1, 0, 0)
                    mean_square(h, 1)
                    update_state(h + 1, 0, 1)
                    rstd(h, 1)
                    gated(h, 0, 1)

            def normalise_keys():
                dve.wait_ge(rms_qk, 1)
                dve.reciprocal(rstd_k[:], rms_k[:]).then_inc(rstd_qk, 1)
                dve.reciprocal(rstd_q[:], rms_q[:]).then_inc(rstd_qk, 1)
                dve.wait_ge(rstd_qk, 2)
                dve.wait_ge(kv_in, 32)
                keys = kv_raw[:, :, 0:AKV * AD].rearrange("p t (h e) -> p t h e", h=AKV)
                for g in range(AKV):
                    r = rstd_k[:].rearrange("p (t h) -> p t h", h=AKV)[:, :, g:g + 1].to_broadcast([P, NKT, AD])
                    dve.tensor_tensor(keys[:, :, g, :], keys[:, :, g, :], r, ALU.mult).then_inc(keys_normed, 1)

            def values_hi():
                for d in range(2):
                    dve.wait_ge(k_turned[d], 3 * RH)
                dve.wait_ge(g12_lo_done, 3 * RH)
                dve.tensor_copy(av[0][:], kv_raw[:, :, AKV * AD:]).then_inc(av_hi_done, 1)

            def keys_lo(g):
                dve.wait_ge(ak_hi_done, g + 1)
                dve.tensor_tensor(ak[1][:, g, :], bank_span(2, KEYS), ak[0][:, g, :].bitcast(F32), ALU.subtract).then_inc(ak_lo_done, 1)

            key_decays(0)
            head_decays(0)
            context_values(0)
            kd_lo(0, 0, 0)
            kd_lo(0, 0, 1)
            outer_hi(0, 0)
            dve.wait_ge(w_lo_done, NB)
            outer_hi(0, 1)
            make_mask(0)
            dve.wait_ge(tile_done, 8 * NB + 14)
            outer_hi(0, 2)
            dve.wait_ge(heads_squared, TT + CT + 2 * TT)
            dve.tensor_scalar(rms_k[:], ssq_k[:].rearrange("p t h -> p (t h)"), 1.0 / AD, EPS, ALU.mult, ALU.add)
            dve.tensor_scalar(rms_q[:], ssq_q[:].rearrange("p t h -> p (t h)"), AD * EPS, None, ALU.add).then_inc(ms_qk, 1)
            new_state(0, 0)
            head(0, False)
            with dve.Fori(1, RH - 1) as h:
                head(h, False)
            head(RH - 1, True)
            for e in range(4):
                gated(RH - 1, 1, e)


            def queries_lo(t, half):
                dve.wait_ge(aq_hi_done, 2 * t + half + 1)
                dst, hi = (v[:, 4 * half:4 * half + 4, :].rearrange("p h i -> p (h i)") for v in (aq[1], aq[0]))
                dve.tensor_tensor(dst, ps[:, 6, :], hi.bitcast(F32), ALU.subtract).then_inc(aq_lo_done, 1)

            def row_maxima(t, u):
                k = AH * t + u
                i = u % 2
                if not (isinstance(t, int) and t == 0 and u < 2):
                    dve.wait_ge(exp_done, k - 1)
                for b in range(3):
                    dve.wait_ge(sc_bank, 3 * k + b + 1)
                    dve.tensor_reduce(row_max[:, i, b:b + 1], ps[:, b, 0:min(W, KEYS - b * W)], AX.X, ALU.max).then_inc(max_bank, 1)
                dve.wait_ge(max_bank, 3 * k + 3)
                dve.tensor_reduce(row_max[:, i, 3:4], row_max[:, i, 0:3], AX.X, ALU.max).then_inc(max_all, 1)
                dve.wait_ge(max_all, k + 1)
                dve.scalar_tensor_tensor(out=neg_max[:, i:i + 1], in0=row_max[:, i, 3:4], scalar=-1.0, in1=rstd_of(t, u),
                                         op0=ALU.mult, op1=ALU.mult).then_inc(neg_done, 1)

            def inverse(t, u):
                k = AH * t + u
                i = u % 2
                dve.wait_ge(exp_done, k + 1)
                if not (isinstance(t, int) and t == 0 and u < 2):
                    dve.wait_ge(soft_done, k - 1)
                dve.reciprocal(row_inv[:, i:i + 1], row_sum[:, i:i + 1]).then_inc(inv_done, 1)

            def soft_lo_half(t, u):
                k = AH * t + u
                dve.wait_ge(soft_hi, k + 1)
                for b in range(3):
                    k0, k1 = piece(b)
                    hi, dst = (soft_t[u // 4][i][:, k0:k1, u % 4, :] for i in range(2))
                    dve.tensor_tensor(dst, ps[:, turn_bank(u, b), 0:(k1 - k0) * P].rearrange("p (k i) -> p k i", i=P), hi.bitcast(F32),
                                      ALU.subtract).then_inc(soft_lo, 1)

            def gate_out(t, g):
                dve.wait_ge(pv_done, 2 * t + g + 1)
                v = att_y[:, 4 * g:4 * g + 4, bass.ds(t * P, P)]
                dve.tensor_tensor(v, ps[:, 7, :].rearrange("p (h i) -> p h i", h=4), v, ALU.mult).then_inc(att_out, 1)

            def ada_gate(t):
                dve.wait_ge(ada_g_done, t + 1)
                dve.tensor_tensor(mod_col(t), ps[:, turn_bank(AH - 1, 0), 0:1], vec_cols[:, bass.ds(t + 24 + 2 * KT, 1)], ALU.add).then_inc(gate_col, 1)

            def tile(t):
                first = isinstance(t, int) and t == 0
                last = isinstance(t, int) and t == TT - 1
                if not first:
                    inverse(t - 1, AH - 1)
                dve.tensor_scalar(tile_rstd[:], rstd_q[:, bass.ds(t * AH, AH)], 1.0, None, ALU.mult).then_inc(tile_ready, 1)
                dve.wait_ge(tile_ready, t + 1)
                for u in range(AH):
                    if u > 0:
                        inverse(t, u - 1)
                    row_maxima(t, u)
                    if u == 2:
                        queries_lo(t, 1)
                    if u == 6 and not last:
                        queries_lo(t + 1, 0)
                    if u > 1:
                        soft_lo_half(t, u - 2)
                    elif not first:
                        soft_lo_half(t - 1, AH - 2 + u)
                    if u in (1, 5) and not first:
                        gate_out(t - 1, u // 4)
                    if u == 7:
                        ada_gate(t)

            queries_lo(0, 0)
            tile(0)
            dve.wait_ge(att_gate_in, 16)
            with dve.Fori(1, TT - 1) as t:
                tile(t)
            tile(TT - 1)
            inverse(TT - 1, AH - 1)
            soft_lo_half(TT - 1, AH - 2)
            soft_lo_half(TT - 1, AH - 1)
            gate_out(TT - 1, 0)

            def y_lo(half, i):
                dve.wait_ge(y_hi_done, 3 * KT * half + i + 1)
                dve.tensor_tensor(y_r(i, 1), y_raw[(i // 2) % 3][:, i % 2, :], y_r(i, 0).bitcast(F32),
                                  ALU.subtract).then_inc(y_lo_done, 1)

            def merge(half, n):
                k = KT * half + n
                dve.wait_ge(mg_in, 32 * k + 32)
                dve.wait_ge(ow_used, CHUNKS * half + 3 * n + 2)
                if not (half == 0 and isinstance(n, int)):
                    dve.wait_ge(z_lo_done, k)
                dve.tensor_tensor(merged[:, 0, :], ps[:, 0, :], merge_gate[:, 0, :], ALU.mult).then_inc(merged_part, 1)
                dve.wait_ge(ow_used, CHUNKS * half + 3 * n + 3)
                dve.tensor_tensor(merged[:, 1, :], ps[:, 1, :], merge_gate[:, 1, :], ALU.mult).then_inc(mg_used, 1)
                dve.wait_ge(mg_used, k + 1)
                dve.tensor_tensor(merged[:, 0, :], merged[:, 0, :], merged[:, 1, :], ALU.add).then_inc(merged_done, 1)
                dve.wait_ge(merged_done, k + 1)
                if isinstance(n, int):
                    if half:
                        dve.wait_ge(ow_used, CHUNKS)
                    else:
                        dve.wait_ge(att_stored, 16 * HALVES)
                dve.tensor_scalar(row_of(z_r[0], n), merged[:, 0, :], 1.0, None, ALU.mult).then_inc(z_hi_done, 1)
                dve.wait_ge(z_hi_done, k + 1)
                dve.tensor_tensor(row_of(z_r[1], n), merged[:, 0, :], row_of(z_r[0], n).bitcast(F32), ALU.subtract).then_inc(z_lo_done, 1)

            for half in range(HALVES):
                if half == 0:
                    for i in range(3 * KT):
                        if i == 6:
                            gate_out(TT - 1, 1)
                        y_lo(0, i)
                merge(half, 0)
                with dve.Fori(1, KT) as n:
                    merge(half, n)
                dve.wait_ge(res_in, 16 * half + 16)
                for n in range(KT):
                    if half == 0:
                        for i in range(3 * n, 3 * n + 3):
                            y_lo(1, i)
                    dve.wait_ge(out_turned, KT * half + n + 1)
                    v = res[:, :, n * P:(n + 1) * P]
                    dve.tensor_tensor(v, v, ps[:, 4 + n % 2, :].rearrange("p (t e) -> p t e", t=4), ALU.add).then_inc(out_added, 1)

        @block.tensor
        def _(pe):
            pe.wait_ge(ident_in_s, 16)
            pe.wait_ge(vec_silu, 1)
            pe.transpose(ps[:, 0, 0:48], vec_rows[:], ident[0:48, 0:48]).then_inc(vec_turned, 1)

            def turn(u):
                bank = unit_bank(u)
                pe.wait_ge(x_normed, TT + CT if u >= UNITS_X else 4 * (u // KT) + 4)
                before = [v for v in range(u) if unit_bank(v) == bank]
                if before:
                    pe.wait_ge(unit_modulated, before[-1] + 1)
                k = u % KT
                n = 4 if u < UNITS_X else CT
                for i in range(n):
                    src = xs[:, 4 * (u // KT) + i, k * P:(k + 1) * P] if u < UNITS_X else cs[:, i, k * P:(k + 1) * P]
                    ins = pe.transpose(ps[:, bank, i * P:(i + 1) * P], src, ident[:])
                ins.then_inc(unit_turned, 1)

            pe.wait_ge(vec_copied, 1)
            vecs = vec_cols[:, 0:2 * KT].rearrange("p (v k) -> p k v", k=KT)
            for n in range(4):
                pe.wait_ge(ada_in[n], 16)
                if n >= 2:
                    pe.wait_ge(rows_out, n - 1)
                for k in range(KT):
                    ins = pe.matmul(ps[0:2, n % 2, :], vecs[:, k, :], ada_block(n)[:, k, :], start=(k == 0), stop=(k == KT - 1))
                ins.then_inc(ada_used, 1)
            turn(0)
            turn(1)
            pe.wait_ge(rows_out, 4)
            for n in range(2 * KT):
                ins = pe.transpose(ps[:, 0, 2 * n:2 * n + 2], ada_rows[:, n * P:(n + 1) * P], ident[0:2, 0:2])
            ins.then_inc(ada_turned, 1)
            for u in range(2, KT):
                turn(u)

            def passes(out, stat, mov, stat_at, mov_at, n):
                for k in range(n):
                    for i, (s, m) in enumerate(((0, 0), (0, 1), (1, 0))):
                        ins = pe.matmul(out, stat_at(stat[s], k), mov_at(mov[m], k),
                                        start=(k == 0 and i == 0), stop=(k == n - 1 and i == 2))
                return ins

            def x_tile(n, j, bank, s, transposed):
                pe.wait_ge(tile_out, n - 3)
                wt = (w_hi[s], w_lo[s])
                if transposed:
                    col, half = j // 2, j % 2
                    ins = passes(ps[:, bank, :], wt, (hx_hi, hx_lo), lambda v, k: v[:, k, col * P:(col + 1) * P],
                                 lambda v, k: v[:, k, half * W:(half + 1) * W], KT)
                else:
                    ins = passes(ps[:, bank, :], (hx_hi, hx_lo), wt, lambda v, k: v[:, k, j * P:(j + 1) * P],
                                 lambda v, k: v[:, k, :], KT)
                ins.then_inc(tile_done, 1)

            def c_tile(n, j, bank, s):
                pe.wait_ge(tile_out, n - 3)
                passes(ps[:, bank, :], (hc_hi, hc_lo), (w_hi[s], w_lo[s]),
                       lambda v, k: v[:, k, (j - TT) * P:(j - TT + 1) * P], lambda v, k: v[:, k, :], KT).then_inc(tile_done, 1)

            wt = (w_hi[0], w_lo[0])
            units = iter(range(KT, UNITS))
            for j, n in enumerate((0, 4, 4, 0, 3, 3, 2, 0)):
                for _ in range(n):
                    turn(next(units))
                half, col = j // 4, j % 4
                if half == 0:
                    pe.wait_ge(first_split(w0_lo_done, w_lo_done, col), col % 3 + 1)
                if col == 0:
                    pe.wait_ge(unit_hi, KT * (half + 1))
                    pe.wait_ge(unit_lo_dve, KT // 2 * (half + 1))
                    pe.wait_ge(unit_lo_pool, KT // 2 * (half + 1))
                    if half == 0:
                        pe.wait_ge(ada_turned, 1)
                if j >= 5:
                    pe.wait_ge(tile_out, j - 4)
                passes(ps[:, j % 5, :], wt, (hx_hi, hx_lo), lambda v, k: v[:, k, col * P:(col + 1) * P],
                       lambda v, k: v[:, k, half * W:(half + 1) * W], KT).then_inc(tile_done, 1)
            pe.wait_ge(unit_hi, UNITS)
            pe.wait_ge(unit_lo_dve, UNITS // 2)
            pe.wait_ge(unit_lo_pool, UNITS // 2)
            for j in range(TT, TT + CT):
                c_tile(j, j, j % 5, 0)
            pe.wait_ge(w_lo_done, 2)
            for j in range(TT):
                x_tile(10 + j, j, j % 5, 1, True)
            for j in range(TT, TT + CT):
                c_tile(10 + j, j, j % 5, 1)

            def ctx_block(b, s):
                pe.wait_ge(w_lo_done, b + 1)
                for j in range(TT):
                    x_tile(10 * b + j, j, j % 5, s, False)
                for j in range(TT, TT + CT):
                    c_tile(10 * b + j, j, j % 5, s)

            def x_block(b, s, transposed):
                pe.wait_ge(w_lo_done, b + 1)
                for j in range(TT):
                    x_tile(8 * b + 14 + j, j, j % 4, s, transposed)

            with pe.Fori(B_RV, B_AKV, 2) as b:
                ctx_block(b, 0)
                ctx_block(b + 1, 1)
            ctx_block(B_AKV, 0)
            with pe.Fori(B_RQ, B_AQ, 2) as b:
                x_block(b, 1, True)
                x_block(b + 1, 0, True)
            x_block(B_AQ, 1, False)
            x_block(B_AQ + 1, 0, False)
            with pe.Fori(B_AG, NB, 2) as b:
                x_block(b, 1, True)
                x_block(b + 1, 0, True)

            def turn_keys(h, m, d):
                c = m - 1 if d == 0 else NCH - m
                pe.wait_ge(rk_in, 16 * h + 16)
                if d == 0:
                    pe.wait_ge(kd_lo_done[1], 4 * h + m)
                    if m == 1 and not (isinstance(h, int) and h == 0):
                        pe.wait_ge(y_out, 8 * h - 4)
                else:
                    pe.wait_ge(kd_lo_done[0], 4 * h + m + 1)
                for j in range(2):
                    for e in range(2):
                        at = c * CH + j * P
                        ins = pe.transpose(ps[:, 0, j * RDK + e * P:j * RDK + (e + 1) * P], rk_raw[:, e, at:at + P], ident[:])
                ins.then_inc(k_turned[d], 1)

            def delta(h, m, d):
                pe.wait_ge(kd_lo_done[d], 4 * h + m + 1)
                if m == 0:
                    pe.wait_ge(cv_lo_done, h + 1)
                    vals, v0 = cv, 0
                    if not (isinstance(h, int) and h == 0):
                        pe.wait_ge(cross_out[d], 4 * h)
                else:
                    vals, v0 = rv, 2 * (m - 1 if d == 0 else NCH - m)
                    pe.wait_ge(cross_out[d], 4 * h + m)
                for e in range(2):
                    ins = passes(ps[:, 2 + 2 * d + e, :], kd[d], vals, lambda v, k: v[:, k, e * P:(e + 1) * P],
                                 lambda v, k: v[:, v0 + k, :], 2)
                ins.then_inc(delta_done[d], 1)

            def scores(h, s):
                if s == 0:
                    pe.wait_ge(g03_lo_pool, 2 * h + 2)
                if s == 1:
                    pe.wait_ge(g12_lo_done, 3 * h + 2)
                    if not (isinstance(h, int) and h == 0):
                        pe.wait_ge(y_out, 8 * h)
                if not (isinstance(h, int) and h == 0 and s == 0):
                    pe.wait_ge(probs_done, 4 * h + s)
                at = s * CH
                for j in range(2):
                    ins = passes(ps[:, 1, j * CH:(j + 1) * CH], rk, rq, lambda v, k: v[:, k, at + j * P:at + (j + 1) * P],
                                 lambda v, k: v[:, k, at:at + CH], 2)
                ins.then_inc(scores_done, 1)

            def cross(h, s, d):
                c = s if d == 0 else NCH - 1 - s
                pe.wait_ge(state_lo_done[d], 4 * h + s + 1)
                for i in range(2):
                    at = c * CH + i * P
                    ins = passes(ps[:, 2 + 2 * d + i, :], rq, state_r[d], lambda v, k: v[:, k, at:at + P],
                                 lambda v, k: v[:, k, :], 2)
                ins.then_inc(cross_done[d], 1)

            def intra(h, s):
                pe.wait_ge(probs_lo_done, 4 * h + s + 1)
                if s == 0:
                    pe.wait_ge(g03_lo_dve, h + 1)
                    if not (isinstance(h, int) and h == 0):
                        pe.wait_ge(y_out, 8 * h - 2)
                else:
                    pe.wait_ge(intra_out, 4 * h + s)
                    if s == 1:
                        pe.wait_ge(g12_lo_done, 3 * h + 3)
                for i in range(2):
                    ins = passes(ps[:, 6 + i, :], probs_r, rv, lambda v, k: v[:, k, i * P:(i + 1) * P],
                                 lambda v, k: v[:, 2 * s + k, :], 2)
                ins.then_inc(intra_done, 1)

            def turn_o(h, g, e, last=False):
                bank = o_bank(g, e)
                pe.wait_ge(o_normed, 2 * h + g + 1)
                if g == 0 and e == 0:
                    pe.wait_ge(kd_lo_done[1], 4 * h + 4)
                elif g == 0:
                    pe.wait_ge(y_out, 8 * h + e)
                elif e < 2:
                    pe.wait_ge(intra_out, 4 * h + 4)
                elif e == 2:
                    pe.wait_ge(probs_done, 4 * h + (4 if last else 5))
                else:
                    pe.wait_ge(y_out, 8 * h + 7)
                for i, t in enumerate(O_GROUPS[g]):
                    ins = pe.transpose(ps[:, bank, i * P:(i + 1) * P], ret_o[:, t, e * P:(e + 1) * P], ident[:])
                ins.then_inc(o_turned, 1)

            def head(h, last):
                first = isinstance(h, int) and h == 0
                scores(h, 0)
                if not first:
                    turn_o(h - 1, 0, 2)
                cross(h, 0, 0)
                if not first:
                    turn_o(h - 1, 0, 3)
                    turn_o(h - 1, 1, 0)
                    turn_o(h - 1, 1, 1)
                turn_keys(h, 1, 0)
                cross(h, 0, 1)
                if not first:
                    turn_o(h - 1, 1, 2)
                turn_keys(h, 1, 1)
                if not first:
                    turn_o(h - 1, 1, 3)
                intra(h, 0)
                delta(h, 1, 0)
                delta(h, 1, 1)
                for s in range(1, NCH):
                    scores(h, s)
                    cross(h, s, 0)
                    if s < NCH - 1:
                        turn_keys(h, s + 1, 0)
                    cross(h, s, 1)
                    if s < NCH - 1:
                        turn_keys(h, s + 1, 1)
                    intra(h, s)
                    if s < NCH - 1:
                        delta(h, s + 1, 0)
                        delta(h, s + 1, 1)
                if last:
                    turn_att_keys(0)
                    for e in range(4):
                        turn_o(h, 0, e)
                    turn_att_keys(1)
                    for e in range(4):
                        turn_o(h, 1, e, True)
                else:
                    delta(h + 1, 0, 0)
                    turn_o(h, 0, 0)
                    delta(h + 1, 0, 1)
                    turn_o(h, 0, 1)

            def turn_att_keys(g):
                pe.wait_ge(keys_normed, g + 1)
                if g == 0:
                    for d in range(2):
                        pe.wait_ge(cross_out[d], 4 * RH)
                else:
                    pe.wait_ge(ak_lo_done, 1)
                for t in range(NKT):
                    ins = pe.transpose(bank_span(2, KEYS)[:, t * P:(t + 1) * P], kv_raw[:, t, g * AD:(g + 1) * AD], ident[:])
                ins.then_inc(ak_turned, 1)

            delta(0, 0, 1)
            pe.wait_ge(tile_out, 8 * NB + 14)
            delta(0, 0, 0)
            head(0, False)
            with pe.Fori(1, RH - 1) as h:
                head(h, False)
            head(RH - 1, True)

            def turn_queries(t, half):
                pe.wait_ge(aq_in[half], 16 * t + 16)
                if not (isinstance(t, int) and t == 0 and half == 0):
                    pe.wait_ge(aq_lo_done, 2 * t + half)
                if half == 0 and not (isinstance(t, int) and t == 0):
                    pe.wait_ge(sc_bank, 3 * (AH * t - 4))
                    pe.wait_ge(soft_lo, 3 * (AH * t - 3) - 3)
                if half == 1 and not (isinstance(t, int) and t == 0):
                    pe.wait_ge(soft_lo, 3 * (AH * t + 1) - 3)
                for h in range(4):
                    ins = pe.transpose(ps[:, 6, h * P:(h + 1) * P], aq_raw[:, half, h * AD:(h + 1) * AD], ident[:])
                ins.then_inc(aq_turned, 1)

            def att_scores(t, u):
                k = AH * t + u
                if not (isinstance(t, int) and t == 0 and u == 0):
                    pe.wait_ge(exp_done, k)
                if u == 0:
                    pe.wait_ge(aq_lo_done, 2 * t + 1)
                if u == 4:
                    pe.wait_ge(aq_lo_done, 2 * t + 2)
                for b in range(3):
                    n = min(W, KEYS - b * W)
                    passes(ps[:, b, 0:n], aq, ak, lambda v, k: v[:, u, :], lambda v, k: v[:, u // 4, b * W:b * W + n], 1).then_inc(sc_bank, 1)

            def turn_soft(t, u):
                k = AH * t + u
                pe.wait_ge(soft_done, k + 1)
                for j in range(NKT):
                    b = j // 4
                    if j % 4 == 0 and not (isinstance(t, int) and t == 0 and 3 * u + b < 4):
                        pe.wait_ge(soft_lo, 3 * k + b - 3)
                    if j == 0 and u == 1:
                        pe.wait_ge(aq_lo_done, 2 * t + 2)
                    if j == 0 and u == 5 and not (isinstance(t, int) and t == TT - 1):
                        pe.wait_ge(aq_lo_done, 2 * t + 3)
                    if j == 0 and u == AH - 1:
                        pe.wait_ge(gate_col, t + 1)
                    at = j % 4 * P
                    ins = pe.transpose(ps[:, turn_bank(u, b), at:at + P], soft[u % 2][:, j * P:(j + 1) * P], ident[:])
                ins.then_inc(soft_turned, 1)

            def values(t, g, part):
                if part == 0:
                    pe.wait_ge(av_lo_done, 1)
                    pe.wait_ge(soft_lo, 3 * (AH * t + 4 * g + 4))
                    if not (isinstance(t, int) and t == 0 and g == 0):
                        pe.wait_ge(att_out, 2 * t + g)
                k0, k1 = ((0, 3), (3, 6), (6, 8), (8, NKT))[part]
                for k in range(k0, k1):
                    for i, (a, b) in enumerate(((0, 0), (0, 1), (1, 0))):
                        ins = pe.matmul(ps[:, 7, :], av[a][:, k, g * AD:(g + 1) * AD],
                                        soft_t[g][b][:, k].rearrange("p h i -> p (h i)"),
                                        start=(k == 0 and i == 0), stop=(k == NKT - 1 and i == 2))
                if part == 3:
                    ins.then_inc(pv_done, 1)

            def tile(t):
                first = isinstance(t, int) and t == 0
                last = isinstance(t, int) and t == TT - 1
                for u in range(AH):
                    att_scores(t, u)
                    if u < 2 and not first:
                        values(t - 1, 0, u + 2)
                    elif 2 <= u <= 5 and not first:
                        values(t - 1, 1, u - 2)
                    elif u >= 6:
                        values(t, 0, u - 6)
                    if u > 0:
                        turn_soft(t, u - 1)
                    elif not first:
                        turn_soft(t - 1, AH - 1)
                    if u == 1:
                        turn_queries(t, 1)
                    if u == 5 and not last:
                        turn_queries(t + 1, 0)
                    if u == 7:
                        pe.wait_ge(ada_g_in, 16 * t + 16)
                        pe.wait_ge(soft_lo, 3 * (AH * t + 7) - 3)
                        for k in range(KT):
                            ins = pe.matmul(ps[:, turn_bank(AH - 1, 0), 0:1], ada_g[:, k, :], vec_cols[:, k:k + 1], start=(k == 0), stop=(k == KT - 1))
                        ins.then_inc(ada_g_done, 1)

            pe.wait_ge(y_out, 8 * RH)
            turn_queries(0, 0)
            pe.wait_ge(ak_lo_done, AKV)
            tile(0)
            with pe.Fori(1, TT - 1) as t:
                tile(t)
            tile(TT - 1)
            values(TT - 1, 0, 2)
            turn_soft(TT - 1, AH - 1)
            values(TT - 1, 0, 3)
            for part in range(4):
                values(TT - 1, 1, part)

            def chunk_ready(half, c):
                pe.wait_ge(ow_lo_done, CHUNKS * half + c + 1)

            def branch_tile(half, n, first):
                k = KT * half + n
                for i in range(3):
                    chunk_ready(half, 3 * n + i)
                    bank = 0 if i < 2 else 1
                    if i == 0:
                        if half == 0 and first:
                            pe.wait_ge(exp_done, TT * AH)
                        else:
                            pe.wait_ge(merged_part, k)
                    if i == 2 and not (half == 0 and first):
                        pe.wait_ge(mg_used, k)
                    for j in range(KT):
                        if first:
                            pe.wait_ge(y_lo_done, 3 * KT * half + KT * i + j + 1)
                        for q, (a, b) in enumerate(((0, 0), (0, 1), (1, 0))):
                            ins = pe.matmul(ps[:, bank, :], ow[i][a][:, j, :], y_r(KT * i + j, b),
                                            start=(i != 1 and j == 0 and q == 0), stop=(i != 0 and j == KT - 1 and q == 2))
                    ins.then_inc(ow_used, 1)

            def out_tile(half, n):
                k = KT * half + n
                c = 3 * KT + n
                chunk_ready(half, c)
                if n == 0:
                    pe.wait_ge(z_lo_done, KT * half + KT)
                if k >= 2:
                    pe.wait_ge(out_gated, k - 1)
                for j in range(KT):
                    for q, (a, b) in enumerate(((0, 0), (0, 1), (1, 0))):
                        ins = pe.matmul(ps[:, 2 + n % 2, :], ow[c % 3][a][:, j, :], z_r[b][:, j, :],
                                        start=(j == 0 and q == 0), stop=(j == KT - 1 and q == 2))
                ins.then_inc(ow_used, 1)

            def turn_out(half, n):
                k = KT * half + n
                pe.wait_ge(out_gated, k + 1)
                if k >= 2:
                    pe.wait_ge(out_added, k - 1)
                for j in range(4):
                    ins = pe.transpose(ps[:, 4 + n % 2, j * P:(j + 1) * P], out_t[:, n % 2, j * P:(j + 1) * P], ident[:])
                ins.then_inc(out_turned, 1)

            for half in range(HALVES):
                branch_tile(half, 0, True)
                with pe.Fori(1, KT) as n:
                    branch_tile(half, n, False)
                for n in range(KT):
                    out_tile(half, n)
                    if n:
                        turn_out(half, n - 1)
                turn_out(half, KT - 1)


NORM_GROUPS = ((0, 4), (4, 10))
LN2 = float(np.log(2.0))


_INS = ["x", "c", "ctx", "c_ctx", "norm_w", "w_ada", "b_ada", "w_in", "ret_log2_decay",
        "q_norm_w", "k_norm_w", "w_o_ret", "w_o_att", "w_out"]


def kernel(**inputs):
    import concourse.bacc as bacc
    from concourse.bass_utils import run_bass_kernel_spmd

    nc = bacc.Bacc("TRN2", target_bir_lowering=False, num_devices=1)
    arrays, args = {}, []
    values = {name: np.ascontiguousarray(inputs[name]) for name in _INS}
    values.update(shape_constants())
    for name, a in values.items():
        arrays[f"{name}_dram"] = a
        args.append(nc.dram_tensor(f"{name}_dram", a.shape, mybir.dt.from_np(a.dtype), kind="ExternalInput").ap())
    out = nc.dram_tensor("out_dram", (1, SEQ, D), F32, kind="ExternalOutput").ap()
    build_program(nc, *args, out)
    r = run_bass_kernel_spmd(nc, [arrays], core_ids=[0])
    return r.results[0]["out_dram"]
```

```python
from contextlib import ExitStack

import numpy as np

import concourse.bass as bass
from concourse import mybir
from concourse.alu_op_type import AluOpType as ALU

F32 = mybir.dt.float32
F32R = mybir.dt.float32r
ACT = mybir.ActivationFunctionType
AX = mybir.AxisListType

P = 128
D = 1024
SEQ = 1024
CTX = 256
GRID_W = 64
KT = D // P
TT = SEQ // P
CT = CTX // P
RH, RDK, RDV = 4, 256, 512
AH, AKV, AD = 8, 2, 128
EPS = 1e-6
ROPE_THETA = 10000.0
W = 512
CH = 256
NCH = SEQ // CH

B_RK, B_RV, B_AKV, B_RQ, B_RG, B_AQ, B_AG, B_MR, B_MA = 0, 2, 6, 7, 9, 13, 15, 17, 19
NB = 21
CTX_BLOCKS = 7


def shape_constants():
    half = AD // 2
    rows = np.repeat(np.arange(SEQ // GRID_W, dtype=np.float32), GRID_W)
    cols = np.tile(np.arange(GRID_W, dtype=np.float32), SEQ // GRID_W)
    freqs = (np.float32(ROPE_THETA) ** (-np.arange(0, half, 2, dtype=np.float32) / np.float32(half))).astype(np.float32)
    ang = np.concatenate([rows[:, None] * freqs, cols[:, None] * freqs], axis=-1).astype(np.float32)
    rope = np.stack([np.cos(ang), np.sin(ang)]).astype(np.float32)
    p = np.arange(P, dtype=np.float32)
    exps = [p + 1, p + 129, 255 - p, 127 - p, p * 0 + 256, 256 - p, 128 - p, p, p + 128, p * 0 + 256]
    j = p[:, None, None] + P * np.arange(2, dtype=np.float32)[None, :, None]
    i = np.arange(CH, dtype=np.float32)[None, None, :]
    d = i - j
    rel = np.stack([np.maximum(d, 0), np.maximum(-d, 0), d >= 0, d <= 0], axis=1).reshape(P, 4, 2 * CH)
    return {"ident_in": np.eye(P, dtype=np.float32), "rope_in": rope,
            "decay_exp_in": np.stack(exps, axis=1).astype(np.float32), "rel_in": rel.astype(np.float32)}


def build_program(nc, x, c, ctx, c_ctx, norm_w, w_ada, b_ada, w_in, ret_log2_decay,
                  q_norm_w, k_norm_w, w_o_ret, w_o_att, w_out,
                  ident_in, rope_in, decay_exp_in, rel_in, out):
    with ExitStack() as held:
        def sem(name):
            return held.enter_context(nc.semaphore(name))

        def sb(stack, name, shape, dt=F32):
            return stack.enter_context(nc.sbuf_tensor(name, shape, dt))

        def scratch(name, shape):
            return nc.dram_tensor(name, shape, F32, kind="Internal").ap()

        proj_x = scratch("proj_x", (NB, 4, P, 2 * W))
        proj_c = scratch("proj_c", (CTX_BLOCKS, P, CT * W))

        ident = sb(held, "ident", [P, P])
        vec_cols = sb(held, "vec_cols", [P, 48])
        mod = sb(held, "mod", [P, 3 * KT, 2])
        log_gamma = sb(held, "log_gamma", [P, 2 * RH])
        decay = sb(held, "decay", [P, RH * 10])
        head_decay = sb(held, "head_decay", [P, 10])
        ones = sb(held, "ones", [P, 1])
        head_gamma = sb(held, "head_gamma", [P, 2])
        kd_decay = sb(held, "kd_decay", [P, 2, 2])
        tile_rstd = sb(held, "tile_rstd", [P, AH])
        ssq_q = sb(held, "ssq_q", [P, TT, AH])
        ssq_k = sb(held, "ssq_k", [P, TT + CT, AKV])
        ps = held.enter_context(nc.psum_tensor("ps", [P, 8, W], F32))

        proj_mem = held.enter_context(ExitStack())
        hx_hi = sb(proj_mem, "hx_hi", [P, KT, SEQ], F32R)
        hx_lo = sb(proj_mem, "hx_lo", [P, KT, SEQ], F32R)
        hc_hi = sb(proj_mem, "hc_hi", [P, KT, CTX], F32R)
        hc_lo = sb(proj_mem, "hc_lo", [P, KT, CTX], F32R)
        with ExitStack() as m:
            ada_rows = sb(m, "ada_rows", [2, 2 * D])
        stage = sb(proj_mem, "stage", [P, 2, 2 * W])

        def weight_halves(s):
            return [sb(proj_mem, f"w{s}_{x}", [P, KT, W], F32R) for x in ("hi", "lo")]

        w_raw = [sb(proj_mem, "w_raw0", [P, KT, W])]
        with ExitStack() as m:
            ada_1_2 = sb(m, "ada_1_2", [P, 2, KT, W])
        halves_0 = weight_halves(0)
        with ExitStack() as m:
            xs = sb(m, "xs", [P, TT, D])
            ada_0_3 = sb(m, "ada_0_3", [P, KT, W])
            cs = sb(m, "cs", [P, CT, D])
            modulated = sb(m, "modulated", [P, 2, W])
            vec_rows = sb(m, "vec_rows", [48, P])
            ssq_x = sb(m, "ssq_x", [P, TT + CT])
            rms_x = sb(m, "rms_x", [P, TT + CT])
            rstd_x = sb(m, "rstd_x", [P, TT + CT])
            a_col = sb(m, "a_col", [P, KT, 2])
            square_junk = sb(m, "square_junk", [P, D])
            log2_decay = sb(m, "log2_decay", [P, 2 * RH])
            lg = sb(m, "lg", [P, 8, 2 * RH])
            decay_exp = sb(m, "decay_exp", [P, 10])
        w_raw.append(sb(proj_mem, "w_raw1", [P, KT, W]))
        w_hi, w_lo = zip(halves_0, weight_halves(1))
        stage_c = sb(proj_mem, "stage_c", [P, CT, W])
        heads_in = sb(proj_mem, "heads_in", [P, 2, W])
        heads_w = sb(proj_mem, "heads_w", [P, W])
        rope_t = sb(proj_mem, "rope_t", [P, W])
        rope_cs = sb(proj_mem, "rope_cs", [P, 2, TT, AD // 2])
        qk_norm = sb(proj_mem, "qk_norm", [P, 2, AD])
        head_junk = sb(proj_mem, "head_junk", [P, 4, AD])
        proj_mem.close()

        y_ret = scratch("y_ret", (RH * 4, P, SEQ))
        with ExitStack() as m:
            rv = [sb(m, f"rv_{x}", [P, TT, RDV], F32R) for x in ("hi", "lo")]
            ret_o = sb(m, "ret_o", [P, TT, RDV])
            gate_y = sb(m, "gate_y", [P, 4, SEQ])
            rk = [sb(m, f"rk_{x}", [P, 2, SEQ], F32R) for x in ("hi", "lo")]
            probs = sb(m, "probs", [P, 2 * CH])
            probs_r = [sb(m, f"probs_{x}", [P, 2, CH], F32R) for x in ("hi", "lo")]
            ret_junk = sb(m, "ret_junk", [P, RDV])
            rq = [sb(m, f"rq_{x}", [P, 2, SEQ], F32R) for x in ("hi", "lo")]
            state = [sb(m, f"state{d}", [P, 2, RDV]) for d in range(2)]
            state_r = [[sb(m, f"state{d}_{x}", [P, 2, RDV], F32R) for x in ("hi", "lo")] for d in range(2)]
            sb(m, "ret_spare", [P, 2 * SEQ])
            rq_raw = sb(m, "rq_raw", [P, 2, SEQ])
            rv_raw = sb(m, "rv_raw", [P, TT, RDV])
            rk_raw = sb(m, "rk_raw", [P, 2, SEQ])
            ck_raw = sb(m, "ck_raw", [P, CT, RDK])
            cv_raw = sb(m, "cv_raw", [P, CT, RDV])
            cv = [sb(m, f"cv_{x}", [P, CT, RDV], F32R) for x in ("hi", "lo")]
            rel = sb(m, "rel", [P, 4, 2 * CH])
            kd = [[sb(m, f"kd{d}_{x}", [P, 2, RDK], F32R) for x in ("hi", "lo")] for d in range(2)]
            mask = sb(m, "mask", [P, 2 * CH])
            mask_b = sb(m, "mask_b", [P, 2 * CH])
            ret_ms = sb(m, "ret_ms", [P, 3, TT])

        y_att = scratch("y_att", (AH, P, W))
        KEYS = SEQ + CTX
        NKT = KEYS // P
        with ExitStack() as m:
            soft_t = [[sb(m, f"soft_t{g}_{x}", [P, NKT, 4, P], F32R) for x in ("hi", "lo")] for g in range(AKV)]
            att_y = sb(m, "att_y", [P, AH, SEQ])
            soft = [sb(m, f"soft{i}", [P, KEYS]) for i in range(2)]
            aq = [sb(m, f"aq_{x}", [P, AH, P], F32R) for x in ("hi", "lo")]
            ada_g = sb(m, "ada_g", [P, KT, P])
            rms_q = sb(m, "rms_q", [P, TT * AH])
            rstd_q = sb(m, "rstd_q", [P, TT * AH])
            rms_k = sb(m, "rms_k", [P, NKT * AKV])
            rstd_k = sb(m, "rstd_k", [P, NKT * AKV])
            row_max = sb(m, "row_max", [P, 2, 4])
            neg_max = sb(m, "neg_max", [P, 2])
            row_sum = sb(m, "row_sum", [P, 2])
            row_inv = sb(m, "row_inv", [P, 2])
            kv_raw = sb(m, "kv_raw", [P, NKT, W])
            aq_raw = sb(m, "aq_raw", [P, 2, W])
            av = [sb(m, f"av_{x}", [P, NKT, AKV * AD], F32R) for x in ("hi", "lo")]
            ak = [sb(m, f"ak_{x}", [P, AKV, KEYS], F32R) for x in ("hi", "lo")]

        with ExitStack() as m:
            y_ret_r = sb(m, "y_ret_r", [P, 2 * KT, 2, W], F32R)
            res = sb(m, "res", [P, 4, D])
            z_r = [sb(m, f"z_{x}", [P, KT, W], F32R) for x in ("hi", "lo")]
            ow = [[sb(m, f"ow{i}_{x}", [P, KT, P], F32R) for x in ("hi", "lo")] for i in range(2)]
            y_raw_2 = sb(m, "y_raw2", [P, 2, W])
            merged = sb(m, "merged", [P, 2, W])
            y_raw = [sb(m, f"y_raw{i}", [P, 2, W]) for i in range(2)] + [y_raw_2]
            ow_raw = [sb(m, f"ow_raw{i}", [P, KT, P]) for i in range(3)]
            ow.append([sb(m, f"ow2_{x}", [P, KT, P], F32R) for x in ("hi", "lo")])
            y_att_r = sb(m, "y_att_r", [P, KT, 2, W], F32R)
            merge_gate = sb(m, "merge_gate", [P, 2, W])
            out_t = sb(m, "out_t", [P, 2, W])

        def y_r(i, part):
            return y_ret_r[:, i, part, :] if i < 2 * KT else y_att_r[:, i - 2 * KT, part, :]

        def y_pair(half, i):
            return KT * half + i // 2

        def y_whole(half, i):
            if half == 0 and i >= 2 * KT:
                return att_y[:, i - 2 * KT, 0:W]
            return y_raw[y_pair(half, i) % 3][:, i % 2, :]

        ident_in_s, vec_in, small_in, ctx_in = sem("ident_in"), sem("vec_in"), sem("small_in"), sem("ctx_in")
        x_in = [sem(f"x_in{i}") for i in range(4)]
        ada_in = [sem(f"ada_in{i}") for i in range(4)]
        w_in_s = [sem(f"w_in{i}") for i in range(2)]
        vec_silu, vec_turned, vec_copied = sem("vec_silu"), sem("vec_turned"), sem("vec_copied")
        x_squared, ms_done, rms_done, x_normed = sem("x_squared"), sem("ms_done"), sem("rms_done"), sem("x_normed")
        ada_part_in = sem("ada_part_in")
        ones_set, gate_step = sem("ones_set"), sem("gate_step")
        ada_used, rows_out, ada_turned = sem("ada_used"), sem("rows_out"), sem("ada_turned")
        unit_turned, unit_modulated, unit_hi = sem("unit_turned"), sem("unit_modulated"), sem("unit_hi")
        unit_lo_pool, unit_lo_dve = sem("unit_lo_pool"), sem("unit_lo_dve")
        dve_step, lg_act, lg_dve, decay_done = sem("dve_step"), sem("lg_act"), sem("lg_dve"), sem("decay_done")
        w_hi_done, w_lo_done = sem("w_hi_done"), sem("w_lo_done")
        part_hi_done, part_lo_done = sem("part_hi_done"), sem("part_lo_done")
        tile_done, tile_out = sem("tile_done"), sem("tile_out")
        heads_squared, heads_roped = sem("heads_squared"), sem("heads_roped")
        stored = [sem(f"stored{i}") for i in range(2)]
        stored_c = sem("stored_c")

        rel_in_s, ck_in, cv_in, rk_in, rq_in, rv_in, gate_in = (
            sem(n) for n in ("rel_in", "ck_in", "cv_in", "rk_in", "rq_in", "rv_in", "gate_in"))
        head_ready, kd_ready = sem("head_ready"), sem("kd_ready")
        cv_hi_done, cv_lo_done, g03_hi_done, g03_lo_pool, g03_lo_values, g12_hi_done, g12_lo_done = (
            sem(n) for n in ("cv_hi", "cv_lo", "g03_hi", "g03_lo_pool", "g03_lo_values", "g12_hi", "g12_lo"))
        k_turned, kd_hi_done, kd_lo_done = ([sem(f"{n}{d}") for d in range(2)] for n in ("k_turned", "kd_hi", "kd_lo"))
        delta_done, state_done, state_hi_done, state_lo_done, cross_done, cross_out = (
            [sem(f"{n}{d}") for d in range(2)]
            for n in ("delta_done", "state_done", "state_hi", "state_lo", "cross_done", "cross_out"))
        scores_done, probs_done, probs_hi_done, probs_lo_done, intra_done, intra_out = (
            sem(n) for n in ("scores_done", "probs_done", "probs_hi", "probs_lo", "intra_done", "intra_out"))
        mask_exp, mask_done = sem("mask_exp"), sem("mask_done")
        o_squared, o_ms, o_rms, o_rstd, o_normed, o_turned, y_out, y_stored = (
            sem(n) for n in ("o_squared", "o_ms", "o_rms", "o_rstd", "o_normed", "o_turned", "y_out", "y_stored"))

        PAIRS = ((0, 3), (1, 2))

        def both(v, pair):
            a, e = pair
            return v[:, a:e + 1:e - a]

        def chunks_of(v):
            return v.rearrange("p d (c i) -> p c d i", c=NCH)

        def v_chunks(v):
            return v.rearrange("p (c t) e -> p c (t e)", c=NCH)

        tile_ready = sem("tile_ready")
        kv_in, att_gate_in, ada_g_in = sem("kv_in"), sem("att_gate_in"), sem("ada_g_in")
        aq_in = [sem(f"aq_in{i}") for i in range(2)]
        ms_qk, rms_qk, rstd_qk, keys_normed, ak_turned, ak_hi_done, ak_lo_done, av_hi_done, av_lo_done = (
            sem(n) for n in ("ms_qk", "rms_qk", "rstd_qk", "keys_normed", "ak_turned", "ak_hi", "ak_lo", "av_hi", "av_lo"))
        aq_turned, aq_hi_done, aq_lo_done = sem("aq_turned"), sem("aq_hi"), sem("aq_lo")
        sc_bank, max_bank, max_all, neg_done, exp_done, inv_done, soft_done, soft_turned, soft_hi, soft_lo = (
            sem(n) for n in ("sc_bank", "max_bank", "max_all", "neg_done", "exp_done", "inv_done", "soft_done",
                             "soft_turned", "soft_hi", "soft_lo"))
        pv_done, att_out, att_stored, ada_g_done, gate_col = (
            sem(n) for n in ("pv_done", "att_out", "att_stored", "ada_g_done", "gate_col"))
        y_in = [sem(f"y_in{i}") for i in range(3)]
        ow_in = [sem(f"ow_in{i}") for i in range(3)]
        y_hi_done, y_lo_done, ow_hi_done, ow_lo_done, ow_used = (
            sem(n) for n in ("y_hi_done", "y_lo_done", "ow_hi_done", "ow_lo_done", "ow_used"))
        mg_in, mg_used, merged_part, merged_done, z_hi_done, z_lo_done = (
            sem(n) for n in ("mg_in", "mg_used", "merged_part", "merged_done", "z_hi", "z_lo"))
        res_in, out_gated, out_turned, out_added, out_stored = (
            sem(n) for n in ("res_in", "out_gated", "out_turned", "out_added", "out_stored"))

        HALVES = SEQ // W
        CHUNKS = 4 * KT

        SLOT_USES = (11, 11, 10)

        def bank_span(b, n):
            return ps[:, b:b + 3, :].rearrange("p b n -> p (b n)")[:, 0:n]

        def turn_bank(u, b):
            return 3 + (3 * u + b) % 4

        def queries_bank(t, half):
            return 2 if isinstance(t, int) and t == 0 and half == 0 else 6

        def piece(b):
            return 4 * b, min(4 * b + 4, NKT)

        def rstd_of(t, u):
            return tile_rstd[:, u:u + 1]

        def mod_col(t):
            return mod[:, bass.ds(t + 2 * KT, 1), 0:1].rearrange("p o v -> p (o v)")

        def row_of(v, n):
            return v[:, bass.ds(n, 1), :].rearrange("p o i -> p (o i)")

        def o_bank(h, g, e):
            if isinstance(h, int) and h == RH - 1:
                return ((3, 4, 5, 6), (7, 3, 4, 5))[g][e]
            return ((0, 6, 7, 1), (1, 0, 1, 0))[g][e]

        KEY_PIECES = 3 * AKV
        KEY_BANKS = (0, 0, 0, 2, 3, 0)

        O_GROUPS = ((2, 3, 4, 5), (6, 7, 0, 1))

        def decay_at(h, i):
            return head_decay[:, i:i + 1]

        UNITS_X, UNITS = 2 * KT, 3 * KT

        def unit_bank(u):
            if u < KT:
                return 2 + u % 6
            return 4 + u % 4 if u < UNITS_X else 5 + (u - UNITS_X) % 3

        def ada_block(n):
            return ada_0_3[:] if n % 3 == 0 else ada_1_2[:, n - 1]

        def unit_target(u):
            if u < UNITS_X:
                at = slice((u // KT) * W, (u // KT + 1) * W)
                return hx_hi[:, u % KT, at], hx_lo[:, u % KT, at]
            return hc_hi[:, u % KT, :], hc_lo[:, u % KT, :]

        def first_count(b, c):
            return 3 * b + c + 1 if c < 3 else b + 1

        class Steps:

            def __init__(self, eng, sem, start=0):
                self.eng, self.sem, self.n = eng, sem, start

            def then(self, ins):
                self.n = self.n + 1
                ins.then_inc(self.sem, 1)
                self.eng.wait_ge(self.sem, self.n)

        def first_split(done_3, done_all, c):
            return done_3 if c < 3 else done_all

        def unit_hi_half(act, u):
            n = W if u < UNITS_X else CTX
            act.wait_ge(unit_modulated, u + 1)
            act.copy(unit_target(u)[0], modulated[:, u % 2, 0:n]).then_inc(unit_hi, 1)

        block = held.enter_context(nc.Block())

        @block.sync
        def _(sp):
            sp.dma_start(ident[:], ident_in).then_inc(ident_in_s, 16)
            sp.dma_start(vec_rows[0:8, :], c.rearrange("o (k p) -> (o k) p", p=P)).then_inc(vec_in, 16)
            sp.dma_start(vec_rows[8:16, :], c_ctx.rearrange("(k p) -> k p", p=P)).then_inc(vec_in, 16)
            sp.dma_start(vec_rows[16:24, :], norm_w.rearrange("o (k p) -> (o k) p", p=P)).then_inc(vec_in, 16)
            sp.dma_start(vec_rows[24:48, :], b_ada.rearrange("o (k p) -> (o k) p", p=P)).then_inc(vec_in, 16)
            x_tiles = x[0].rearrange("(t p) d -> p t d", p=P)
            ada_tiles = w_ada[0].rearrange("(k p) n -> p k n", p=P)
            w_tiles = w_in[0].rearrange("(k p) n -> p k n", p=P)

            def load_ada(n):
                if n == 0:
                    h = KT // 2
                    sp.dma_start(ada_block(0)[:, 0:h, :], ada_tiles[:, 0:h, 0:W]).then_inc(ada_part_in, 16)
                    sp.dma_start(ada_block(0)[:, h:KT, :], ada_tiles[:, h:KT, 0:W]).then_inc(ada_in[0], 16)
                    return
                if n == 3:
                    sp.wait_ge(ada_used, 1)
                sp.dma_start(ada_block(n), ada_tiles[:, :, n * W:(n + 1) * W]).then_inc(ada_in[n], 16)

            def load_x(i):
                sp.dma_start(xs[:, 2 * i:2 * i + 2, :], x_tiles[:, 2 * i:2 * i + 2, :]).then_inc(x_in[i], 16)

            def load_weights(b, s):
                sp.dma_start(w_raw[s][:], w_tiles[:, :, bass.ds(b * W, W)]).then_inc(w_in_s[s], 16)

            load_ada(0)
            load_ada(1)
            load_ada(2)
            load_ada(3)
            load_x(0)
            load_x(1)
            load_weights(0, 0)
            load_x(2)
            load_x(3)
            sp.dma_start(cs[:], ctx[0].rearrange("(t p) d -> p t d", p=P)).then_inc(ctx_in, 16)

            def store_first(g):
                sp.wait_ge(tile_out, 2 * g + 2)
                sp.dma_start(proj_x[0, 2 * (g % 2):2 * (g % 2) + 2, :, (g // 2) * W:(g // 2 + 1) * W].rearrange("c p n -> p c n"),
                             stage[:, g % 2, :].rearrange("p (c n) -> p c n", c=2)).then_inc(stored[g % 2], 16)

            store_first(0)
            store_first(1)
            sp.wait_ge(unit_lo_pool, UNITS // 2)
            sp.wait_ge(unit_lo_dve, UNITS // 2)
            sp.wait_ge(unit_hi, UNITS)
            sp.wait_ge(decay_done, 8)
            load_weights(1, 1)
            rope_src = rope_in.rearrange("s (t p) e -> s p t e", p=P)
            for i in range(2):
                sp.dma_start(rope_cs[:, i], rope_src[i]).then_inc(small_in, 16)
                sp.dma_start(qk_norm[:, i, :], (q_norm_w if i == 0 else k_norm_w).partition_broadcast(P)
                             .rearrange("p o d -> p (o d)")).then_inc(small_in, 16)
            sp.wait_ge(part_hi_done, 3)
            sp.wait_ge(part_lo_done, 3)
            sp.wait_ge(w_lo_done, 1)
            load_weights(2, 0)
            store_first(2)
            store_first(3)
            sp.wait_ge(tile_out, 10)
            sp.dma_start(proj_c[0], stage_c[:].rearrange("p t n -> p (t n)")).then_inc(stored_c, 16)

            def project(b, s, more, kind):
                if more:
                    if isinstance(b, int) and b == 1:
                        sp.wait_ge(part_hi_done, 6)
                        sp.wait_ge(part_lo_done, 6)
                    sp.wait_ge(w_hi_done, b + 1)
                    sp.wait_ge(w_lo_done, b + 1)
                    load_weights(b + 2, s)
                for g in range(4):
                    if kind in ("akv", "aq"):
                        base = 0 if kind == "akv" else TT + CT + (b - B_AQ) * TT
                        sp.wait_ge(heads_roped, base + 2 * g + 2)
                    else:
                        n0 = 10 * b if kind in ("rk", "rv") else 10 * CTX_BLOCKS + 8 * (b - CTX_BLOCKS)
                        sp.wait_ge(tile_out, n0 + 2 * g + 2)
                    sp.dma_start(proj_x[b, g], stage[:, g % 2, :]).then_inc(stored[g % 2], 16)
                if kind in ("rk", "rv", "akv"):
                    if kind == "akv":
                        sp.wait_ge(heads_roped, TT + CT)
                    else:
                        sp.wait_ge(tile_out, 10 * b + 10)
                    sp.dma_start(proj_c[b], stage_c[:].rearrange("p t n -> p (t n)")).then_inc(stored_c, 16)

            project(1, 1, True, "rk")
            with sp.Fori(B_RV, B_AKV, 2) as b:
                project(b, 0, True, "rv")
                project(b + 1, 1, True, "rv")
            project(B_AKV, 0, True, "akv")
            with sp.Fori(B_RQ, B_AQ, 2) as b:
                project(b, 1, True, "t")
                project(b + 1, 0, True, "t")
            project(B_AQ, 1, True, "aq")
            project(B_AQ + 1, 0, True, "aq")
            with sp.Fori(B_AG, NB - 3, 2) as b:
                project(b, 1, True, "t")
                project(b + 1, 0, True, "t")
            project(NB - 2, 1, False, "t")

            groups = proj_x.rearrange("b g p n -> (b g) p n")

            def load_head(h, first):
                pair, at = (h // 2, h % 2 * RDK) if isinstance(h, int) else (sp.snap(h // 2), sp.snap(h % 2 * RDK))
                k_at, v_at, q_at = 4 * B_RK + 2 * h, 4 * B_RV + 4 * h, 4 * B_RQ + 2 * h
                if not first:
                    sp.wait_ge(g03_lo_pool, 2 * h)
                    sp.wait_ge(kd_lo_done[0], 4 * h - 3)
                    sp.wait_ge(kd_lo_done[1], 4 * h - 3)
                sp.dma_start(ck_raw[:], proj_c[bass.ds(pair, 1)].rearrange("b p (t n) -> p (b t) n", t=CT)
                             [:, :, bass.ds(at, RDK)]).then_inc(ck_in, 16)
                if not first:
                    sp.wait_ge(cv_lo_done, h)
                sp.dma_start(cv_raw[:], proj_c[B_RV + h].rearrange("p (t n) -> p t n", t=CT)).then_inc(cv_in, 16)
                if not first:
                    sp.wait_ge(g12_lo_done, 3 * h)
                    sp.wait_ge(g03_lo_values, h)
                    sp.wait_ge(k_turned[0], 3 * h)
                    sp.wait_ge(k_turned[1], 3 * h)
                sp.dma_start(rk_raw[:], groups[bass.ds(k_at, 2)].rearrange("g p n -> p g n")).then_inc(rk_in, 16)
                sp.dma_start(rv_raw[:], groups[bass.ds(v_at, 4)].rearrange("g p (t e) -> p g t e", t=2)).then_inc(rv_in, 16)
                sp.dma_start(rq_raw[:], groups[bass.ds(q_at, 2)].rearrange("g p n -> p g n")).then_inc(rq_in, 16)

            def load_gate(h):
                sp.dma_start(gate_y[:], groups[bass.ds(4 * B_RG + 4 * h, 4)].rearrange("g p n -> p g n")).then_inc(gate_in, 16)

            def store_y(h):
                sp.wait_ge(y_out, 8 * h + 8)
                sp.dma_start(y_ret[bass.ds(4 * h, 4)].rearrange("g p n -> p g n"), gate_y[:]).then_inc(y_stored, 16)
                sp.wait_ge(y_stored, 16 * h + 16)

            for s in range(2):
                sp.wait_ge(stored[s], 16 * 2 * (NB - 1))
            sp.wait_ge(stored_c, 16 * CTX_BLOCKS)
            sp.wait_ge(heads_roped, TT + CT + 2 * TT)
            sp.wait_ge(w_hi_done, NB - 1)
            sp.wait_ge(w_lo_done, NB - 1)
            sp.wait_ge(tile_done, 8 * (NB - 1) + 14)
            sp.dma_start(rel[:], rel_in).then_inc(rel_in_s, 16)
            load_head(0, True)
            project(NB - 1, 0, False, "t")
            load_gate(0)
            for s in range(2):
                sp.wait_ge(stored[s], 16 * 2 * NB)
            with sp.Fori(1, RH) as h:
                load_head(h, False)
                store_y(h - 1)
                load_gate(h)
            sp.wait_ge(g12_lo_done, 3 * RH)
            sp.wait_ge(g03_lo_pool, 2 * RH)
            sp.wait_ge(g03_lo_values, RH)
            for i, src in ((0, groups[4 * B_AKV:4 * B_AKV + 4].rearrange("g p n -> p g n")), (TT, proj_c[B_AKV])):
                n = TT if i == 0 else CT
                dst = kv_raw[:, i:i + n, :].rearrange("p t n -> p (t n)")
                if i == 0:
                    dst = dst.rearrange("p (g n) -> p g n", g=4)
                sp.dma_start(dst, src).then_inc(kv_in, 16)

            def load_queries(t, half):
                pair, at = (t // 2, t % 2 * W) if isinstance(t, int) else (sp.snap(t // 2), sp.snap(t % 2 * W))
                if not (isinstance(t, int) and t == 0):
                    sp.wait_ge(aq_turned, 2 * t - 1 + half)
                row = groups[bass.ds(pair + 4 * (B_AQ + half), 1)].rearrange("g p n -> (g p) n")
                sp.dma_start(aq_raw[:, half, :], row[:, bass.ds(at, W)]).then_inc(aq_in[half], 16)

            def load_ada_gate(t):
                if not (isinstance(t, int) and t == 0):
                    sp.wait_ge(ada_g_done, t)
                sp.dma_start(ada_g[:], ada_tiles[:, :, bass.ds((t + 2 * KT) * P, P)]).then_inc(ada_g_in, 16)

            load_queries(0, 0)
            load_queries(0, 1)
            load_ada_gate(0)
            store_y(RH - 1)
            sp.dma_start(att_y[:], groups[4 * B_AG:4 * B_AG + 8].rearrange("g p n -> p g n")).then_inc(att_gate_in, 16)
            with sp.Fori(1, TT) as t:
                load_queries(t, 0)
                load_queries(t, 1)
                load_ada_gate(t)
            ow_ret = w_o_ret[0].rearrange("(b k p) n -> b p k n", p=P, k=KT)
            ow_att = w_o_att[0].rearrange("(k p) n -> p k n", p=P)
            ow_out = w_out[0].rearrange("(k p) n -> p k n", p=P)
            x_rows = x[0].rearrange("(t p) d -> p t d", p=P)
            out_rows = out[0].rearrange("(t p) d -> p t d", p=P)

            def load_chunk(half, c, slot, src):
                done = CHUNKS * half + c
                if not (isinstance(c, int) and half == 0 and c < 3):
                    sp.wait_ge(ow_lo_done, done - (1 if half and isinstance(c, int) and c < 2 else 2))
                sp.dma_start(ow_raw[slot][:], src).then_inc(ow_in[slot], 16)

            def load_chunks(half, n):
                at = bass.ds(n * P, P)
                load_chunk(half, 3 * n, 0, ow_ret[0][:, :, at])
                load_chunk(half, 3 * n + 1, 1, ow_ret[1][:, :, at])
                load_chunk(half, 3 * n + 2, 2, ow_att[:, :, at])

            def load_merge(half, n):
                load_chunks(half, n)
                load_gates(half, n)

            def load_gates(half, n):
                if not (isinstance(n, int) and half == 0 and n == 0):
                    sp.wait_ge(mg_used, KT * half + n)
                for i, b in enumerate((B_MR, B_MA)):
                    src = groups[bass.ds(n + 4 * b, 1)].rearrange("g p n -> (g p) n")
                    sp.dma_start(merge_gate[:, i, :], src[:, half * W:(half + 1) * W]).then_inc(mg_in, 16)

            def load_y(half, i):
                if i < KT:
                    src = y_ret[2 * i:2 * i + 2].rearrange("g p n -> p g n")[:, :, half * W:(half + 1) * W]
                else:
                    src = y_att[2 * i - 2 * KT:2 * i - 2 * KT + 2].rearrange("g p n -> p g n")
                p = KT * half + i
                if p >= 3:
                    last = p - 3
                    sp.wait_ge(y_lo_done, 2 * last + 2 if last < KT else 3 * KT + 2 * (last - KT) + 2)
                if i == KT:
                    sp.wait_ge(att_stored, 16)
                sp.dma_start(y_raw[p % 3][:], src).then_inc(y_in[p % 3], 16)

            def store_out(half, part):
                sp.wait_ge(out_added, KT * half + 2 * part + 2)
                at = slice(2 * part * P, (2 * part + 2) * P)
                sp.dma_start(out_rows[:, 4 * half:4 * half + 4, at], res[:, :, at]).then_inc(out_stored, 16)

            sp.wait_ge(aq_turned, 2 * TT)
            sp.wait_ge(ak_lo_done, KEY_PIECES)
            sp.wait_ge(av_lo_done, 1)
            load_chunk(0, 0, 0, ow_ret[0][:, :, 0:P])
            load_y(0, 0)
            load_chunk(0, 1, 1, ow_ret[1][:, :, 0:P])
            load_y(0, 1)
            load_chunk(0, 2, 2, ow_att[:, :, 0:P])
            sp.wait_ge(sc_bank, 3 * AH * TT)
            sp.wait_ge(ada_g_done, TT)
            load_y(0, 2)
            load_gates(0, 0)
            for i in range(3, KT):
                load_y(0, i)
            load_chunks(0, 1)
            sp.wait_ge(att_out, 2 * TT)
            sp.dma_start(y_att.rearrange("h p n -> p h n"), att_y[:, :, W:2 * W]).then_inc(att_stored, 16)
            load_gates(0, 1)
            for half in range(HALVES):
                if half:
                    load_gates(half, 0)
                    store_out(0, 3)
                    sp.wait_ge(out_stored, 64)
                with sp.Fori(1 if half else 2, KT) as n:
                    load_merge(half, n)
                sp.dma_start(res[:], x_rows[:, 4 * half:4 * half + 4, :]).then_inc(res_in, 16)
                for n in range(3):
                    load_chunk(half, 3 * KT + n, n, ow_out[:, :, n * P:(n + 1) * P])
                for n in range(KT):
                    if n + 3 < KT:
                        load_chunk(half, 3 * KT + n + 3, n % 3, ow_out[:, :, (n + 3) * P:(n + 4) * P])
                    if half == 0:
                        for i in range(12 * n // 8, 12 * (n + 1) // 8):
                            load_y(1, i)
                    if n in (3, 5):
                        store_out(half, n // 2 - 1)
                if half == 0:
                    load_chunks(1, 0)
                store_out(half, 2)
            store_out(1, 3)
            sp.wait_ge(out_stored, 64 * HALVES)

        @block.gpsimd
        def _(pool):
            pool.memset(ones[:], 1.0).then_inc(ones_set, 1)

            def unit_lo(u):
                hi, lo = unit_target(u)
                n = W if u < UNITS_X else CTX
                pool.wait_ge(unit_hi, u + 1)
                pool.tensor_tensor(lo, modulated[:, u % 2, 0:n], hi.bitcast(F32), ALU.subtract).then_inc(unit_lo_pool, 1)

            def first_lo(b, c):
                at = slice(c * P, (c + 1) * P)
                pool.wait_ge(first_split(part_hi_done, w_hi_done, c), first_count(b, c))
                pool.tensor_tensor(w_lo[b][:, :, at], w_raw[b][:, :, at], w_hi[b][:, :, at].bitcast(F32),
                                   ALU.subtract).then_inc(first_split(part_lo_done, w_lo_done, c), 1)

            first_lo(0, 0)
            for u in range(0, KT, 2):
                unit_lo(u)
            for c in range(1, 4):
                first_lo(0, c)
            for u in range(KT, UNITS, 2):
                unit_lo(u)

            def split_lo(b, s):
                pool.wait_ge(w_hi_done, b + 1)
                pool.tensor_tensor(w_lo[s][:], w_raw[s][:], w_hi[s][:].bitcast(F32), ALU.subtract).then_inc(w_lo_done, 1)

            for c in range(4):
                first_lo(1, c)
            with pool.Fori(2, NB - 1, 2) as b:
                split_lo(b, 0)
                split_lo(b + 1, 1)
            split_lo(NB - 1, 0)

            def lo(dst, hi, whole, done):
                pool.tensor_tensor(dst, whole, hi.bitcast(F32), ALU.subtract).then_inc(done, 1)

            def context_lo(h):
                pool.wait_ge(cv_hi_done, h + 1)
                lo(cv[1][:], cv[0][:], cv_raw[:], cv_lo_done)

            def outer_lo(h):
                for i, (r, raw) in enumerate(((rk, rk_raw), (rq, rq_raw))):
                    pool.wait_ge(g03_hi_done, 3 * h + i + 1)
                    lo(both(chunks_of(r[1]), PAIRS[0]), both(chunks_of(r[0]), PAIRS[0]), both(chunks_of(raw), PAIRS[0]), g03_lo_pool)
                pool.wait_ge(g03_hi_done, 3 * h + 3)
                lo(both(v_chunks(rv[1]), PAIRS[0]), both(v_chunks(rv[0]), PAIRS[0]), both(v_chunks(rv_raw), PAIRS[0]), g03_lo_values)

            def head(h, last):
                for s in range(NCH):
                    pool.wait_ge(probs_hi_done, NCH * h + s + 1)
                    lo(probs_r[1][:].rearrange("p t i -> p (t i)"), probs_r[0][:].rearrange("p t i -> p (t i)"), probs[:], probs_lo_done)
                    if s == 0:
                        for i, (r, raw, view) in enumerate(((rk, rk_raw, chunks_of), (rq, rq_raw, chunks_of), (rv, rv_raw, v_chunks))):
                            pool.wait_ge(g12_hi_done, 3 * h + i + 1)
                            lo(both(view(r[1]), PAIRS[1]), both(view(r[0]), PAIRS[1]), both(view(raw), PAIRS[1]), g12_lo_done)
                    if s == 2 and not last:
                        context_lo(h + 1)
                    if s == 3 and not last:
                        outer_lo(h + 1)

            context_lo(0)
            outer_lo(0)
            with pool.Fori(0, RH - 1) as h:
                head(h, False)
            head(RH - 1, True)

            pool.wait_ge(av_hi_done, 1)
            lo(av[1][:], av[0][:], kv_raw[:, :, AKV * AD:], av_lo_done)

            with pool.Fori(0, TT) as t:
                pool.wait_ge(ada_g_in, 16 * t + 16)
                pool.tensor_tensor(ada_g[:], ada_g[:], vec_cols[:, 0:KT].unsqueeze(2).to_broadcast([P, KT, P]),
                                   ALU.mult).then_inc(gate_step, 1)
                for i, n in enumerate((4, 2, 1)):
                    pool.wait_ge(gate_step, 4 * t + i + 1)
                    pool.tensor_tensor(ada_g[:, 0:n, :], ada_g[:, 0:n, :], ada_g[:, n:2 * n, :], ALU.add).then_inc(gate_step, 1)

            def split_chunk(half, c, slot):
                pool.wait_ge(ow_hi_done, CHUNKS * half + c + 1)
                lo(ow[slot][1][:], ow[slot][0][:], ow_raw[slot][:], ow_lo_done)

            for half in range(HALVES):
                for i in range(3):
                    split_chunk(half, i, i)
                with pool.Fori(1, KT) as n:
                    for i in range(3):
                        split_chunk(half, 3 * n + i, i)
                for c in range(3 * KT, CHUNKS):
                    split_chunk(half, c, c % 3)

        @block.scalar
        def _(act):
            act.dma_start(log2_decay[:], ret_log2_decay[0].rearrange("a h -> (a h)").partition_broadcast(P)).then_inc(small_in, 16)
            act.dma_start(decay_exp[:], decay_exp_in).then_inc(small_in, 16)
            act.wait_ge(vec_in, 64)
            act.activation(vec_rows[0:16, :], vec_rows[0:16, :], ACT.Silu).then_inc(vec_silu, 1)
            act.wait_ge(small_in, 32)
            act.activation(lg[:, 0, :], log2_decay[:], ACT.Exp, scale=LN2).then_inc(lg_act, 1)
            act.wait_ge(lg_dve, 1)
            act.activation(lg[:, 2, :], lg[:, 1, :], ACT.Ln).then_inc(lg_act, 1)
            act.wait_ge(lg_dve, 2)
            for h in range(RH):
                for d in range(2):
                    act.activation(decay[:, 10 * h + 5 * d:10 * h + 5 * d + 5], decay_exp[:, 5 * d:5 * d + 5], ACT.Exp,
                                   scale=log_gamma[:, RH * d + h:RH * d + h + 1]).then_inc(decay_done, 1)

            def token_squares(i):
                a, e = NORM_GROUPS[i]
                for t in range(a, e):
                    if t < TT:
                        act.wait_ge(x_in[t // 2], 16)
                    else:
                        act.wait_ge(ctx_in, 16)
                    if t:
                        act.wait_ge(x_squared, t)
                    src = xs[:, t, :] if t < TT else cs[:, t - TT, :]
                    act.activation(square_junk[:], src, ACT.Square, accum_out=ssq_x[:, t:t + 1]).then_inc(x_squared, 1)
                act.wait_ge(ms_done, i + 1)
                act.activation(rms_x[:, a:e], rms_x[:, a:e], ACT.Sqrt).then_inc(rms_done, 1)

            token_squares(0)
            for u in range(KT):
                unit_hi_half(act, u)
            token_squares(1)

            def plain_tile(b, n0, j, bank, func, scale):
                act.wait_ge(tile_done, n0 + j + 1)
                if j < TT:
                    g = j // 2
                    if j % 2 == 0 and not (isinstance(b, int) and b == 0 and g < 2):
                        act.wait_ge(stored[g % 2], 16 * (2 * b + g // 2))
                    dst = stage[:, g % 2, (j % 2) * W:(j % 2 + 1) * W]
                else:
                    if j == TT and not (isinstance(b, int) and b == 0):
                        act.wait_ge(stored_c, 16 * b)
                    dst = stage_c[:, j - TT, :]
                act.activation(dst, ps[:, bank, :], func, scale=scale).then_inc(tile_out, 1)

            def heads_tile(k, n, j, tiles, heads, stat):
                act.wait_ge(tile_done, n + 1)
                if not (isinstance(k, int) and k < 2):
                    act.wait_ge(heads_roped, k - 1)
                if not (isinstance(k, int) and k < 1):
                    act.wait_ge(heads_squared, k)
                act.copy(heads_in[:, j % 2, :], ps[:, j % (tiles // 2), :]).then_inc(tile_out, 1)
                act.wait_ge(tile_out, n + 1)
                for h in range(heads):
                    sq = act.activation(head_junk[:, h, :], heads_in[:, j % 2, h * AD:(h + 1) * AD], ACT.Square,
                                        accum_out=stat[:, h:h + 1])
                sq.then_inc(heads_squared, 1)

            units = iter(range(KT, UNITS))
            for j, n in enumerate((0, 0, 4, 4, 0, 3, 3, 2, 0, 0)):
                for _ in range(n):
                    unit_hi_half(act, next(units))
                plain_tile(0, 0, j, j % 5, ACT.Copy, RDK ** -0.5)
            for b in range(1, B_RV):
                for j in range(TT + CT):
                    plain_tile(b, 10 * b, j, j % 5, ACT.Copy, RDK ** -0.5)
            with act.Fori(B_RV, B_AKV, 1) as b:
                for j in range(TT + CT):
                    plain_tile(b, 10 * b, j, j % 5, ACT.Copy, 1.0)
            for j in range(TT + CT):
                heads_tile(j, 10 * B_AKV + j, j, TT + CT, AKV, ssq_k[:, j, :])
            act.wait_ge(heads_roped, TT + CT)
            with act.Fori(B_RQ, B_RG, 1) as b:
                for j in range(TT):
                    plain_tile(b, 8 * b + 14, j, j % 4, ACT.Copy, 1.0)
            with act.Fori(B_RG, B_AQ, 1) as b:
                for j in range(TT):
                    plain_tile(b, 8 * b + 14, j, j % 4, ACT.Silu, 1.0)
            for i in range(2):
                for j in range(TT):
                    heads_tile(TT + CT + TT * i + j, 8 * (B_AQ + i) + 14 + j, j, TT, 4, ssq_q[:, j, 4 * i:4 * i + 4])
            act.wait_ge(heads_roped, TT + CT + 2 * TT)
            with act.Fori(B_AG, B_MR, 1) as b:
                for j in range(TT):
                    plain_tile(b, 8 * b + 14, j, j % 4, ACT.Silu, 1.0)
            with act.Fori(B_MR, NB - 1, 1) as b:
                for j in range(TT):
                    plain_tile(b, 8 * b + 14, j, j % 4, ACT.Sigmoid, 1.0)

            def last_tile(j):
                plain_tile(NB - 1, 8 * (NB - 1) + 14, j, j % 4, ACT.Sigmoid, 1.0)

            def kd_hi(h, m, d):
                if not (isinstance(h, int) and h == 0 and m == 0):
                    act.wait_ge(delta_done[d], 4 * h + m)
                if m == 0:
                    act.wait_ge(ck_in, 16 * h + 16)
                else:
                    act.wait_ge(k_turned[d], 3 * h + m)
                for j in range(2):
                    src = ck_raw[:, j, :] if m == 0 else ps[:, 0, j * RDK:(j + 1) * RDK]
                    ins = act.activation(kd[d][0][:, j, :], src, ACT.Copy, scale=kd_decay[:, d, j:j + 1])
                ins.then_inc(kd_hi_done[d], 1)

            def state_hi(h, m, d):
                act.wait_ge(state_done[d], 4 * h + m + 1)
                if not (isinstance(h, int) and h == 0 and m == 0):
                    act.wait_ge(cross_done[d], 4 * h + m)
                act.copy(state_r[d][0][:], state[d][:]).then_inc(state_hi_done[d], 1)

            def o_squares(h, g, tiles=(0, 1, 2, 3)):
                first = isinstance(h, int) and h == 0 and g == 0
                act.wait_ge(intra_out, 4 * h + 3 + g)
                act.wait_ge(cross_out[1], 4 * h + 3 + g)
                for i in tiles:
                    t = O_GROUPS[g][i]
                    if not (first and i == 0):
                        act.wait_ge(o_squared, 8 * h + 4 * g + i)
                    act.activation(ret_junk[:], ret_o[:, t, :], ACT.Square,
                                   accum_out=ret_ms[:, 0, 4 * g + i:4 * g + i + 1]).then_inc(o_squared, 1)

            def o_root(h, g):
                act.wait_ge(o_ms, 2 * h + g + 1)
                act.activation(ret_ms[:, 1, 4 * g:4 * g + 4], ret_ms[:, 1, 4 * g:4 * g + 4], ACT.Sqrt).then_inc(o_rms, 1)

            def o_scale(h, g):
                act.wait_ge(o_rstd, 2 * h + g + 1)
                for i, t in enumerate(O_GROUPS[g]):
                    ins = act.activation(ret_o[:, t, :], ret_o[:, t, :], ACT.Copy, scale=ret_ms[:, 2, 4 * g + i:4 * g + i + 1])
                ins.then_inc(o_normed, 1)

            def cross_first(h, s, d):
                c = s if d == 0 else NCH - 1 - s
                act.wait_ge(cross_done[d], 4 * h + s + 1)
                act.wait_ge(head_ready, h + 1)
                if not (isinstance(h, int) and h == 0):
                    act.wait_ge(o_turned, 8 * h)
                for i in range(2):
                    ins = act.activation(ret_o[:, 2 * c + i, :], ps[:, 2 + 2 * d + i, :], ACT.Copy, scale=decay_at(h, 5 * d + i))
                ins.then_inc(cross_out[d], 1)

            def context_keys(h):
                act.wait_ge(kd_ready, 2 * h + 2)
                kd_hi(h, 0, 0)
                kd_hi(h, 0, 1)

            def mask_exps(h):
                if not (isinstance(h, int) and h == 0):
                    act.wait_ge(probs_done, 4 * h)
                for d, m in enumerate((mask, mask_b)):
                    act.activation(m[:], rel[:, d, :], ACT.Exp, scale=head_gamma[:, d:d + 1]).then_inc(mask_exp, 1)

            def probs_hi(h, s):
                act.wait_ge(probs_done, 4 * h + s + 1)
                if not (isinstance(h, int) and h == 0 and s == 0):
                    act.wait_ge(intra_done, 4 * h + s)
                act.copy(probs_r[0][:].rearrange("p t i -> p (t i)"), probs[:]).then_inc(probs_hi_done, 1)

            def head(h, last):
                first = isinstance(h, int) and h == 0
                for s in range(NCH):
                    tail = s == 0 and not first
                    state_hi(h, s, 0)
                    if tail:
                        o_squares(h - 1, 1, (0, 1))
                    state_hi(h, s, 1)
                    if tail:
                        o_squares(h - 1, 1, (2, 3))
                    probs_hi(h, s)
                    if tail:
                        o_root(h - 1, 1)
                    if s == 1:
                        cross_first(h, s, 0)
                    if s < NCH - 1:
                        kd_hi(h, s + 1, 0)
                    if tail:
                        o_scale(h - 1, 1)
                    if s == 1:
                        cross_first(h, s, 1)
                    if s < NCH - 1:
                        kd_hi(h, s + 1, 1)
                    if s == 0:
                        cross_first(h, s, 0)
                        cross_first(h, s, 1)
                if last:
                    keys_hi(0)
                    o_squares(h, 0)
                    keys_hi(1)
                    o_root(h, 0)
                    keys_hi(2)
                    keys_hi(3)
                    o_scale(h, 0)
                    keys_hi(4)
                    keys_hi(5)
                else:
                    context_keys(h + 1)
                    o_squares(h, 0)
                    mask_exps(h + 1)
                    o_root(h, 0)
                    o_scale(h, 0)

            def keys_hi(n):
                act.wait_ge(ak_turned, n + 1)
                g, (k0, k1) = n // 3, piece(n % 3)
                act.copy(ak[0][:, g, k0 * P:k1 * P], ps[:, KEY_BANKS[n], 0:(k1 - k0) * P]).then_inc(ak_hi_done, 1)

            for j in range(6):
                last_tile(j)
            act.wait_ge(rel_in_s, 16)
            context_keys(0)
            mask_exps(0)
            last_tile(6)
            last_tile(7)
            head(0, False)
            act.wait_ge(ms_qk, 1)
            act.activation(rms_k[:], rms_k[:], ACT.Sqrt)
            act.activation(rms_q[:], rms_q[:], ACT.Sqrt).then_inc(rms_qk, 1)
            with act.Fori(1, RH - 1) as h:
                head(h, False)
            head(RH - 1, True)

            def queries_hi(t, half):
                act.wait_ge(aq_turned, 2 * t + half + 1)
                act.copy(aq[0][:, 4 * half:4 * half + 4, :].rearrange("p h i -> p (h i)"), ps[:, queries_bank(t, half), :]).then_inc(aq_hi_done, 1)

            def exponent(t, u):
                k = AH * t + u
                act.wait_ge(neg_done, k + 1)
                if not (isinstance(t, int) and t == 0 and u < 2):
                    act.wait_ge(soft_turned, k - 1)
                act.activation(soft[u % 2][:], bank_span(0, KEYS), ACT.Exp, bias=neg_max[:, u % 2:u % 2 + 1],
                               scale=rstd_of(t, u), accum_out=row_sum[:, u % 2:u % 2 + 1]).then_inc(exp_done, 1)

            def scale_soft(t, u):
                k = AH * t + u
                act.wait_ge(inv_done, k + 1)
                act.activation(soft[u % 2][:], soft[u % 2][:], ACT.Copy, scale=row_inv[:, u % 2:u % 2 + 1]).then_inc(soft_done, 1)

            def soft_hi_half(t, u):
                k = AH * t + u
                if isinstance(t, int) and t == 0 and u == 4:
                    act.wait_ge(y_stored, 16 * RH)
                act.wait_ge(soft_turned, k + 1)
                b = 0
                while b < 3:
                    e = b + 1
                    while e < 3 and turn_bank(u, e) > turn_bank(u, b):
                        e += 1
                    k0, k1 = piece(b)[0], piece(e - 1)[1]
                    src = ps[:, turn_bank(u, b):turn_bank(u, e - 1) + 1, :].rearrange("p b n -> p (b n)")[:, 0:(k1 - k0) * P]
                    ins = act.copy(soft_t[u // 4][0][:, k0:k1, u % 4, :], src.rearrange("p (k i) -> p k i", i=P))
                    b = e
                ins.then_inc(soft_hi, 1)

            def tile(t):
                first = isinstance(t, int) and t == 0
                for u in range(AH):
                    exponent(t, u)
                    if first and u == 0:
                        o_scale(RH - 1, 1)
                    if u > 0:
                        soft_hi_half(t, u - 1)
                    elif not first:
                        soft_hi_half(t - 1, AH - 1)
                    scale_soft(t, u)
                    if u == 1:
                        queries_hi(t, 1)
                    if u == 5 and not (isinstance(t, int) and t == TT - 1):
                        queries_hi(t + 1, 0)

            queries_hi(0, 0)
            o_squares(RH - 1, 1)
            o_root(RH - 1, 1)
            tile(0)
            with act.Fori(1, TT - 1) as t:
                tile(t)
            tile(TT - 1)
            soft_hi_half(TT - 1, AH - 1)

            def chunk_hi(half, c, slot, uses):
                act.wait_ge(ow_in[slot], 16 * uses)
                if not (isinstance(c, int) and half == 0 and c < 3):
                    act.wait_ge(ow_used, CHUNKS * half + c - (1 if half and isinstance(c, int) and c < 2 else 2))
                act.copy(ow[slot][0][:], ow_raw[slot][:]).then_inc(ow_hi_done, 1)

            def chunk_hi_at(half, c):
                chunk_hi(half, c, c % 3, SLOT_USES[c % 3] * half + c // 3 + 1)

            def y_hi(half, i):
                if half == 0 and i >= 2 * KT:
                    act.wait_ge(att_out, TT)
                else:
                    act.wait_ge(y_in[y_pair(half, i) % 3], 16 * (y_pair(half, i) // 3 + 1))
                act.copy(y_r(i, 0), y_whole(half, i)).then_inc(y_hi_done, 1)

            for half in range(HALVES):
                if half == 0:
                    chunk_hi_at(0, 0)
                    act.wait_ge(pv_done, 2 * TT - 1)
                    for i in range(10):
                        y_hi(0, i)
                        if i == 1:
                            chunk_hi_at(0, 1)
                    act.wait_ge(pv_done, 2 * TT)
                    for i in range(10, 3 * KT):
                        y_hi(0, i)
                        if i in (11, 18, 21):
                            chunk_hi_at(0, {11: 2, 18: 3, 21: 4}[i])
                    chunk_hi_at(0, 5)
                else:
                    chunk_hi_at(1, 1)
                    chunk_hi_at(1, 2)
                with act.Fori(1 if half else 2, KT) as n:
                    for i in range(3):
                        chunk_hi(half, 3 * n + i, i, SLOT_USES[i] * half + n + 1)
                for c in range(3):
                    chunk_hi_at(half, 3 * KT + c)
                for n in range(KT):
                    k = KT * half + n
                    if half == 0 and n == KT - 1:
                        chunk_hi_at(1, 0)
                    act.wait_ge(ow_used, CHUNKS * half + 3 * KT + n + 1)
                    if k >= 2:
                        act.wait_ge(out_turned, k - 1)
                    act.activation(out_t[:, n % 2, :], ps[:, 2 + n % 2, :], ACT.Copy, scale=mod[:, 2 * KT + n, 0:1]).then_inc(out_gated, 1)
                    if n + 3 < KT:
                        chunk_hi_at(half, 3 * KT + n + 3)
                    if half == 0:
                        for i in range(3 * n, 3 * n + 3):
                            y_hi(1, i)

        @block.vector
        def _(dve):
            own = Steps(dve, dve_step)
            dve.wait_ge(vec_turned, 1)
            dve.tensor_copy(vec_cols[:], ps[:, 0, 0:48]).then_inc(vec_copied, 1)

            def rows_from_psum(n):
                dve.wait_ge(ada_used, n + 1)
                dve.tensor_copy(ada_rows[:, n * W:(n + 1) * W], ps[0:2, n % 2, :]).then_inc(rows_out, 1)

            def norm_group(i):
                a, e = NORM_GROUPS[i]
                dve.wait_ge(x_squared, e)
                dve.tensor_scalar(rms_x[:, a:e], ssq_x[:, a:e], 1.0 / D, EPS, ALU.mult, ALU.add).then_inc(ms_done, 1)
                if i == 0:
                    rows_from_psum(3)
                dve.wait_ge(rms_done, i + 1)
                own.then(dve.reciprocal(rstd_x[:, a:e], rms_x[:, a:e]))
                for t in range(a, e):
                    v = xs[:, t, :] if t < TT else cs[:, t - TT, :]
                    dve.tensor_scalar(v, v, rstd_x[:, t:t + 1], None, ALU.mult).then_inc(x_normed, 1)

            def unit(u):
                hi, lo = unit_target(u)
                n = W if u < UNITS_X else CTX
                v = 0 if u < UNITS_X else 1
                dve.wait_ge(unit_turned, u + 1)
                if u >= 2:
                    dve.wait_ge(unit_hi, u - 1)
                    if u % 2:
                        dve.wait_ge(unit_lo_dve, (u - 1) // 2)
                    else:
                        dve.wait_ge(unit_lo_pool, u // 2)
                dve.tensor_scalar(modulated[:, u % 2, 0:n], ps[:, unit_bank(u), 0:n], a_col[:, u % KT, v:v + 1],
                                  mod[:, u % KT, v:v + 1], ALU.mult, ALU.add).then_inc(unit_modulated, 1)

            def unit_lo(u):
                hi, lo = unit_target(u)
                n = W if u < UNITS_X else CTX
                dve.wait_ge(unit_hi, u + 1)
                dve.tensor_tensor(lo, modulated[:, u % 2, 0:n], hi.bitcast(F32), ALU.subtract).then_inc(unit_lo_dve, 1)

            dve.wait_ge(lg_act, 1)
            u_, w_, ln_, d_, m_, r_ = (lg[:, i, :] for i in range(6))
            dve.tensor_scalar(w_, u_, -1.0, 1.0, ALU.mult, ALU.add).then_inc(lg_dve, 1)
            dve.wait_ge(lg_dve, 1)
            own.then(dve.tensor_scalar(d_, w_, -1.0, None, ALU.add))
            own.then(dve.tensor_scalar(m_, d_, 0.0, None, ALU.is_equal))
            own.then(dve.tensor_tensor(d_, d_, m_, ALU.add))
            own.then(dve.reciprocal(r_, d_))
            own.then(dve.tensor_tensor(r_, r_, u_, ALU.mult))
            dve.wait_ge(lg_act, 2)
            own.then(dve.tensor_tensor(r_, r_, ln_, ALU.mult))
            own.then(dve.tensor_tensor(m_, m_, u_, ALU.mult))
            own.then(dve.tensor_tensor(r_, r_, m_, ALU.add))
            dve.tensor_scalar(log_gamma[:], r_, -1.0, None, ALU.mult).then_inc(lg_dve, 1)

            for n in range(3):
                rows_from_psum(n)
            norm_group(0)
            dve.wait_ge(ada_turned, 1)
            own.then(dve.tensor_tensor(mod[:, 0:2 * KT, :], ps[:, 0, 0:4 * KT].rearrange("p (n v) -> p n v", v=2),
                                       vec_cols[:, 24:24 + 2 * KT].unsqueeze(2).to_broadcast([P, 2 * KT, 2]), ALU.add))
            own.then(dve.tensor_scalar(a_col[:], mod[:, KT:2 * KT, :], 1.0, None, ALU.add))
            own.then(dve.tensor_tensor(a_col[:], a_col[:], vec_cols[:, 16:24].unsqueeze(2).to_broadcast([P, KT, 2]),
                                       ALU.mult))

            def split_hi(b, s, used_tiles, loads):
                if used_tiles is not None:
                    dve.wait_ge(tile_done, used_tiles)
                dve.wait_ge(w_in_s[s], 16 * loads)
                dve.tensor_copy(w_hi[s][:], w_raw[s][:]).then_inc(w_hi_done, 1)

            def first_hi(c, b=0):
                at = slice(c * P, (c + 1) * P)
                dve.wait_ge(w_in_s[b], 16)
                dve.tensor_copy(w_hi[b][:, :, at], w_raw[b][:, :, at]).then_inc(first_split(part_hi_done, w_hi_done, c), 1)

            for u in range(UNITS):
                if u == 0:
                    first_hi(0)
                if u == KT - 2:
                    first_hi(1)
                if u == KT:
                    first_hi(2)
                    first_hi(3)
                    norm_group(1)
                unit(u)
                if u % 2:
                    unit_lo(u)

            def rotate_tile(k, n, j, heads, t, w_index, dst, slot_free):
                src = heads_in[:, j % 2, :]
                dve.wait_ge(tile_out, n + 1)
                slot_free()
                wide = heads * AD
                bcast = qk_norm[:, w_index, :].unsqueeze(1).to_broadcast([P, heads, AD])
                to = heads_w[:, 0:wide] if t is not None else dst[:, 0:wide]
                if wide < W:
                    own.then(dve.tensor_copy(dst[:, wide:W], src[:, wide:W]))
                ins = dve.tensor_tensor(to.rearrange("p (h e) -> p h e", h=heads),
                                        src[:, 0:wide].rearrange("p (h e) -> p h e", h=heads), bcast, ALU.mult)
                if t is None:
                    ins.then_inc(heads_roped, 1)
                    return
                own.then(ins)

                def pairs(v):
                    return v[:, 0:wide].rearrange("p (h e two) -> p h e two", h=heads, two=2)

                def table(i):
                    return rope_cs[:, i, t, :].unsqueeze(1).to_broadcast([P, heads, AD // 2])

                xw, rot, d = pairs(heads_w), pairs(rope_t), pairs(dst)
                dve.tensor_tensor(d[:, :, :, 0], xw[:, :, :, 0], table(0), ALU.mult)
                own.then(dve.tensor_tensor(d[:, :, :, 1], xw[:, :, :, 1], table(0), ALU.mult))
                dve.tensor_tensor(rot[:, :, :, 0], xw[:, :, :, 1], table(1), ALU.mult)
                own.then(dve.tensor_tensor(rot[:, :, :, 1], xw[:, :, :, 0], table(1), ALU.mult))
                own.then(dve.tensor_tensor(d[:, :, :, 0], d[:, :, :, 0], rot[:, :, :, 0], ALU.subtract))
                dve.tensor_tensor(d[:, :, :, 1], d[:, :, :, 1], rot[:, :, :, 1], ALU.add).then_inc(heads_roped, 1)
                dve.wait_ge(heads_roped, k + 1)

            def stage_slot(b, j):
                def free():
                    if j % 2 == 0:
                        dve.wait_ge(stored[(j // 2) % 2], 16 * (2 * b + j // 4))
                return stage[:, (j // 2) % 2, (j % 2) * W:(j % 2 + 1) * W], free

            for c in range(4):
                first_hi(c, 1)
            split_hi(2, 0, 10, 2)
            split_hi(3, 1, 20, 2)
            with dve.Fori(4, B_AKV + 2, 2) as b:
                split_hi(b, 0, 10 * b - 10, b // 2 + 1)
                split_hi(b + 1, 1, 10 * b, b // 2 + 1)
            dve.wait_ge(small_in, 96)
            for j in range(TT + CT):
                if j < TT:
                    dst, free = stage_slot(B_AKV, j)
                    rotate_tile(j, 10 * B_AKV + j, j, AKV, j, 1, dst, free)
                else:
                    rotate_tile(j, 10 * B_AKV + j, j, AKV, None, 1, stage_c[:, j - TT, :],
                                lambda: dve.wait_ge(stored_c, 16 * B_AKV))
            with dve.Fori(8, 14, 2) as b:
                split_hi(b, 0, 8 * b + 6, b // 2 + 1)
                split_hi(b + 1, 1, 8 * b + 14, b // 2 + 1)
            for i in range(2):
                b = B_AQ + i
                split_hi(b + 1, (b + 1) % 2, 8 * b + 14, (b + 1) // 2 + 1)
                for j in range(TT):
                    dst, free = stage_slot(b, j)
                    rotate_tile(TT + CT + TT * i + j, 8 * b + 14 + j, j, 4, j, 0, dst, free)
            with dve.Fori(16, NB - 1, 2) as b:
                split_hi(b, 0, 8 * b + 6, b // 2 + 1)
                split_hi(b + 1, 1, 8 * b + 14, b // 2 + 1)
            split_hi(NB - 1, 0, 8 * (NB - 1) + 6, (NB - 1) // 2 + 1)

            def kd_lo(h, m, d):
                dve.wait_ge(kd_hi_done[d], 4 * h + m + 1)
                for j in range(2):
                    src = ck_raw[:, j, :] if m == 0 else ps[:, 0, j * RDK:(j + 1) * RDK]
                    ins = dve.scalar_tensor_tensor(out=kd[d][1][:, j, :], in0=src, scalar=kd_decay[:, d, j:j + 1],
                                                   in1=kd[d][0][:, j, :].bitcast(F32), op0=ALU.mult, op1=ALU.subtract)
                ins.then_inc(kd_lo_done[d], 1)

            def delta_ps(d):
                return ps[:, 2 + 2 * d:4 + 2 * d, :]

            def update_state(h, m, d):
                dve.wait_ge(delta_done[d], 4 * h + m + 1)
                if not (isinstance(h, int) and h == 0 and m == 0):
                    dve.wait_ge(state_lo_done[d], 4 * h + m)
                    dve.wait_ge(state_hi_done[d], 4 * h + m)
                if m == 0:
                    dve.tensor_copy(state[d][:], delta_ps(d)).then_inc(state_done[d], 1)
                else:
                    dve.scalar_tensor_tensor(out=state[d][:], in0=state[d][:], scalar=decay_at(h, 5 * d + 4),
                                             in1=delta_ps(d), op0=ALU.mult, op1=ALU.add).then_inc(state_done[d], 1)

            def state_lo(h, m, d):
                dve.wait_ge(state_hi_done[d], 4 * h + m + 1)
                dve.tensor_tensor(state_r[d][1][:], state[d][:], state_r[d][0][:].bitcast(F32),
                                  ALU.subtract).then_inc(state_lo_done[d], 1)

            def mean_square(h, g):
                dve.wait_ge(o_squared, 8 * h + 4 * g + 4)
                dve.tensor_scalar(ret_ms[:, 1, 4 * g:4 * g + 4], ret_ms[:, 0, 4 * g:4 * g + 4], 1.0 / RDV, EPS,
                                  ALU.mult, ALU.add).then_inc(o_ms, 1)

            def rstd(h, g):
                dve.wait_ge(o_rms, 2 * h + g + 1)
                dve.reciprocal(ret_ms[:, 2, 4 * g:4 * g + 4], ret_ms[:, 1, 4 * g:4 * g + 4]).then_inc(o_rstd, 1)

            def gated(h, g, e):
                bank = o_bank(h, g, e)
                dve.wait_ge(o_turned, 8 * h + 4 * g + e + 1)
                dve.wait_ge(gate_in, 16 * h + 16)
                if g == 0:
                    v = gate_y[:, e, 2 * P:6 * P]
                    dve.tensor_tensor(v, ps[:, bank, :], v, ALU.mult).then_inc(y_out, 1)
                else:
                    v = gate_y[:, e, 6 * P:8 * P]
                    dve.tensor_tensor(v, ps[:, bank, 0:2 * P], v, ALU.mult)
                    v = gate_y[:, e, 0:2 * P]
                    dve.tensor_tensor(v, ps[:, bank, 2 * P:4 * P], v, ALU.mult).then_inc(y_out, 1)

            def cross_again(h, s, d):
                c = s if d == 0 else NCH - 1 - s
                dve.wait_ge(cross_done[d], 4 * h + s + 1)
                dve.wait_ge(cross_out[1 - d], 4 * h + NCH - s)
                if d == 1:
                    dve.wait_ge(intra_out, 4 * h + NCH - s)
                for i in range(2):
                    ins = dve.scalar_tensor_tensor(out=ret_o[:, 2 * c + i, :], in0=ps[:, 2 + 2 * d + i, :],
                                                   scalar=decay_at(h, 5 * d + i), in1=ret_o[:, 2 * c + i, :],
                                                   op0=ALU.mult, op1=ALU.add)
                ins.then_inc(cross_out[d], 1)

            def key_decays(h):
                if not (isinstance(h, int) and h == 0):
                    dve.wait_ge(mask_exp, 2 * h)
                    dve.wait_ge(kd_hi_done[0], 4 * h)
                    dve.wait_ge(kd_hi_done[1], 4 * h)
                    dve.wait_ge(kd_lo_done[0], 4 * h)
                    dve.wait_ge(kd_lo_done[1], 4 * h)
                dve.tensor_scalar(kd_decay[:], decay[:, bass.ds(h * 10, 10)].rearrange("p (d c) -> p d c", d=2)[:, :, 2:4],
                                  1.0, None, ALU.mult).then_inc(kd_ready, 1)
                dve.tensor_scalar(head_gamma[:], log_gamma[:].rearrange("p (d h) -> p d h", d=2)[:, :, bass.ds(h, 1)]
                                  .rearrange("p d o -> p (d o)"), 1.0, None, ALU.mult).then_inc(kd_ready, 1)
                dve.wait_ge(kd_ready, 2 * h + 2)

            def head_decays(h):
                if not (isinstance(h, int) and h == 0):
                    dve.wait_ge(cross_out[0], 4 * h)
                    dve.wait_ge(cross_out[1], 4 * h)
                dve.tensor_scalar(head_decay[:], decay[:, bass.ds(h * 10, 10)], 1.0, None, ALU.mult).then_inc(head_ready, 1)
                dve.wait_ge(head_ready, h + 1)

            def context_values(h):
                dve.wait_ge(cv_in, 16 * h + 16)
                if not (isinstance(h, int) and h == 0):
                    dve.wait_ge(delta_done[1], 4 * h - 3)
                dve.tensor_copy(cv[0][:], cv_raw[:]).then_inc(cv_hi_done, 1)

            OPERANDS = ((rk, rk_raw, chunks_of, rk_in), (rq, rq_raw, chunks_of, rq_in), (rv, rv_raw, v_chunks, rv_in))

            def outer_hi(h, i):
                r, raw, view, arrived = OPERANDS[i]
                dve.wait_ge(arrived, 16 * h + 16)
                dve.tensor_copy(both(view(r[0]), PAIRS[0]), both(view(raw), PAIRS[0])).then_inc(g03_hi_done, 1)

            def inner_hi(i):
                r, raw, view, _ = OPERANDS[i]
                dve.tensor_copy(both(view(r[0]), PAIRS[1]), both(view(raw), PAIRS[1])).then_inc(g12_hi_done, 1)

            def make_mask(h):
                dve.wait_ge(mask_exp, 2 * h + 2)
                dve.tensor_tensor(mask[:], mask[:], rel[:, 2, :], ALU.mult).then_inc(mask_done, 1)
                dve.tensor_tensor(mask_b[:], mask_b[:], rel[:, 3, :], ALU.mult).then_inc(mask_done, 1)
                dve.wait_ge(mask_done, 3 * h + 2)
                dve.tensor_tensor(mask[:], mask[:], mask_b[:], ALU.add).then_inc(mask_done, 1)

            def new_state(h, m):
                update_state(h, m, 0)
                state_lo(h, m, 0)
                update_state(h, m, 1)

            def mask_scores(h, s):
                dve.wait_ge(scores_done, 4 * h + s + 1)
                if s == 0:
                    dve.wait_ge(mask_done, 3 * h + 3)
                if isinstance(h, int) and h == 0 and s == 0:
                    for i in range(2):
                        dve.wait_ge(stored[i], 16 * 2 * NB)
                if not (isinstance(h, int) and h == 0 and s == 0):
                    dve.wait_ge(probs_lo_done, 4 * h + s)
                dve.tensor_tensor(probs[:], ps[:, 1, :], mask[:], ALU.mult).then_inc(probs_done, 1)

            def add_intra(h, s):
                dve.wait_ge(intra_done, 4 * h + s + 1)
                dve.wait_ge(cross_out[0], 4 * h + s + 1)
                v = ret_o[:, 2 * s:2 * s + 2, :]
                dve.tensor_tensor(v, v, ps[:, 6:8, :], ALU.add).then_inc(intra_out, 1)

            def head(h, last):
                first = isinstance(h, int) and h == 0
                mask_scores(h, 0)
                if not first:
                    for e in range(3):
                        gated(h - 1, 0, e)
                state_lo(h, 0, 1)
                if not first:
                    mean_square(h - 1, 1)
                    rstd(h - 1, 1)
                    gated(h - 1, 0, 3)
                kd_lo(h, 1, 0)
                inner_hi(0)
                kd_lo(h, 1, 1)
                inner_hi(1)
                if not first:
                    for e in range(4):
                        gated(h - 1, 1, e)
                inner_hi(2)
                add_intra(h, 0)
                new_state(h, 1)
                mask_scores(h, 1)
                state_lo(h, 1, 1)
                kd_lo(h, 2, 0)
                kd_lo(h, 2, 1)
                add_intra(h, 1)
                new_state(h, 2)
                mask_scores(h, 2)
                state_lo(h, 2, 1)
                cross_again(h, 2, 0)
                kd_lo(h, 3, 0)
                cross_again(h, 2, 1)
                kd_lo(h, 3, 1)
                if last:
                    key_roots()
                    normalise_keys(0)
                    normalise_keys(1)
                else:
                    context_values(h + 1)
                add_intra(h, 2)
                new_state(h, 3)
                mask_scores(h, 3)
                state_lo(h, 3, 1)
                if last:
                    keys_lo(0)
                else:
                    key_decays(h + 1)
                cross_again(h, 3, 0)
                if last:
                    keys_lo(1)
                else:
                    kd_lo(h + 1, 0, 0)
                    kd_lo(h + 1, 0, 1)
                    outer_hi(h + 1, 0)
                cross_again(h, 3, 1)
                mean_square(h, 0)
                if not last:
                    outer_hi(h + 1, 1)
                    make_mask(h + 1)
                rstd(h, 0)
                if last:
                    keys_lo(2)
                    keys_lo(3)
                add_intra(h, 3)
                if last:
                    keys_lo(4)
                    keys_lo(5)
                else:
                    update_state(h + 1, 0, 0)
                    head_decays(h + 1)
                    outer_hi(h + 1, 2)
                    state_lo(h + 1, 0, 0)
                    update_state(h + 1, 0, 1)

            def key_roots():
                dve.wait_ge(rms_qk, 1)
                dve.reciprocal(rstd_k[:], rms_k[:]).then_inc(rstd_qk, 1)
                dve.reciprocal(rstd_q[:], rms_q[:]).then_inc(rstd_qk, 1)
                dve.wait_ge(rstd_qk, 2)
                dve.wait_ge(kv_in, 32)

            def normalise_keys(g):
                keys = kv_raw[:, :, g * AD:(g + 1) * AD]
                r = rstd_k[:].rearrange("p (t h) -> p t h", h=AKV)[:, :, g:g + 1].to_broadcast([P, NKT, AD])
                dve.tensor_tensor(keys, keys, r, ALU.mult).then_inc(keys_normed, 1)

            def values_hi():
                for d in range(2):
                    dve.wait_ge(k_turned[d], 3 * RH)
                dve.wait_ge(g12_lo_done, 3 * RH)
                dve.tensor_copy(av[0][:], kv_raw[:, :, AKV * AD:]).then_inc(av_hi_done, 1)

            def keys_lo(n):
                dve.wait_ge(ak_hi_done, n + 1)
                g, (k0, k1) = n // 3, piece(n % 3)
                dve.tensor_tensor(ak[1][:, g, k0 * P:k1 * P], ps[:, KEY_BANKS[n], 0:(k1 - k0) * P],
                                  ak[0][:, g, k0 * P:k1 * P].bitcast(F32), ALU.subtract).then_inc(ak_lo_done, 1)

            key_decays(0)
            head_decays(0)
            context_values(0)
            kd_lo(0, 0, 0)
            kd_lo(0, 0, 1)
            outer_hi(0, 0)
            dve.wait_ge(w_lo_done, NB)
            outer_hi(0, 1)
            make_mask(0)
            dve.wait_ge(tile_done, 8 * NB + 14)
            outer_hi(0, 2)
            dve.wait_ge(heads_squared, TT + CT + 2 * TT)
            dve.tensor_scalar(rms_k[:], ssq_k[:].rearrange("p t h -> p (t h)"), 1.0 / AD, EPS, ALU.mult, ALU.add)
            dve.tensor_scalar(rms_q[:], ssq_q[:].rearrange("p t h -> p (t h)"), AD * EPS, None, ALU.add).then_inc(ms_qk, 1)
            new_state(0, 0)
            head(0, False)
            with dve.Fori(1, RH - 1) as h:
                head(h, False)
            head(RH - 1, True)


            def queries_lo(t, half):
                dve.wait_ge(aq_hi_done, 2 * t + half + 1)
                dst, hi = (v[:, 4 * half:4 * half + 4, :].rearrange("p h i -> p (h i)") for v in (aq[1], aq[0]))
                dve.tensor_tensor(dst, ps[:, queries_bank(t, half), :], hi.bitcast(F32), ALU.subtract).then_inc(aq_lo_done, 1)

            def row_maxima(t, u):
                k = AH * t + u
                i = u % 2
                if not (isinstance(t, int) and t == 0 and u < 2):
                    dve.wait_ge(exp_done, k - 1)
                for b in range(3):
                    dve.wait_ge(sc_bank, 3 * k + b + 1)
                    dve.tensor_reduce(row_max[:, i, b:b + 1], ps[:, b, 0:min(W, KEYS - b * W)], AX.X, ALU.max).then_inc(max_bank, 1)
                dve.wait_ge(max_bank, 3 * k + 3)
                dve.tensor_reduce(row_max[:, i, 3:4], row_max[:, i, 0:3], AX.X, ALU.max).then_inc(max_all, 1)
                dve.wait_ge(max_all, k + 1)
                dve.scalar_tensor_tensor(out=neg_max[:, i:i + 1], in0=row_max[:, i, 3:4], scalar=-1.0, in1=rstd_of(t, u),
                                         op0=ALU.mult, op1=ALU.mult).then_inc(neg_done, 1)

            def inverse(t, u):
                k = AH * t + u
                i = u % 2
                dve.wait_ge(exp_done, k + 1)
                if not (isinstance(t, int) and t == 0 and u < 2):
                    dve.wait_ge(soft_done, k - 1)
                dve.reciprocal(row_inv[:, i:i + 1], row_sum[:, i:i + 1]).then_inc(inv_done, 1)

            def soft_lo_half(t, u):
                k = AH * t + u
                dve.wait_ge(soft_hi, k + 1)
                for b in range(3):
                    k0, k1 = piece(b)
                    hi, dst = (soft_t[u // 4][i][:, k0:k1, u % 4, :] for i in range(2))
                    dve.tensor_tensor(dst, ps[:, turn_bank(u, b), 0:(k1 - k0) * P].rearrange("p (k i) -> p k i", i=P), hi.bitcast(F32),
                                      ALU.subtract).then_inc(soft_lo, 1)

            def gate_out(t, g):
                dve.wait_ge(pv_done, 2 * t + g + 1)
                v = att_y[:, 4 * g:4 * g + 4, bass.ds(t * P, P)]
                dve.tensor_tensor(v, ps[:, 7, :].rearrange("p (h i) -> p h i", h=4), v, ALU.mult).then_inc(att_out, 1)

            def ada_gate(t):
                dve.wait_ge(ada_g_done, t + 1)
                dve.tensor_tensor(mod_col(t), ps[:, turn_bank(AH - 1, 0), 0:1], vec_cols[:, bass.ds(t + 24 + 2 * KT, 1)], ALU.add).then_inc(gate_col, 1)

            def tile(t):
                first = isinstance(t, int) and t == 0
                last = isinstance(t, int) and t == TT - 1
                if not first:
                    inverse(t - 1, AH - 1)
                dve.tensor_scalar(tile_rstd[:], rstd_q[:, bass.ds(t * AH, AH)], 1.0, None, ALU.mult).then_inc(tile_ready, 1)
                dve.wait_ge(tile_ready, t + 1)
                for u in range(AH):
                    if u > 0:
                        inverse(t, u - 1)
                    row_maxima(t, u)
                    if first and u < 2:
                        for e in range(4):
                            gated(RH - 1, u, e)
                    if first and u == 0:
                        values_hi()
                    if u == 2:
                        queries_lo(t, 1)
                    if u == 6 and not last:
                        queries_lo(t + 1, 0)
                    if u > 1:
                        soft_lo_half(t, u - 2)
                    elif not first:
                        soft_lo_half(t - 1, AH - 2 + u)
                    if u in (1, 5) and not first:
                        gate_out(t - 1, u // 4)
                    if u == 7:
                        ada_gate(t)

            queries_lo(0, 0)
            mean_square(RH - 1, 1)
            rstd(RH - 1, 1)
            tile(0)
            dve.wait_ge(att_gate_in, 16)
            with dve.Fori(1, TT - 1) as t:
                tile(t)
            tile(TT - 1)
            inverse(TT - 1, AH - 1)
            soft_lo_half(TT - 1, AH - 2)
            soft_lo_half(TT - 1, AH - 1)
            gate_out(TT - 1, 0)

            def y_lo(half, i):
                dve.wait_ge(y_hi_done, 3 * KT * half + i + 1)
                dve.tensor_tensor(y_r(i, 1), y_whole(half, i), y_r(i, 0).bitcast(F32),
                                  ALU.subtract).then_inc(y_lo_done, 1)

            def merge(half, n):
                k = KT * half + n
                dve.wait_ge(mg_in, 32 * k + 32)
                dve.wait_ge(ow_used, CHUNKS * half + 3 * n + 2)
                if not (half == 0 and isinstance(n, int)):
                    dve.wait_ge(z_lo_done, k)
                dve.tensor_tensor(merged[:, 0, :], ps[:, 0, :], merge_gate[:, 0, :], ALU.mult).then_inc(merged_part, 1)
                dve.wait_ge(ow_used, CHUNKS * half + 3 * n + 3)
                dve.tensor_tensor(merged[:, 1, :], ps[:, 1, :], merge_gate[:, 1, :], ALU.mult).then_inc(mg_used, 1)
                dve.wait_ge(mg_used, k + 1)
                dve.tensor_tensor(merged[:, 0, :], merged[:, 0, :], merged[:, 1, :], ALU.add).then_inc(merged_done, 1)
                dve.wait_ge(merged_done, k + 1)
                if isinstance(n, int):
                    if half:
                        dve.wait_ge(ow_used, CHUNKS)
                    else:
                        dve.wait_ge(att_stored, 16)
                dve.tensor_scalar(row_of(z_r[0], n), merged[:, 0, :], 1.0, None, ALU.mult).then_inc(z_hi_done, 1)
                dve.wait_ge(z_hi_done, k + 1)
                dve.tensor_tensor(row_of(z_r[1], n), merged[:, 0, :], row_of(z_r[0], n).bitcast(F32), ALU.subtract).then_inc(z_lo_done, 1)

            for half in range(HALVES):
                if half == 0:
                    for i in range(3 * KT):
                        if i == 6:
                            gate_out(TT - 1, 1)
                        y_lo(0, i)
                merge(half, 0)
                with dve.Fori(1, KT) as n:
                    merge(half, n)
                dve.wait_ge(res_in, 16 * half + 16)
                for n in range(KT):
                    if half == 0:
                        for i in range(3 * n, 3 * n + 3):
                            y_lo(1, i)
                    dve.wait_ge(out_turned, KT * half + n + 1)
                    v = res[:, :, n * P:(n + 1) * P]
                    dve.tensor_tensor(v, v, ps[:, 4 + n % 2, :].rearrange("p (t e) -> p t e", t=4), ALU.add).then_inc(out_added, 1)

        @block.tensor
        def _(pe):
            pe.wait_ge(ident_in_s, 16)
            pe.wait_ge(ones_set, 1)
            pe.wait_ge(vec_silu, 1)
            pe.transpose(ps[:, 0, 0:48], vec_rows[:], ident[0:48, 0:48]).then_inc(vec_turned, 1)

            def turn(u):
                bank = unit_bank(u)
                pe.wait_ge(x_normed, TT + CT if u >= UNITS_X else 4 * (u // KT) + 4)
                before = [v for v in range(u) if unit_bank(v) == bank]
                if before:
                    pe.wait_ge(unit_modulated, before[-1] + 1)
                k = u % KT
                n = 4 if u < UNITS_X else CT
                for i in range(n):
                    src = xs[:, 4 * (u // KT) + i, k * P:(k + 1) * P] if u < UNITS_X else cs[:, i, k * P:(k + 1) * P]
                    ins = pe.transpose(ps[:, bank, i * P:(i + 1) * P], src, ident[:])
                ins.then_inc(unit_turned, 1)

            pe.wait_ge(vec_copied, 1)
            vecs = vec_cols[:, 0:2 * KT].rearrange("p (v k) -> p k v", k=KT)
            for n in range(4):
                pe.wait_ge(ada_in[n] if n else ada_part_in, 16)
                if n >= 2:
                    pe.wait_ge(rows_out, n - 1)
                for k in range(KT):
                    if n == 0 and k == KT // 2:
                        pe.wait_ge(ada_in[0], 16)
                    ins = pe.matmul(ps[0:2, n % 2, :], vecs[:, k, :], ada_block(n)[:, k, :], start=(k == 0), stop=(k == KT - 1))
                ins.then_inc(ada_used, 1)
            pe.wait_ge(rows_out, 4)
            for n in range(2 * KT):
                ins = pe.transpose(ps[:, 0, 2 * n:2 * n + 2], ada_rows[:, n * P:(n + 1) * P], ident[0:2, 0:2])
            ins.then_inc(ada_turned, 1)
            for u in range(KT):
                turn(u)

            def passes(out, stat, mov, stat_at, mov_at, n):
                for k in range(n):
                    for i, (s, m) in enumerate(((0, 0), (0, 1), (1, 0))):
                        ins = pe.matmul(out, stat_at(stat[s], k), mov_at(mov[m], k),
                                        start=(k == 0 and i == 0), stop=(k == n - 1 and i == 2))
                return ins

            def x_tile(n, j, bank, s, transposed):
                pe.wait_ge(tile_out, n - 3)
                wt = (w_hi[s], w_lo[s])
                if transposed:
                    col, half = j // 2, j % 2
                    ins = passes(ps[:, bank, :], wt, (hx_hi, hx_lo), lambda v, k: v[:, k, col * P:(col + 1) * P],
                                 lambda v, k: v[:, k, half * W:(half + 1) * W], KT)
                else:
                    ins = passes(ps[:, bank, :], (hx_hi, hx_lo), wt, lambda v, k: v[:, k, j * P:(j + 1) * P],
                                 lambda v, k: v[:, k, :], KT)
                ins.then_inc(tile_done, 1)

            def c_tile(n, j, bank, s):
                pe.wait_ge(tile_out, n - 3)
                passes(ps[:, bank, :], (hc_hi, hc_lo), (w_hi[s], w_lo[s]),
                       lambda v, k: v[:, k, (j - TT) * P:(j - TT + 1) * P], lambda v, k: v[:, k, :], KT).then_inc(tile_done, 1)

            wt = (w_hi[0], w_lo[0])
            units = iter(range(KT, UNITS))
            for j, n in enumerate((0, 0, 4, 4, 0, 3, 3, 2)):
                for _ in range(n):
                    turn(next(units))
                half, col = j // 4, j % 4
                if half == 0:
                    pe.wait_ge(first_split(part_lo_done, w_lo_done, col), first_count(0, col))
                if j == 4:
                    pe.wait_ge(unit_modulated, KT + 5)
                if j >= 5:
                    pe.wait_ge(tile_out, j - 4)
                for k in range(KT):
                    if col == 0:
                        pe.wait_ge(unit_hi, KT * half + k + 1)
                        pe.wait_ge(unit_lo_dve if k % 2 else unit_lo_pool, (KT * half + k) // 2 + 1)
                    for i, (a, b) in enumerate(((0, 0), (0, 1), (1, 0))):
                        ins = pe.matmul(ps[:, j % 5, :], wt[a][:, k, col * P:(col + 1) * P],
                                        (hx_hi, hx_lo)[b][:, k, half * W:(half + 1) * W],
                                        start=(k == 0 and i == 0), stop=(k == KT - 1 and i == 2))
                ins.then_inc(tile_done, 1)
            pe.wait_ge(unit_hi, UNITS)
            pe.wait_ge(unit_lo_dve, UNITS // 2)
            pe.wait_ge(unit_lo_pool, UNITS // 2)
            for j in range(TT, TT + CT):
                c_tile(j, j, j % 5, 0)
            for j in range(TT):
                if j % 2 == 0:
                    pe.wait_ge(first_split(part_lo_done, w_lo_done, j // 2), first_count(1, j // 2))
                x_tile(10 + j, j, j % 5, 1, True)
            for j in range(TT, TT + CT):
                c_tile(10 + j, j, j % 5, 1)

            def ctx_block(b, s):
                pe.wait_ge(w_lo_done, b + 1)
                for j in range(TT):
                    x_tile(10 * b + j, j, j % 5, s, False)
                for j in range(TT, TT + CT):
                    c_tile(10 * b + j, j, j % 5, s)

            def x_block(b, s, transposed):
                pe.wait_ge(w_lo_done, b + 1)
                for j in range(TT):
                    x_tile(8 * b + 14 + j, j, j % 4, s, transposed)

            with pe.Fori(B_RV, B_AKV, 2) as b:
                ctx_block(b, 0)
                ctx_block(b + 1, 1)
            ctx_block(B_AKV, 0)
            with pe.Fori(B_RQ, B_AQ, 2) as b:
                x_block(b, 1, True)
                x_block(b + 1, 0, True)
            x_block(B_AQ, 1, False)
            x_block(B_AQ + 1, 0, False)
            with pe.Fori(B_AG, NB, 2) as b:
                x_block(b, 1, True)
                x_block(b + 1, 0, True)

            def turn_keys(h, m, d):
                c = m - 1 if d == 0 else NCH - m
                pe.wait_ge(rk_in, 16 * h + 16)
                if d == 0:
                    pe.wait_ge(kd_lo_done[1], 4 * h + m)
                    if m == 1 and not (isinstance(h, int) and h == 0):
                        pe.wait_ge(y_out, 8 * h - 7)
                else:
                    pe.wait_ge(kd_lo_done[0], 4 * h + m + 1)
                for j in range(2):
                    for e in range(2):
                        at = c * CH + j * P
                        ins = pe.transpose(ps[:, 0, j * RDK + e * P:j * RDK + (e + 1) * P], rk_raw[:, e, at:at + P], ident[:])
                ins.then_inc(k_turned[d], 1)

            def delta(h, m, d):
                pe.wait_ge(kd_lo_done[d], 4 * h + m + 1)
                if m == 0:
                    pe.wait_ge(cv_lo_done, h + 1)
                    vals, v0 = cv, 0
                    if not (isinstance(h, int) and h == 0):
                        pe.wait_ge(cross_out[d], 4 * h)
                else:
                    vals, v0 = rv, 2 * (m - 1 if d == 0 else NCH - m)
                    pe.wait_ge(cross_out[d], 4 * h + m)
                for e in range(2):
                    ins = passes(ps[:, 2 + 2 * d + e, :], kd[d], vals, lambda v, k: v[:, k, e * P:(e + 1) * P],
                                 lambda v, k: v[:, v0 + k, :], 2)
                ins.then_inc(delta_done[d], 1)

            def scores(h, s):
                if s == 0:
                    pe.wait_ge(g03_lo_pool, 2 * h + 2)
                if s == 1:
                    pe.wait_ge(g12_lo_done, 3 * h + 2)
                    if not (isinstance(h, int) and h == 0):
                        pe.wait_ge(y_out, 8 * h)
                if not (isinstance(h, int) and h == 0 and s == 0):
                    pe.wait_ge(probs_done, 4 * h + s)
                at = s * CH
                for j in range(2):
                    ins = passes(ps[:, 1, j * CH:(j + 1) * CH], rk, rq, lambda v, k: v[:, k, at + j * P:at + (j + 1) * P],
                                 lambda v, k: v[:, k, at:at + CH], 2)
                ins.then_inc(scores_done, 1)

            def cross(h, s, d):
                c = s if d == 0 else NCH - 1 - s
                pe.wait_ge(state_lo_done[d], 4 * h + s + 1)
                for i in range(2):
                    at = c * CH + i * P
                    ins = passes(ps[:, 2 + 2 * d + i, :], rq, state_r[d], lambda v, k: v[:, k, at:at + P],
                                 lambda v, k: v[:, k, :], 2)
                ins.then_inc(cross_done[d], 1)

            def intra(h, s):
                pe.wait_ge(probs_lo_done, 4 * h + s + 1)
                if s == 0:
                    pe.wait_ge(g03_lo_values, h + 1)
                    if not (isinstance(h, int) and h == 0):
                        pe.wait_ge(y_out, 8 * h - 5)
                else:
                    pe.wait_ge(intra_out, 4 * h + s)
                    if s == 1:
                        pe.wait_ge(g12_lo_done, 3 * h + 3)
                for i in range(2):
                    ins = passes(ps[:, 6 + i, :], probs_r, rv, lambda v, k: v[:, k, i * P:(i + 1) * P],
                                 lambda v, k: v[:, 2 * s + k, :], 2)
                ins.then_inc(intra_done, 1)

            def turn_o(h, g, e):
                bank = o_bank(h, g, e)
                last = isinstance(h, int) and h == RH - 1
                pe.wait_ge(o_normed, 2 * h + g + 1)
                if last and g == 0:
                    if e == 0:
                        pe.wait_ge(ak_lo_done, 5)
                    elif e < 3:
                        pe.wait_ge(cross_out[1], 4 * h + 4)
                    else:
                        pe.wait_ge(intra_out, 4 * h + 4)
                elif last:
                    pe.wait_ge(intra_out, 4 * h + 4)
                    pe.wait_ge(y_out, 8 * h + e)
                elif g == 0 and e == 0:
                    pe.wait_ge(kd_lo_done[1], 4 * h + 4)
                elif g == 0 and e < 3:
                    pe.wait_ge(intra_out, 4 * h + 4)
                elif g == 0:
                    pe.wait_ge(probs_done, 4 * h + 5)
                elif e == 0:
                    pe.wait_ge(y_out, 8 * h + 4)
                elif e == 1:
                    pe.wait_ge(kd_lo_done[1], 4 * h + 6)
                else:
                    pe.wait_ge(y_out, 8 * h + 3 + e)
                for i, t in enumerate(O_GROUPS[g]):
                    ins = pe.transpose(ps[:, bank, i * P:(i + 1) * P], ret_o[:, t, e * P:(e + 1) * P], ident[:])
                ins.then_inc(o_turned, 1)

            def head(h, last):
                first = isinstance(h, int) and h == 0
                scores(h, 0)
                if not first:
                    for e in range(3):
                        turn_o(h - 1, 0, e)
                cross(h, 0, 0)
                if not first:
                    turn_o(h - 1, 0, 3)
                turn_keys(h, 1, 0)
                cross(h, 0, 1)
                turn_keys(h, 1, 1)
                if not first:
                    for e in range(4):
                        turn_o(h - 1, 1, e)
                intra(h, 0)
                delta(h, 1, 0)
                delta(h, 1, 1)
                for s in range(1, NCH):
                    ending = last and s == NCH - 1
                    scores(h, s)
                    if ending:
                        turn_att_keys(0)
                    cross(h, s, 0)
                    if s < NCH - 1:
                        turn_keys(h, s + 1, 0)
                    elif ending:
                        turn_att_keys(1)
                    cross(h, s, 1)
                    if s < NCH - 1:
                        turn_keys(h, s + 1, 1)
                    elif ending:
                        turn_att_keys(2)
                        turn_att_keys(3)
                    intra(h, s)
                    if s < NCH - 1:
                        delta(h, s + 1, 0)
                        delta(h, s + 1, 1)
                if last:
                    turn_att_keys(4)
                    turn_att_keys(5)
                else:
                    delta(h + 1, 0, 0)
                    delta(h + 1, 0, 1)

            def turn_att_keys(n):
                g, (k0, k1) = n // 3, piece(n % 3)
                pe.wait_ge(keys_normed, g + 1)
                if n == 0:
                    pe.wait_ge(kd_lo_done[1], 4 * RH)
                elif n < 3:
                    pe.wait_ge(ak_lo_done, n)
                elif n < 5:
                    pe.wait_ge(cross_out[0], 4 * RH)
                else:
                    pe.wait_ge(ak_lo_done, 3)
                for k in range(k0, k1):
                    ins = pe.transpose(ps[:, KEY_BANKS[n], (k - k0) * P:(k - k0 + 1) * P], kv_raw[:, k, g * AD:(g + 1) * AD], ident[:])
                ins.then_inc(ak_turned, 1)

            delta(0, 0, 1)
            pe.wait_ge(tile_out, 8 * NB + 14)
            delta(0, 0, 0)
            head(0, False)
            with pe.Fori(1, RH - 1) as h:
                head(h, False)
            head(RH - 1, True)

            def turn_queries(t, half):
                pe.wait_ge(aq_in[half], 16 * t + 16)
                if not (isinstance(t, int) and t == 0 and half == 0):
                    pe.wait_ge(aq_lo_done, 2 * t + half)
                if half == 0 and not (isinstance(t, int) and t == 0):
                    pe.wait_ge(sc_bank, 3 * (AH * t - 4))
                    pe.wait_ge(soft_lo, 3 * (AH * t - 3) - 3)
                if half == 1 and not (isinstance(t, int) and t == 0):
                    pe.wait_ge(soft_lo, 3 * (AH * t + 1) - 3)
                for h in range(4):
                    ins = pe.transpose(ps[:, queries_bank(t, half), h * P:(h + 1) * P], aq_raw[:, half, h * AD:(h + 1) * AD], ident[:])
                ins.then_inc(aq_turned, 1)

            def att_scores(t, u):
                k = AH * t + u
                if not (isinstance(t, int) and t == 0 and u == 0):
                    pe.wait_ge(exp_done, k)
                if u == 0:
                    pe.wait_ge(aq_lo_done, 2 * t + 1)
                if u == 4:
                    pe.wait_ge(aq_lo_done, 2 * t + 2)
                for b in range(3):
                    n = min(W, KEYS - b * W)
                    passes(ps[:, b, 0:n], aq, ak, lambda v, k: v[:, u, :], lambda v, k: v[:, u // 4, b * W:b * W + n], 1).then_inc(sc_bank, 1)

            def turn_soft(t, u):
                k = AH * t + u
                pe.wait_ge(soft_done, k + 1)
                if isinstance(t, int) and t == 0 and u == 0:
                    pe.wait_ge(y_out, 8 * RH)
                for j in range(NKT):
                    b = j // 4
                    if j % 4 == 0 and not (isinstance(t, int) and t == 0 and 3 * u + b < 4):
                        pe.wait_ge(soft_lo, 3 * k + b - 3)
                    if j == 0 and u == 1:
                        pe.wait_ge(aq_lo_done, 2 * t + 2)
                    if j == 0 and u == 5 and not (isinstance(t, int) and t == TT - 1):
                        pe.wait_ge(aq_lo_done, 2 * t + 3)
                    if j == 0 and u == AH - 1:
                        pe.wait_ge(gate_col, t + 1)
                    at = j % 4 * P
                    ins = pe.transpose(ps[:, turn_bank(u, b), at:at + P], soft[u % 2][:, j * P:(j + 1) * P], ident[:])
                ins.then_inc(soft_turned, 1)

            def values(t, g, part):
                if part == 0:
                    pe.wait_ge(av_lo_done, 1)
                    pe.wait_ge(soft_lo, 3 * (AH * t + 4 * g + 4))
                    if not (isinstance(t, int) and t == 0 and g == 0):
                        pe.wait_ge(att_out, 2 * t + g)
                k0, k1 = ((0, 3), (3, 6), (6, 8), (8, NKT))[part]
                for k in range(k0, k1):
                    for i, (a, b) in enumerate(((0, 0), (0, 1), (1, 0))):
                        ins = pe.matmul(ps[:, 7, :], av[a][:, k, g * AD:(g + 1) * AD],
                                        soft_t[g][b][:, k].rearrange("p h i -> p (h i)"),
                                        start=(k == 0 and i == 0), stop=(k == NKT - 1 and i == 2))
                if part == 3:
                    ins.then_inc(pv_done, 1)

            def tile(t):
                first = isinstance(t, int) and t == 0
                last = isinstance(t, int) and t == TT - 1
                for u in range(AH):
                    att_scores(t, u)
                    if first and u < 2:
                        for e in range(4):
                            turn_o(RH - 1, u, e)
                    if u < 2 and not first:
                        values(t - 1, 0, u + 2)
                    elif 2 <= u <= 5 and not first:
                        values(t - 1, 1, u - 2)
                    elif u >= 6:
                        values(t, 0, u - 6)
                    if u > 0:
                        turn_soft(t, u - 1)
                    elif not first:
                        turn_soft(t - 1, AH - 1)
                    if u == 1:
                        turn_queries(t, 1)
                    if u == 5 and not last:
                        turn_queries(t + 1, 0)
                    if u == 7:
                        pe.wait_ge(gate_step, 4 * t + 4)
                        pe.wait_ge(soft_lo, 3 * (AH * t + 7) - 3)
                        pe.matmul(ps[:, turn_bank(AH - 1, 0), 0:1], ada_g[:, 0, :], ones[:]).then_inc(ada_g_done, 1)

            pe.wait_ge(ak_lo_done, 4)
            turn_queries(0, 0)
            pe.wait_ge(ak_lo_done, KEY_PIECES)
            tile(0)
            with pe.Fori(1, TT - 1) as t:
                tile(t)
            tile(TT - 1)
            values(TT - 1, 0, 2)
            turn_soft(TT - 1, AH - 1)
            values(TT - 1, 0, 3)
            for part in range(4):
                values(TT - 1, 1, part)

            def chunk_ready(half, c):
                pe.wait_ge(ow_lo_done, CHUNKS * half + c + 1)

            def branch_tile(half, n, first):
                k = KT * half + n
                for i in range(3):
                    chunk_ready(half, 3 * n + i)
                    bank = 0 if i < 2 else 1
                    if i == 0:
                        if half == 0 and first:
                            pe.wait_ge(exp_done, TT * AH)
                        else:
                            pe.wait_ge(merged_part, k)
                    if i == 2 and not (half == 0 and first):
                        pe.wait_ge(mg_used, k)
                    for j in range(KT):
                        if first:
                            pe.wait_ge(y_lo_done, 3 * KT * half + KT * i + j + 1)
                        for q, (a, b) in enumerate(((0, 0), (0, 1), (1, 0))):
                            ins = pe.matmul(ps[:, bank, :], ow[i][a][:, j, :], y_r(KT * i + j, b),
                                            start=(i != 1 and j == 0 and q == 0), stop=(i != 0 and j == KT - 1 and q == 2))
                    ins.then_inc(ow_used, 1)

            def out_tile(half, n):
                k = KT * half + n
                c = 3 * KT + n
                chunk_ready(half, c)
                if k >= 2:
                    pe.wait_ge(out_gated, k - 1)
                for j in range(KT):
                    if n == 0:
                        pe.wait_ge(z_lo_done, KT * half + j + 1)
                    for q, (a, b) in enumerate(((0, 0), (0, 1), (1, 0))):
                        ins = pe.matmul(ps[:, 2 + n % 2, :], ow[c % 3][a][:, j, :], z_r[b][:, j, :],
                                        start=(j == 0 and q == 0), stop=(j == KT - 1 and q == 2))
                ins.then_inc(ow_used, 1)

            def turn_out(half, n):
                k = KT * half + n
                pe.wait_ge(out_gated, k + 1)
                if k >= 2:
                    pe.wait_ge(out_added, k - 1)
                for j in range(4):
                    ins = pe.transpose(ps[:, 4 + n % 2, j * P:(j + 1) * P], out_t[:, n % 2, j * P:(j + 1) * P], ident[:])
                ins.then_inc(out_turned, 1)

            for half in range(HALVES):
                branch_tile(half, 0, True)
                with pe.Fori(1, KT) as n:
                    branch_tile(half, n, False)
                for n in range(KT):
                    out_tile(half, n)
                    if n:
                        turn_out(half, n - 1)
                turn_out(half, KT - 1)


NORM_GROUPS = ((0, 4), (4, 10))
LN2 = float(np.log(2.0))


_INS = ["x", "c", "ctx", "c_ctx", "norm_w", "w_ada", "b_ada", "w_in", "ret_log2_decay",
        "q_norm_w", "k_norm_w", "w_o_ret", "w_o_att", "w_out"]


def kernel(**inputs):
    import concourse.bacc as bacc
    from concourse.bass_utils import run_bass_kernel_spmd

    nc = bacc.Bacc("TRN2", target_bir_lowering=False, num_devices=1)
    arrays, args = {}, []
    values = {name: np.ascontiguousarray(inputs[name]) for name in _INS}
    values.update(shape_constants())
    for name, a in values.items():
        arrays[f"{name}_dram"] = a
        args.append(nc.dram_tensor(f"{name}_dram", a.shape, mybir.dt.from_np(a.dtype), kind="ExternalInput").ap())
    out = nc.dram_tensor("out_dram", (1, SEQ, D), F32, kind="ExternalOutput").ap()
    build_program(nc, *args, out)
    r = run_bass_kernel_spmd(nc, [arrays], core_ids=[0])
    return r.results[0]["out_dram"]
```
